# Optimizing a Trainium2 kernel written in Bass

```python
import jax, jax.numpy as jnp
from jax import lax
import numpy as np
import math

D_MODEL = 1024
BATCH = 1
SEQ = 256
DEPTH = 4

N_MIXERS = 3
N_A = (DEPTH + 2) // 3
N_B = (DEPTH + 1) // 3
N_C = DEPTH // 3

ATTN_GROUPS = ((128, 1), (512, 4), (2048, 16))
N_GROUPS = len(ATTN_GROUPS)
HEADS_PER_GROUP = 16
HEAD_DIM = 64
ROT_DIM = HEAD_DIM // 4
ROPE_THETA = 500000.0
QKV_WIDTH = 3 * N_GROUPS * HEADS_PER_GROUP * HEAD_DIM
ATTN_OUT_WIDTH = HEADS_PER_GROUP * HEAD_DIM

SC_WIDTH = 3
CONF_CONV_WIDTH = 31
FFN_DIM = 2816
FFN_CONV_WIDTH = 3
EPS_RMS = 1e-6
EPS_LN = 1e-5
NEG_INF = -1e30


def rms_norm(x, g):
    xf = x.astype(jnp.float32)
    y = xf * lax.rsqrt(jnp.mean(xf * xf, axis=-1, keepdims=True) + EPS_RMS)
    return (y * g.astype(jnp.float32)).astype(x.dtype)

def layer_norm(x, g, b):
    xf = x.astype(jnp.float32)
    mu = jnp.mean(xf, axis=-1, keepdims=True)
    var = jnp.mean(jnp.square(xf - mu), axis=-1, keepdims=True)
    y = (xf - mu) * lax.rsqrt(var + EPS_LN)
    return (y * g.astype(jnp.float32) + b.astype(jnp.float32)).astype(x.dtype)

def causal_dwconv(x, w):
    k_width, ch = w.shape
    return lax.conv_general_dilated(
        x, w[:, None, :].astype(x.dtype), window_strides=(1,), padding=[(k_width - 1, 0)],
        dimension_numbers=("NWC", "WIO", "NWC"), feature_group_count=ch)

def rope_partial(t, cos, sin):
    half = ROT_DIM // 2
    tr = t[..., :ROT_DIM].astype(jnp.float32)
    t1, t2 = tr[..., :half], tr[..., half:]
    rot = jnp.concatenate([t1 * cos - t2 * sin, t2 * cos + t1 * sin], axis=-1)
    return jnp.concatenate([rot.astype(t.dtype), t[..., ROT_DIM:]], axis=-1)

def dilated_group_attention(q, k, v, window, dilation):
    B, S, H, Dh = q.shape
    L = S // dilation
    W = window // dilation
    nb = -(-L // W)
    Lp = nb * W

    def to_sub(t):
        t = t.reshape(B, L, dilation, H, Dh).transpose(0, 2, 1, 3, 4).reshape(B * dilation, L, H, Dh)
        t = jnp.pad(t, ((0, 0), (0, Lp - L), (0, 0), (0, 0)))
        return t.reshape(B * dilation, nb, W, H, Dh)

    def with_prev(t):
        prev = jnp.pad(t[:, :-1], ((0, 0), (1, 0), (0, 0), (0, 0), (0, 0)))
        return jnp.concatenate([prev, t], axis=2)

    qb, kb, vb = to_sub(q), to_sub(k), to_sub(v)
    kk, vv = with_prev(kb), with_prev(vb)
    scale = 1.0 / np.sqrt(Dh).astype(np.float32)
    s = jnp.einsum("bnqhd,bnkhd->bnhqk", qb, kk, preferred_element_type=jnp.float32) * scale
    qi = jnp.arange(W)[:, None]
    kj = jnp.arange(2 * W)[None, :]
    dist = qi - kj + W
    blk = jnp.arange(nb)[:, None, None]
    valid = (dist >= 0) & (dist <= W) & ((blk > 0) | (kj >= W))
    s = jnp.where(valid[None, :, None], s, NEG_INF)
    lse = jax.nn.logsumexp(s, axis=-1)
    p = jnp.exp(s - lse[..., None])
    o = jnp.einsum("bnhqk,bnkhd->bnqhd", p.astype(v.dtype), vv)
    o = o.reshape(B * dilation, Lp, H, Dh)[:, :L]
    o = o.reshape(B, dilation, L, H, Dh).transpose(0, 2, 1, 3, 4).reshape(B, S, H, Dh)
    lse = lse.transpose(0, 1, 3, 2).reshape(B * dilation, Lp, H)[:, :L]
    lse = lse.reshape(B, dilation, L, H).transpose(0, 2, 1, 3).reshape(B, S, H)
    return o, lse

def dilated_attention_mixer(x, positions, w_qkv, w_o):
    B, S, _ = x.shape
    GH = N_GROUPS * HEADS_PER_GROUP
    qkv = (x @ w_qkv).reshape(B, S, 3, GH, HEAD_DIM)
    inv_freq = ROPE_THETA ** (-jnp.arange(0, ROT_DIM, 2, dtype=jnp.float32) / ROT_DIM)
    ang = positions.astype(jnp.float32)[..., None] * inv_freq
    cos, sin = jnp.cos(ang)[:, :, None, :], jnp.sin(ang)[:, :, None, :]
    q = rope_partial(qkv[:, :, 0], cos, sin)
    k = rope_partial(qkv[:, :, 1], cos, sin)
    v = qkv[:, :, 2]
    outs, lses = [], []
    for g, (window, dilation) in enumerate(ATTN_GROUPS):
        sl = slice(g * HEADS_PER_GROUP, (g + 1) * HEADS_PER_GROUP)
        o, l = dilated_group_attention(q[:, :, sl], k[:, :, sl], v[:, :, sl], window, dilation)
        outs.append(o)
        lses.append(l)
    alpha = jax.nn.softmax(jnp.stack(lses, axis=0), axis=0)
    o = jnp.sum(alpha[..., None] * jnp.stack(outs, axis=0).astype(jnp.float32), axis=0)
    return o.astype(x.dtype).reshape(B, S, ATTN_OUT_WIDTH) @ w_o

def short_conv_mixer(x, w_in, w_conv, w_out):
    b_gate, c_gate, h = jnp.split(x @ w_in, 3, axis=-1)
    return (b_gate * causal_dwconv(c_gate * h, w_conv)) @ w_out

def conformer_conv_mixer(x, w_pw1, b_pw1, w_dw, b_dw, ln_g, ln_b, w_pw2, b_pw2):
    a, g = jnp.split(x @ w_pw1 + b_pw1, 2, axis=-1)
    h = a * jax.nn.sigmoid(g)
    h = causal_dwconv(h, w_dw) + b_dw
    h = jax.nn.silu(layer_norm(h, ln_g, ln_b))
    return h @ w_pw2 + b_pw2

def conv_ffn(x, w_in, w_conv, w_out):
    u = causal_dwconv(x @ w_in, w_conv)
    g, v = jnp.split(u, 2, axis=-1)
    return (jax.nn.silu(g) * v) @ w_out

def first_inputs(seed: int = 0) -> dict:
    key = jax.random.key(seed)
    ks = jax.random.split(key, 24)
    f32 = jnp.float32
    D, F = D_MODEL, FFN_DIM

    def nrm(k, shape, scale):
        return jax.random.normal(k, shape, f32) * scale

    def gain(k, shape):
        return 1.0 + 0.1 * jax.random.normal(k, shape, f32)

    return {
        "x": jax.random.normal(ks[0], (BATCH, SEQ, D), f32),
        "positions": jnp.broadcast_to(jnp.arange(SEQ, dtype=jnp.int32)[None, :], (BATCH, SEQ)),
        "mix_norm_pre": gain(ks[1], (DEPTH, D)),
        "mix_norm_post": gain(ks[2], (DEPTH, D)),
        "ffn_norm_pre": gain(ks[3], (DEPTH, D)),
        "ffn_norm_post": gain(ks[4], (DEPTH, D)),
        "attn_w_qkv": nrm(ks[5], (N_A, D, QKV_WIDTH), D ** -0.5),
        "attn_w_o": nrm(ks[6], (N_A, ATTN_OUT_WIDTH, D), ATTN_OUT_WIDTH ** -0.5),
        "sc_w_in": nrm(ks[7], (N_B, D, 3 * D), D ** -0.5),
        "sc_w_conv": nrm(ks[8], (N_B, SC_WIDTH, D), SC_WIDTH ** -0.5),
        "sc_w_out": nrm(ks[9], (N_B, D, D), D ** -0.5),
        "cc_w_pw1": nrm(ks[10], (N_C, D, 2 * D), D ** -0.5),
        "cc_b_pw1": nrm(ks[11], (N_C, 2 * D), 0.01),
        "cc_w_dw": nrm(ks[12], (N_C, CONF_CONV_WIDTH, D), CONF_CONV_WIDTH ** -0.5),
        "cc_b_dw": nrm(ks[13], (N_C, D), 0.01),
        "cc_ln_g": gain(ks[14], (N_C, D)),
        "cc_ln_b": nrm(ks[15], (N_C, D), 0.01),
        "cc_w_pw2": nrm(ks[16], (N_C, D, D), D ** -0.5),
        "cc_b_pw2": nrm(ks[17], (N_C, D), 0.01),
        "ffn_w_in": nrm(ks[18], (DEPTH, D, 2 * F), D ** -0.5),
        "ffn_w_conv": nrm(ks[19], (DEPTH, FFN_CONV_WIDTH, 2 * F), FFN_CONV_WIDTH ** -0.5),
        "ffn_w_out": nrm(ks[20], (DEPTH, F, D), F ** -0.5),
    }

def first_block(x, positions, mix_norm_pre, mix_norm_post, ffn_norm_pre, ffn_norm_post,
              attn_w_qkv, attn_w_o, sc_w_in, sc_w_conv, sc_w_out,
              cc_w_pw1, cc_b_pw1, cc_w_dw, cc_b_dw, cc_ln_g, cc_ln_b, cc_w_pw2, cc_b_pw2,
              ffn_w_in, ffn_w_conv, ffn_w_out):
    h = x
    for i in range(DEPTH):
        kind, j = i % N_MIXERS, i // N_MIXERS
        a = rms_norm(h, mix_norm_pre[i])
        if kind == 0:
            m = dilated_attention_mixer(a, positions, attn_w_qkv[j], attn_w_o[j])
        elif kind == 1:
            m = short_conv_mixer(a, sc_w_in[j], sc_w_conv[j], sc_w_out[j])
        else:
            m = conformer_conv_mixer(a, cc_w_pw1[j], cc_b_pw1[j], cc_w_dw[j], cc_b_dw[j],
                                     cc_ln_g[j], cc_ln_b[j], cc_w_pw2[j], cc_b_pw2[j])
        h = h + rms_norm(m, mix_norm_post[i])
        f = conv_ffn(rms_norm(h, ffn_norm_pre[i]), ffn_w_in[i], ffn_w_conv[i], ffn_w_out[i])
        h = h + rms_norm(f, ffn_norm_post[i])
    return h


DEPTH_2 = 1

N_META = 16
A_HEADS = 4
A_DK = 64
A_DV = 2 * A_DK
B_HEADS = 4
B_DQ = 128
B_DC = 256
B_DV = 128
IDX_HEADS = 8
IDX_DIM = 64
IDX_TOPK_MAX = 256
REL_BUCKETS = 32
REL_MAX_DIST = 128
N_BIAS_HEADS = A_HEADS + B_HEADS
D_FF = 2816
Q_BLOCK = 128
EPS = 1e-6
A_SCALE = A_DK ** -0.5
B_SCALE = B_DC ** -0.5

IN_SIZES = (
    A_HEADS * 2 * A_DK,
    A_HEADS * 2 * A_DK,
    A_HEADS * A_DV,
    B_HEADS * B_DQ,
    B_DC,
    IDX_HEADS * IDX_DIM,
    IDX_DIM,
    IDX_HEADS,
)
N_IN = sum(IN_SIZES)
IN_SPLITS = [int(v) for v in np.cumsum(IN_SIZES)[:-1]]
D_MIX = A_HEADS * A_DV + B_HEADS * B_DV


def rmsnorm(x, g):
    xf = x.astype(jnp.float32)
    y = xf * lax.rsqrt(jnp.mean(xf * xf, axis=-1, keepdims=True) + EPS)
    return (y * g.astype(jnp.float32)).astype(x.dtype)

def swiglu(x, w_gate, w_up, w_down):
    return (jax.nn.silu(x @ w_gate) * (x @ w_up)) @ w_down

def rel_bucket(q_pos, k_pos):
    max_exact = REL_BUCKETS // 2
    n = jnp.maximum(q_pos - k_pos, 0)
    nf = jnp.maximum(n, 1).astype(jnp.float32)
    large = max_exact + (jnp.log(nf / max_exact) / math.log(REL_MAX_DIST / max_exact)
                         * (REL_BUCKETS - max_exact)).astype(jnp.int32)
    large = jnp.minimum(large, REL_BUCKETS - 1)
    return jnp.where(n < max_exact, n, large)

def diff_attention(q, k, v, lam, bias_a, subln_g, lam_init):
    bsz, length = q.shape[0], q.shape[1]
    outs = []
    for start in range(0, length, Q_BLOCK):
        stop = min(start + Q_BLOCK, length)
        q_pos = jnp.arange(start, stop)
        k_pos = jnp.arange(stop)
        bias = bias_a[rel_bucket(q_pos[:, None], k_pos[None, :])].transpose(2, 0, 1)
        s = jnp.einsum('bqhmd,bkhmd->bhmqk', q[:, start:stop], k[:, :stop]).astype(jnp.float32)
        s = s * A_SCALE + bias[None, :, None].astype(jnp.float32)
        s = jnp.where(k_pos[None, :] <= q_pos[:, None], s, -jnp.inf)
        p = jax.nn.softmax(s, axis=-1)
        a = p[:, :, 0] - lam * p[:, :, 1]
        outs.append(jnp.einsum('bhqk,bkhd->bqhd', a.astype(v.dtype), v[:, :stop]))
    o = jnp.concatenate(outs, axis=1)
    o = rmsnorm(o, subln_g) * (1.0 - lam_init)
    return o.reshape(bsz, length, A_HEADS * A_DV)

def dsa_attention(q_lat, c, iq, ik, iw, w_uv, bias_b, topk):
    bsz, length = q_lat.shape[0], q_lat.shape[1]
    gather = jax.vmap(lambda cb, ib: cb[ib])
    outs = []
    for start in range(0, length, Q_BLOCK):
        stop = min(start + Q_BLOCK, length)
        q_pos = jnp.arange(start, stop)
        k_pos = jnp.arange(stop)
        dots = jnp.einsum('bqhd,bkd->bqhk', iq[:, start:stop], ik[:, :stop]).astype(jnp.float32)
        w = iw[:, start:stop].astype(jnp.float32) * (IDX_HEADS ** -0.5)
        score = jnp.einsum('bqh,bqhk->bqk', w, jax.nn.relu(dots * (IDX_DIM ** -0.5)))
        score = jnp.where(k_pos[None, None, :] <= q_pos[None, :, None], score, -jnp.inf)
        _, sel = lax.top_k(score, min(topk, stop))
        valid = sel <= q_pos[None, :, None]
        g = gather(c, sel)
        bias = bias_b[rel_bucket(q_pos[None, :, None], sel)].transpose(0, 3, 1, 2)
        s = jnp.einsum('bqhc,bqkc->bhqk', q_lat[:, start:stop], g).astype(jnp.float32)
        s = s * B_SCALE + bias.astype(jnp.float32)
        s = jnp.where(valid[:, None], s, -jnp.inf)
        p = jax.nn.softmax(s, axis=-1)
        o_lat = jnp.einsum('bhqk,bqkc->bqhc', p.astype(g.dtype), g)
        outs.append(jnp.einsum('bqhc,hcd->bqhd', o_lat, w_uv))
    o = jnp.concatenate(outs, axis=1)
    return o.reshape(bsz, length, B_HEADS * B_DV)

def second_inputs(seed: int = 0) -> dict:
    key = jax.random.key(seed)
    ks = jax.random.split(key, 32)
    f32 = jnp.float32

    def nrm(k, shape, scale):
        return jax.random.normal(k, shape, f32) * scale

    def gain(k, shape):
        return 1.0 + 0.02 * jax.random.normal(k, shape, f32)

    L = DEPTH_2
    return {
        'x': nrm(ks[0], (BATCH, SEQ, D_MODEL), 1.0),
        'meta_tokens': nrm(ks[1], (N_META, D_MODEL), 1.0),
        'rel_bias': nrm(ks[2], (REL_BUCKETS, N_BIAS_HEADS), 0.1),
        'ffn1_norm': gain(ks[3], (L, D_MODEL)),
        'ffn1_w_gate': nrm(ks[4], (L, D_MODEL, D_FF), D_MODEL ** -0.5),
        'ffn1_w_up': nrm(ks[5], (L, D_MODEL, D_FF), D_MODEL ** -0.5),
        'ffn1_w_down': nrm(ks[6], (L, D_FF, D_MODEL), D_FF ** -0.5),
        'mix_norm': gain(ks[7], (L, D_MODEL)),
        'w_in': nrm(ks[8], (L, D_MODEL, N_IN), D_MODEL ** -0.5),
        'a_q_norm': gain(ks[9], (L, A_DK)),
        'a_k_norm': gain(ks[10], (L, A_DK)),
        'a_lambda_q1': nrm(ks[11], (L, A_DK), 0.1),
        'a_lambda_k1': nrm(ks[12], (L, A_DK), 0.1),
        'a_lambda_q2': nrm(ks[13], (L, A_DK), 0.1),
        'a_lambda_k2': nrm(ks[14], (L, A_DK), 0.1),
        'a_subln': gain(ks[15], (L, A_DV)),
        'b_kv_norm': gain(ks[16], (L, B_DC)),
        'b_w_uk': nrm(ks[17], (L, B_HEADS, B_DQ, B_DC), B_DQ ** -0.5),
        'b_q_norm': gain(ks[18], (L, B_DC)),
        'b_w_uv': nrm(ks[19], (L, B_HEADS, B_DC, B_DV), B_DC ** -0.5),
        'w_out': nrm(ks[20], (L, D_MIX, D_MODEL), D_MIX ** -0.5),
        'ffn2_norm': gain(ks[21], (L, D_MODEL)),
        'ffn2_w_gate': nrm(ks[22], (L, D_MODEL, D_FF), D_MODEL ** -0.5),
        'ffn2_w_up': nrm(ks[23], (L, D_MODEL, D_FF), D_MODEL ** -0.5),
        'ffn2_w_down': nrm(ks[24], (L, D_FF, D_MODEL), D_FF ** -0.5),
    }

def second_block(x, meta_tokens, rel_bias, ffn1_norm, ffn1_w_gate, ffn1_w_up, ffn1_w_down,
              mix_norm, w_in, a_q_norm, a_k_norm, a_lambda_q1, a_lambda_k1, a_lambda_q2,
              a_lambda_k2, a_subln, b_kv_norm, b_w_uk, b_q_norm, b_w_uv, w_out,
              ffn2_norm, ffn2_w_gate, ffn2_w_up, ffn2_w_down):
    bsz, seq = x.shape[0], x.shape[1]
    topk = min(IDX_TOPK_MAX, seq // 4)
    meta = jnp.broadcast_to(meta_tokens.astype(x.dtype)[None], (bsz, N_META, D_MODEL))
    h = jnp.concatenate([meta, x], axis=1)
    length = h.shape[1]
    bias_a = rel_bias[:, :A_HEADS]
    bias_b = rel_bias[:, A_HEADS:]

    for l in range(DEPTH_2):
        h = h + 0.5 * swiglu(rmsnorm(h, ffn1_norm[l]), ffn1_w_gate[l], ffn1_w_up[l], ffn1_w_down[l])

        u = rmsnorm(h, mix_norm[l]) @ w_in[l]
        qa, ka, va, qb, ckv, iq, ik, iw = jnp.split(u, IN_SPLITS, axis=-1)

        qa = rmsnorm(qa.reshape(bsz, length, A_HEADS, 2, A_DK), a_q_norm[l])
        ka = rmsnorm(ka.reshape(bsz, length, A_HEADS, 2, A_DK), a_k_norm[l])
        va = va.reshape(bsz, length, A_HEADS, A_DV)
        lam_init = 0.8 - 0.6 * math.exp(-0.3 * l)
        lam = (jnp.exp(jnp.sum(a_lambda_q1[l].astype(jnp.float32) * a_lambda_k1[l].astype(jnp.float32)))
               - jnp.exp(jnp.sum(a_lambda_q2[l].astype(jnp.float32) * a_lambda_k2[l].astype(jnp.float32)))
               + lam_init)
        o_a = diff_attention(qa, ka, va, lam, bias_a, a_subln[l], lam_init)

        qb = qb.reshape(bsz, length, B_HEADS, B_DQ)
        q_lat = rmsnorm(jnp.einsum('blhd,hdc->blhc', qb, b_w_uk[l]), b_q_norm[l])
        c = rmsnorm(ckv, b_kv_norm[l])
        iq = iq.reshape(bsz, length, IDX_HEADS, IDX_DIM)
        o_b = dsa_attention(q_lat, c, iq, ik, iw, b_w_uv[l], bias_b, topk)

        h = h + jnp.concatenate([o_a, o_b], axis=-1) @ w_out[l]

        h = h + 0.5 * swiglu(rmsnorm(h, ffn2_norm[l]), ffn2_w_gate[l], ffn2_w_up[l], ffn2_w_down[l])

    return h[:, N_META:]


def setup_inputs(seed=0):
    out = dict(first_inputs(seed))
    for name, value in second_inputs(seed + 1).items():
        if name != "x":
            out[name + "_2"] = value
    return out


def reference(
    x, positions, mix_norm_pre, mix_norm_post, ffn_norm_pre, ffn_norm_post, attn_w_qkv,
    attn_w_o, sc_w_in, sc_w_conv, sc_w_out, cc_w_pw1, cc_b_pw1, cc_w_dw, cc_b_dw, cc_ln_g,
    cc_ln_b, cc_w_pw2, cc_b_pw2, ffn_w_in, ffn_w_conv, ffn_w_out, meta_tokens_2, rel_bias_2,
    ffn1_norm_2, ffn1_w_gate_2, ffn1_w_up_2, ffn1_w_down_2, mix_norm_2, w_in_2, a_q_norm_2,
    a_k_norm_2, a_lambda_q1_2, a_lambda_k1_2, a_lambda_q2_2, a_lambda_k2_2, a_subln_2,
    b_kv_norm_2, b_w_uk_2, b_q_norm_2, b_w_uv_2, w_out_2, ffn2_norm_2, ffn2_w_gate_2,
    ffn2_w_up_2, ffn2_w_down_2,
):
    x = first_block(
        x, positions, mix_norm_pre, mix_norm_post, ffn_norm_pre, ffn_norm_post, attn_w_qkv,
        attn_w_o, sc_w_in, sc_w_conv, sc_w_out, cc_w_pw1, cc_b_pw1, cc_w_dw, cc_b_dw, cc_ln_g,
        cc_ln_b, cc_w_pw2, cc_b_pw2, ffn_w_in, ffn_w_conv, ffn_w_out,
    )
    return second_block(
        x, meta_tokens_2, rel_bias_2, ffn1_norm_2, ffn1_w_gate_2, ffn1_w_up_2, ffn1_w_down_2,
        mix_norm_2, w_in_2, a_q_norm_2, a_k_norm_2, a_lambda_q1_2, a_lambda_k1_2, a_lambda_q2_2,
        a_lambda_k2_2, a_subln_2, b_kv_norm_2, b_w_uk_2, b_q_norm_2, b_w_uv_2, w_out_2,
        ffn2_norm_2, ffn2_w_gate_2, ffn2_w_up_2, ffn2_w_down_2,
    )


_drawn_inputs = setup_inputs


def setup_inputs(seed=0):
    import zlib

    import numpy as np

    out = dict(_drawn_inputs(seed))
    spreads = {}
    factors = {'cc_b_pw1': 7.819,
     'cc_b_dw': 3.794,
     'cc_ln_b': 7.971,
     'cc_b_pw2': 4.695,
     'rel_bias_2': 5.611,
     'ffn1_norm_2': 8.0,
     'mix_norm_2': 7.46,
     'a_q_norm_2': 8.0,
     'a_k_norm_2': 8.0,
     'a_lambda_q2_2': 26.448,
     'a_lambda_k2_2': 22.84,
     'a_subln_2': 200.0,
     'b_kv_norm_2': 8.0,
     'b_q_norm_2': 8.0,
     'ffn2_norm_2': 23.109,
     'a_lambda_q1_2': 8.0,
     'a_lambda_k1_2': 8.0}
    for name, (base, spread) in spreads.items():
        noise = np.random.default_rng([zlib.crc32(name.encode()), seed]).standard_normal(out[name].shape)
        drawn = base * np.exp(spread * noise) if base else spread * noise
        out[name] = __import__('jax').numpy.asarray(drawn.astype(out[name].dtype))
    for name, factor in factors.items():
        out[name] = (out[name] * factor).astype(out[name].dtype)
    return out
```

```python
import math
from contextlib import ExitStack

import numpy as np
import concourse.bass as bass
from concourse import mybir

F32 = mybir.dt.float32
F32R = mybir.dt.float32r
BF16 = mybir.dt.bfloat16
I32 = mybir.dt.int32
ALU = mybir.AluOpType
ACT = mybir.ActivationFunctionType
AX = mybir.AxisListType.X

P = 128
SEQ = 256
META = 16
TW = SEQ + META
QT = SEQ // P
D = 1024
KD = D // P
FF = 2816
KF = FF // P
DEPTH = 4
NEG = -1.0e30
TAKEN = -3.0e38
TAPS = 31
PAD = TAPS - 1
SW = 256
SLAB = KD * SW
GROUPS = 3
HEADS = 16
HD = 64
N_BIAS = 8
BUCKETS = 32
SKEW = 400
TOPK = SEQ // 4
LAM_INIT = 0.8 - 0.6 * math.exp(0.0)
OA_CLAMP = 2.0 ** 65
OA_SCALE = 2.0 ** -10
OA_STD_MAX = math.sqrt(2.0 ** 128 * OA_SCALE ** 2 / P)
TWO_PI = 2.0 * math.pi
PI_A = 6.28125
PI_B = float(np.float32(np.floor((TWO_PI - PI_A) * 2.0 ** 20) / 2.0 ** 20))
PI_C = TWO_PI - PI_A - PI_B
ROUND = 1.5 * 2.0 ** 23

C_IDENT, C_BLK, C_FREQ, C_SIGN, C_HOT, C_CAUSAL = 0, 128, 256, 257, 258, 258 + SKEW
C_MASK = C_CAUSAL + TW
C_END = C_MASK + 1152


def constants():
    c = np.zeros((P, C_END), np.float32)
    p = np.arange(P)
    c[:, C_IDENT:C_IDENT + P] = np.eye(P)
    c[:, C_BLK:C_BLK + P] = (p[:, None] // HD == p[None, :] // HD)
    rot = p % HD < 16
    inv = np.float32(500000.0) ** (-np.arange(0, 16, 2, dtype=np.float32) / np.float32(16))
    c[:, C_FREQ] = np.where(rot, inv[p % 8], 0.0)
    c[:, C_SIGN] = np.where(p % HD < 8, 1.0, -1.0)
    half = BUCKETS // 2
    for i in range(SKEW - 1):
        n = TW - 1 - i
        if n < 0:
            b = BUCKETS
        elif n < half:
            b = n
        else:
            large = np.float32(np.log(np.float32(n) / np.float32(half))) / np.float32(math.log(128 / half))
            b = min(half + int(np.float32(large * np.float32(half))), BUCKETS - 1)
        c[b, C_HOT + i] = 1.0
    k = np.arange(TW)
    c[:, C_CAUSAL:C_CAUSAL + TW] = np.where(k[None, :] > (P + META + p)[:, None], NEG, 0.0)
    at = C_MASK
    for qt in range(2):
        for window, dil in ((128, 1), (512, 4), (2048, 16)):
            dist = (qt * P + p)[:, None] - np.arange((qt + 1) * P)[None, :]
            ok = (dist >= 0) & (dist % dil == 0) & (dist <= window)
            c[:, at:at + (qt + 1) * P] = np.where(ok, 0.0, NEG)
            at += (qt + 1) * P
    return c


class Phase:

    def __init__(self, kind, n, kts, src, c0=META, w=SEQ, gain=0, bias=None, scale=1.0, layer=0, no=0):
        self.kind, self.n, self.kts, self.src = kind, n, kts, src
        self.spb = len(kts)
        self.c0, self.w = c0, w
        self.gain, self.bias, self.scale, self.layer, self.no = gain, bias, scale, layer, no
        self.s0, self.base, self.before, self.prev, self.nxt = 0, {}, None, None, None


def param_rows():
    return [
        ("mix_norm_pre", DEPTH * KD), ("mix_norm_post", DEPTH * KD), ("ffn_norm_pre", DEPTH * KD),
        ("ffn_norm_post", DEPTH * KD), ("ffn_w_conv", DEPTH * 3 * 2 * KF), ("sc_w_conv", 3 * KD),
        ("cc_b_pw1", 2 * KD), ("cc_w_dw", TAPS * KD), ("cc_b_dw", KD), ("cc_ln_g", KD),
        ("cc_ln_b", KD), ("cc_b_pw2", KD), ("ffn1_norm_2", KD), ("mix_norm_2", KD),
        ("ffn2_norm_2", KD), ("a_subln_2", 1), ("b_kv_norm_2", 2), ("b_q_norm_2", 2),
        ("a_q_norm_2", 1), ("a_k_norm_2", 1),
    ]


def par_loads():
    n, row = 0, 0
    for name, rows in param_rows():
        if name in ("a_q_norm_2", "a_k_norm_2"):
            n += 2
        else:
            n += (row + rows - 1) // P - row // P + 1
        row += rows
    return n


def build(nc, A, out, upto=99):
    col, at = {}, 0
    for name, rows in param_rows():
        col[name] = at
        at += rows
    n_par = at
    n_par_tiles = -(-n_par // P)

    def kmajor(w):
        return w.rearrange("(k p) n -> p k n", p=P)

    phases = []

    def cols(w, first, step):
        v = kmajor(w)
        return lambda i, j: v[:, :, bass.ds(i * step[j] + first[j], SW)]

    def ffn_out(w):
        v = kmajor(w)
        ks = [(0, 8), (8, 15), (15, 22)]
        return lambda i, j: v[:, ks[j % 3][0]:ks[j % 3][1], bass.ds(i * 2 * SW + (j // 3) * SW, SW)]

    K8 = [KD, KD]
    K22 = [8, 7, 7, 8, 7, 7]
    attn_no = 0
    for l in range(DEPTH):
        kind = l % 3
        gain = dict(gain=col["mix_norm_post"] + l * KD)
        phases.append(Phase("prenorm", 0, [], None, gain=col["mix_norm_pre"] + l * KD, c0=META, w=SEQ))
        if kind == 0:
            wq, wo = A["attn_w_qkv"][l // 3], A["attn_w_o"][l // 3]
            phases.append(Phase("qk", 12, K8, cols(wq, (0, SW), (512, 512))))
            phases.append(Phase("v", 6, K8, cols(wq, (6144, 6144 + SW), (512, 512))))
            phases.append(Phase("attention", 0, [], None, no=attn_no))
            attn_no += 1
            phases.append(Phase("out", 2, K8, cols(wo, (0, SW), (512, 512)), bias=None, **gain))
        elif kind == 1:
            wi, wo = A["sc_w_in"][0], A["sc_w_out"][0]
            phases.append(Phase("sc_ch", 4, K8, cols(wi, (D, 2 * D), (SW, SW))))
            phases.append(Phase("sc_b", 2, K8, cols(wi, (0, SW), (512, 512))))
            phases.append(Phase("out", 2, K8, cols(wo, (0, SW), (512, 512)), bias=None, **gain))
        else:
            wi, wo = A["cc_w_pw1"][0], A["cc_w_pw2"][0]
            phases.append(Phase("cc_in", 4, K8, cols(wi, (D, 0), (SW, SW))))
            phases.append(Phase("cc_mid", 0, [], None))
            phases.append(Phase("out", 2, K8, cols(wo, (0, SW), (512, 512)), bias=col["cc_b_pw2"], **gain))
        phases.append(Phase("postnorm", 0, [], None, gain=None))
        phases.append(Phase("prenorm", 0, [], None, gain=col["ffn_norm_pre"] + l * KD, c0=META, w=SEQ))
        phases.append(Phase("ffn_in", 11, K8, cols(A["ffn_w_in"][l], (0, FF), (SW, SW)), layer=l))
        phases.append(Phase("out", 2, K22, ffn_out(A["ffn_w_out"][l]), bias=None,
                            gain=col["ffn_norm_post"] + l * KD))
        phases.append(Phase("postnorm", 0, [], None))
    marks = [i for i, ph in enumerate(phases) if ph.kind == "postnorm"]

    def swiglu(tag, c0, w):
        phases.append(Phase("prenorm", 0, [], None, gain=col[tag + "_norm_2"], c0=c0, w=w))
        g, u = kmajor(A[tag + "_w_gate_2"][0]), kmajor(A[tag + "_w_up_2"][0])
        phases.append(Phase("swiglu", 11, K8, lambda i, j: (g, u)[j][:, :, bass.ds(i * SW, SW)], c0=c0, w=w))
        phases.append(Phase("add", 2, K22, ffn_out(A[tag + "_w_down_2"][0]), c0=c0, w=w, scale=0.5))

    swiglu("ffn1", 0, TW)
    phases.append(Phase("prenorm", 0, [], None, gain=col["mix_norm_2"], c0=0, w=TW))
    win = kmajor(A["w_in_2"][0])
    z_cols = [0, 512, 1536, 2304]
    phases.append(Phase("z", 4, K8, lambda i, j: win[:, :, z_cols[i] + j * SW:z_cols[i] + (j + 1) * SW]))
    phases.append(Phase("ckv", 1, K8, lambda i, j: win[:, :, 2048:2304] if j == 0 else win[:, :, 2816:2888]))
    phases.append(Phase("va", 1, K8, lambda i, j: win[:, :, 1024 + j * SW:1024 + (j + 1) * SW]))
    phases.append(Phase("mix2", 0, [], None))
    phases.append(Phase("add", 2, K8, cols(A["w_out_2"][0], (0, SW), (512, 512)), c0=META, w=SEQ, scale=1.0))
    swiglu("ffn2", META, SEQ)
    if upto < 8:
        phases = phases[:marks[upto] + 1]
    elif upto < 11:
        adds = [i for i, ph in enumerate(phases) if ph.kind == "add"]
        phases = phases[:adds[upto - 8] + 1]

    s = 0
    count = dict(t=KD, da=2, db=2, mid=0, pre=0, post=0, hid=0, hh=0, h=KD, fm=2, fs=0, tap=0, ssq=2)
    previous = None
    streams = []
    for ph in phases:
        ph.s0 = s
        ph.base = dict(count)
        s += ph.n * ph.spb
        if ph.n:
            streams.append(ph)
            count["t"] += 4 * ph.n
            count["da"] += 2 * ph.n
            count["db"] += 2 * ph.n
        if ph.kind == "prenorm":
            count["pre"] += 1
        if ph.kind == "postnorm":
            count["post"] += 1
            count["h"] += KD
        ph.before = previous
        if ph.kind in ("add", "postnorm"):
            previous = ph if ph.kind == "add" else None
        if ph.spb == 6:
            count["mid"] += 4 * ph.n
        if ph.kind in ("ffn_in", "swiglu"):
            count["hid"] += KF
            count["hh"] += KF
        if ph.kind == "ffn_in":
            count["fm"] += KF
            count["fs"] += KF
            count["tap"] += 2 * KF
        if ph.kind in ("attention", "sc_b", "cc_mid"):
            count["hid"] += KD
        if ph.kind in ("sc_b", "cc_mid"):
            count["hh"] += KD
        if ph.kind == "mix2":
            count["hid"] += 4
        if ph.kind == "out":
            count["ssq"] += KD
    for prev, ph in zip(streams, streams[1:]):
        prev.nxt, ph.prev = ph, prev
    final = Phase("end", 0, [], None)
    final.base, final.before = count, previous
    n_par_loads = par_loads()

    with ExitStack() as ctx:
        def sb(name, shape, dt=F32):
            return ctx.enter_context(nc.sbuf_tensor(name, shape, dt))

        def sem(name):
            return ctx.enter_context(nc.semaphore(name))

        raw = [sb(f"raw{j}", [P, KD, SW]) for j in range(2)]
        w_hi = [sb(f"w_hi{j}", [P, KD, SW], F32R) for j in range(2)]
        w_lo = [sb(f"w_lo{j}", [P, KD, SW], F32R) for j in range(2)]
        h = sb("h", [P, KD, TW])

        base = nc.sbuf_base
        where = [base]

        def region(nbytes):
            at = where[0]
            where[0] += -(-nbytes // 32) * 32
            return at

        TILE = TW * 4
        R_A = region(2 * KD * TILE)
        R_M = region(2 * KD * TILE)
        R_H = region(2 * KF * TILE)
        R_Q = region(48 * SEQ * 4)
        fence = sb("fence", [P, (where[0] - base) // 4])

        def put(name, shape, offset, dt=F32):
            return nc.alloc_sbuf_tensor_at(name, shape, dt, offset=offset)

        a_hi = put("a_hi", [P, KD, TW], R_A, F32R)
        a_lo = put("a_lo", [P, KD, TW], R_A + KD * TILE, F32R)
        m_out = put("m_out", [P, KD, TW], R_M)
        work = put("work", [P, KD, TW], R_M + KD * TILE)
        hid_hi = put("hid_hi", [P, KF, TW], R_H, F32R)
        hid_lo = put("hid_lo", [P, KF, TW], R_H + KF * TILE, F32R)
        qk = put("qk", [P, 48, SEQ], R_Q)
        v_tok = [put(f"v_tok{t}", [P, 3072], R_H + t * KF * TILE + KD * TILE) for t in range(2)]
        roped = [put(f"roped{j}", [P, 6, SEQ], R_A + j * 6 * SEQ * 4) for j in range(2)]
        prob = [put("prob0", [P, 384], R_A + 12 * SEQ * 4),
                put("prob1", [P, 768], R_A + 12 * SEQ * 4 + 384 * 4)]
        o_tok = put("o_tok", [P, 2, D], R_M)
        probT = [put(f"probT{j}", [P, 384], R_M + 2 * D * 4 + j * 384 * 4) for j in range(3)]
        rope_c = put("rope_c", [P, 3, SEQ], R_M + 2 * D * 4 + 3 * 384 * 4)
        rope_s = sb("rope_s", [P, 3, SEQ])
        cv = put("cv", [P, 4, SEQ], R_Q)
        sg = put("sg", [P, 2, TW], R_Q + 4 * SEQ * 4)
        hs = put("hs", [P, 2, TW], R_Q + 4 * SEQ * 4 + 2 * TILE)
        ch = put("ch", [P, 4, SEQ], R_Q + 4 * SEQ * 4 + 4 * TILE)
        y_sc = put("y_sc", [P, KD, SEQ], R_Q + 4 * SEQ * 4 + 4 * TILE + 4 * SEQ * 4)
        gpad = put("gpad", [P, KD, PAD + SEQ], R_Q + 8192)
        cacc = put("cacc", [P, KD, SEQ], R_Q + 8192 + KD * (PAD + SEQ) * 4)
        p_stage = put("p_stage", [P, 8, P], R_M)
        x_stage = put("x_stage", [P, 2, D], R_Q)
        m_stage = put("m_stage", [META, D], R_Q + 8 * D)
        skew_stage = put("skew_stage", [P, N_BIAS, SKEW], R_Q + 12 * D)
        trig = [put(f"trig{j}", [P, SEQ], R_Q + 25 * D + j * D) for j in range(6)]
        pos_i = put("pos_i", [P, SEQ], R_Q + 32 * D, I32)
        hot = put("hot", [BUCKETS + 1, SKEW], R_Q + 33 * D)
        relw = put("relw", [BUCKETS + 1, N_BIAS, P], R_Q + 35 * D)
        mask_f = put("mask_f", [P, 1152], R_Q + 40 * D)
        z = put("z", [P, 20, TW], R_Q)
        o2 = R_Q + 20 * TILE
        qlat = put("qlat", [P, 8, SEQ], o2)
        c_tok = put("c_tok", [P, 3, 256], o2 + 8 * SEQ * 4)
        va = put("va", [P, 3, 512], o2 + 8 * SEQ * 4 + 3072)
        uk = put("uk", [P, 4, 256], o2 + 8 * SEQ * 4 + 3072 + 6144)
        uv = put("uv", [P, 8, P], o2 + 8 * SEQ * 4 + 3072 + 6144 + 4096)
        tmp1 = put("tmp1", [P, 14, TW], R_H + KD * TILE)
        tmp2 = put("tmp2", [P, 14, TW], R_H + KF * TILE + KD * TILE)
        y_out = put("y_out", [P, 2, D], R_Q)

        par = sb("par", [P, n_par])
        ident = sb("ident", [P, P])
        identb = sb("identb", [P, P], BF16)
        ones = sb("ones", [P, P])
        blk64 = sb("blk64", [P, P])
        maskb = sb("maskb", [P, 1152], BF16)
        trc = sb("trc", [P, 2, SEQ])
        trs = sb("trs", [P, 2, SEQ])
        rstd = sb("rstd", [P, TW])
        std = sb("std", [P, TW])
        ssq = sb("ssq", [P, TW])
        sqt = sb("sqt", [P, 2, TW])
        small = sb("small", [P, 64])
        freq = small[:, 0:2]
        eps_rms, eps_ln = small[:, 2:3], small[:, 3:4]
        nmax, rsum, rinv = small[:, 4:6], small[:, 6:8], small[:, 8:10]
        lam = small[:, 10:11]
        lvec = small[0:HD, 12:16]
        lprod = small[0:HD, 16:18]
        lexp = small[:, 18:20]
        sub08 = small[:, 20:21]
        eps_oa = small[:, 21:22]
        bgain = small[:, 24:32]
        relb = small[0:BUCKETS + 1, 32:40]
        iwq = sb("iwq", [P, 16])
        mark = sb("mark", [P, 26])
        st2 = sb("st2", [P, 16])
        top8 = sb("top8", [P, 8])

        ps = ctx.enter_context(nc.psum_tensor("ps", [P, 8, 512], F32))

        raw_landed = [sem(f"raw_landed{j}") for j in range(2)]
        hi_ready, lo_ready, mid_used = sem("hi_ready"), sem("lo_ready"), sem("mid_used")
        tile_done, drained_a, drained_b = sem("tile_done"), sem("drained_a"), sem("drained_b")
        x_landed, par_landed, const_landed = sem("x_landed"), sem("par_landed"), sem("const_landed")
        pos_landed, lam_landed, rel_landed = sem("pos_landed"), sem("lam_landed"), sem("rel_landed")
        consts_cast, par_turned, par_ready = sem("consts_cast"), sem("par_turned"), sem("par_ready")
        start_set, chain, lam_exp, cc_silu = sem("start_set"), sem("chain"), sem("lam_exp"), sem("cc_silu")
        relw_ready, rel_done, skew_ready, skew_stored, bias_landed = (
            sem("relw_ready"), sem("rel_done"), sem("skew_ready"), sem("skew_stored"), sem("bias_landed"))
        trig_ready, lprod_ready, lam_done, lam_ready, mask_ready = (
            sem("trig_ready"), sem("lprod_ready"), sem("lam_done"), sem("lam_ready"), sem("mask_ready"))
        arg_ready = sem("arg_ready")
        sq_ready, sum_done, std_ready, rstd_ready, an_ready, ahi_ready, a_ready = (
            sem("sq_ready"), sem("sum_done"), sem("std_ready"), sem("rstd_ready"), sem("an_ready"),
            sem("ahi_ready"), sem("a_ready"))
        h_ready, mh_ready = sem("h_ready"), sem("mh_ready")
        ssq_ready, post_sum, post_std, post_rstd = (
            sem("ssq_ready"), sem("post_sum"), sem("post_std"), sem("post_rstd"))
        tap_ready, silu_ready, hid_mul, hid_hi_ready, hid_ready = (
            sem("tap_ready"), sem("silu_ready"), sem("hid_mul"), sem("hid_hi_ready"), sem("hid_ready"))
        rope_in, rope_mid, rope_t1, rope_ready = sem("rope_in"), sem("rope_mid"), sem("rope_t1"), sem("rope_ready")
        sc_done = [sem(f"scores_done{q}") for q in range(2)]
        mx_ready = [sem(f"max_ready{q}") for q in range(2)]
        ex_ready = [sem(f"exp_ready{q}") for q in range(2)]
        rv_ready = [sem(f"rinv_ready{q}") for q in range(2)]
        pt_done = [sem(f"turned{j}") for j in range(3)]
        pt_copied = [sem(f"turned_copied{j}") for j in range(3)]
        o_done = [sem(f"o_done{q}") for q in range(2)]
        o_drained = [sem(f"o_drained{q}") for q in range(2)]
        oT_done, oT_hi = sem("oT_done"), sem("oT_hi")
        out_done, out_copied, out_stored = sem("out_done"), sem("out_copied"), sem("out_stored")
        cc_sum, cc_stat, cc_mu, cc_norm = sem("cc_sum"), sem("cc_stat"), sem("cc_mu"), sem("cc_norm")
        u_landed, tap_mid, sc_tap, cc_tap, tables_ready = (
            sem("u_landed"), sem("tap_mid"), sem("sc_tap"), sem("cc_tap"), sem("tables_ready"))
        oa_clamped = sem("oa_clamped")
        oa_hi, ob_hi, ob_lo = sem("oa_hi"), sem("ob_hi"), sem("ob_lo")
        iw_done, iw_ready = sem("iw_done"), sem("iw_ready")
        ql_done, ql_copied, qn_ready = sem("ql_done"), sem("ql_copied"), sem("qn_ready")
        gn_sq, gn_sum, gn_std, gn_rstd, gn_out = (
            sem("gn_sq"), sem("gn_sum"), sem("gn_std"), sem("gn_rstd"), sem("gn_out"))
        ct_done, ct_copied = sem("ct_done"), sem("ct_copied")
        ix_done, ix_relu, ix_used, sel_ready = sem("ix_done"), sem("ix_relu"), sem("ix_used"), sem("sel_ready")
        s2_done, s2_biased, s2_max, s2_exp, s2_prob = (
            sem("s2_done"), sem("s2_biased"), sem("s2_max"), sem("s2_exp"), sem("s2_prob"))
        t2_done, t2_copied, ol_done, ol_copied, o2_done, o2_copied = (
            sem("t2_done"), sem("t2_copied"), sem("ol_done"), sem("ol_copied"), sem("o2_done"), sem("o2_copied"))

        scratch = nc.dram_tensor("skew_scratch", (P, N_BIAS, SKEW), F32, kind="Internal").ap()

        def bodies(eng, n, body):
            if n > 1:
                with eng.Fori(0, n - 1) as i:
                    body(i, False)
            body(n - 1, True)

        def slot_free(eng, ph, i, j):
            first = isinstance(i, int) and i == 0
            if first and ph.s0 == 0 and j < 2:
                return
            if j == 1:
                eng.wait_ge(tile_done, i * 4 + ph.base["t"])
            elif j == 0 and first:
                if ph.prev.spb == 2:
                    eng.wait_ge(tile_done, ph.base["t"] - 2)
                else:
                    eng.wait_ge(mid_used, ph.base["mid"])
            elif j == 0 and ph.spb == 2:
                eng.wait_ge(tile_done, i * 4 + (ph.base["t"] - 2))
            elif j == 0:
                eng.wait_ge(mid_used, i * 4 + ph.base["mid"])
            elif j == 4:
                eng.wait_ge(tile_done, i * 4 + (ph.base["t"] + 2))
            else:
                eng.wait_ge(mid_used, i * 4 + (ph.base["mid"] + {2: 1, 3: 2, 5: 3}[j]))

        def h_wait(eng, ph, k):
            b = ph.before
            if b is None:
                eng.wait_ge(h_ready, ph.base["h"] - KD + k + 1)
            elif k % 4 < 2:
                eng.wait_ge(drained_a, b.base["da"] + 2 * (k // 4) + k % 2 + 1)
            else:
                eng.wait_ge(drained_b, b.base["db"] + 2 * (k // 4) + k % 2 + 1)

        def slab_view(t, ph, j):
            if ph.kind == "ckv" and j == 1:
                return t[j % 2][:, :, 0:72]
            return t[j % 2][:, 0:ph.kts[j], :]

        KEYS = [META + P, TW]
        KT = [(0, META), (META, P), (META + P, P)]
        tmp1f = tmp1[:].rearrange("p a t -> p (a t)")
        tmp2f = tmp2[:].rearrange("p a t -> p (a t)")
        causal = tmp2[:, 0, :]
        sel_add = [tmp2[:, 3, :], tmp2[:, 4, :]]
        relu = [tmp2[:, 5 + j, :] for j in range(4)]
        o_a = tmp2f[:, 9 * TW:9 * TW + 4 * SEQ].rearrange("p (h t) -> p h t", h=4)
        s2 = [[tmp1[:, 2 * c + m, :] for m in range(2)] for c in range(2)]
        t2 = [tmp1[:, 4 + c, :] for c in range(2)]
        p2 = [tmp1[:, 6 + c, :] for c in range(2)]
        p2T = tmp1f[:, 8 * TW:8 * TW + 3 * P].rearrange("p (k t) -> p k t", k=3)
        olT = tmp1f[:, 10 * TW:10 * TW + 2 * P].rearrange("p (c t) -> p c t", c=2)

        gq, gk, gc, gl = col["a_q_norm_2"], col["a_k_norm_2"], col["b_kv_norm_2"], col["b_q_norm_2"]
        norms = [([z[:, t, :]], blk64, 1.0 / HD, [par[:, gq:gq + 1]]) for t in range(4)]
        norms += [([z[:, 4 + t, :]], blk64, 1.0 / HD, [par[:, gk:gk + 1]]) for t in range(4)]
        norms += [([z[:, 16, :], z[:, 17, :]], ones, 1.0 / 256, [par[:, gc:gc + 1], par[:, gc + 1:gc + 2]])]
        norms += [([qlat[:, 2 * t, :], qlat[:, 2 * t + 1, :]], ones, 1.0 / 256,
                   [par[:, gl:gl + 1], par[:, gl + 1:gl + 2]]) for t in range(4)]
        n_first = len(norms)
        norms += [([o_a[:, t, :]], ones, 1.0 / P, [sub08]) for t in range(4)]
        tiles_before = [sum(len(x[0]) for x in norms[:n]) for n in range(len(norms) + 1)]

        def gn_squares(act, n):
            for k, src in enumerate(norms[n][0]):
                slot = tiles_before[n] + k
                if slot >= KD:
                    owner = max(m for m in range(len(norms)) if tiles_before[m] <= slot - KD)
                    act.wait_ge(gn_sum, owner + 1)
                if n >= n_first:
                    act.wait_ge(oa_clamped, n - n_first + 1)
                act.activation(work[:, slot % KD, 0:src.shape[-1]], src, ACT.Square,
                               scale=1.0 if n < n_first else OA_SCALE).then_inc(gn_sq, 1)

        def gn_root(act, n):
            act.wait_ge(gn_sum, n + 1)
            act.wait_ge(gn_rstd, n)
            if n > n_first:
                act.wait_ge(gn_out, tiles_before[n])
            w = norms[n][0][0].shape[-1]
            act.activation(std[:, 0:w], ps[:, 4 + n % 2, 0:w], ACT.Sqrt, bias=eps_rms if n < n_first else eps_oa, scale=norms[n][2]
                           ).then_inc(gn_std, 1)

        def gn_sums(pe, n):
            srcs, mat = norms[n][0], norms[n][1]
            if n >= 2:
                pe.wait_ge(gn_std, n - 1)
            pe.wait_ge(gn_sq, tiles_before[n + 1])
            for k, src in enumerate(srcs):
                w = src.shape[-1]
                mm = pe.matmul(ps[:, 4 + n % 2, 0:w], mat[:], work[:, (tiles_before[n] + k) % KD, 0:w],
                               start=(k == 0), stop=(k == len(srcs) - 1))
            mm.then_inc(gn_sum, 1)

        def gn_scale(dve, n, link=None):
            srcs, _, _, gains = norms[n]
            w = srcs[0].shape[-1]
            dve.wait_ge(gn_std, n + 1)
            dve.wait_ge(gn_out, tiles_before[n])
            dve.reciprocal(rstd[:, 0:w], std[:, 0:w]).then_inc(gn_rstd, 1)
            dve.wait_ge(gn_rstd, n + 1)
            if n >= n_first:
                link(dve.scalar_tensor_tensor(out=rstd[:, 0:w], in0=std[:, 0:w], scalar=OA_STD_MAX, in1=rstd[:, 0:w],
                                              op0=ALU.is_lt, op1=ALU.mult))
            for src, g in zip(srcs, gains):
                dve.scalar_tensor_tensor(out=src, in0=src, scalar=g, in1=rstd[:, 0:w], op0=ALU.mult,
                                         op1=ALU.mult).then_inc(gn_out, 1)

        def combo(c):
            return (c % 8) // 4, c % 4

        def scores_count(c):
            return 2 * (c + 1) if c < 8 else 16 + (c - 7)

        def mix2_scalar(act, B):
            act.wait_ge(drained_b, B["db"])
            act.wait_ge(drained_a, B["da"])
            for n in range(8):
                act.wait_ge(ql_done, n + 1)
                act.copy(qlat[:, n, :], ps[:, n % 4, 0:SEQ]).then_inc(ql_copied, 1)
            gn_squares(act, 0)
            for n in range(n_first):
                if n + 1 < n_first:
                    if n + 1 == n_first - 4:
                        act.wait_ge(ql_copied, 8)
                    gn_squares(act, n + 1)
                gn_root(act, n)
            for k, (k0, kn) in enumerate(KT):
                act.wait_ge(ct_done, k + 1)
                act.copy(c_tok[0:kn, k, :], ps[0:kn, k, 0:256]).then_inc(ct_copied, 1)
            for n in range(16):
                act.wait_ge(ix_done, n + 1)
                if n >= 4:
                    act.wait_ge(ix_used, n - 3)
                w = KEYS[n // 8]
                act.activation(relu[n % 4][:, 0:w], ps[:, n % 4, 0:w], ACT.Relu, scale=HD ** -0.5
                               ).then_inc(ix_relu, 1)

            def exps(c):
                q, _ = combo(c)
                w = KEYS[q]
                for m in range(2 if c < 8 else 1):
                    act.wait_ge(s2_max, scores_count(c - 1) + m + 1 if c else m + 1)
                    act.activation(s2[c % 2][m][:, 0:w], s2[c % 2][m][:, 0:w], ACT.Exp,
                                   bias=st2[:, 8 * (c % 2) + m:8 * (c % 2) + m + 1],
                                   accum_out=st2[:, 8 * (c % 2) + 2 + m:8 * (c % 2) + 3 + m]).then_inc(s2_exp, 1)

            exps(0)
            for c in range(16):
                if c == 8:
                    act.wait_ge(o2_copied, 8)
                    gn_squares(act, n_first)
                    for n in range(n_first, len(norms)):
                        if n + 1 < len(norms):
                            gn_squares(act, n + 1)
                        gn_root(act, n)
                    for t in range(4):
                        act.wait_ge(gn_out, tiles_before[n_first] + t + 1)
                        act.copy(hid_hi[:, t, 0:SEQ], o_a[:, t, :]).then_inc(oa_hi, 1)
                if c + 1 < 16:
                    exps(c + 1)
                q, head = combo(c)
                act.wait_ge(t2_done, c + 1)
                if 1 <= c <= 8:
                    act.wait_ge(o2_done, c)
                elif c > 8:
                    act.wait_ge(ol_done, c - 8)
                act.copy(p2T[0:META, 0, :], ps[0:META, 6, 0:P])
                act.copy(p2T[:, 1:2 + q, :], ps[:, 6, P:(2 + q) * P].rearrange("p (k t) -> p k t", t=P)
                         ).then_inc(t2_copied, 1)
                if c >= 8:
                    act.wait_ge(ol_done, c - 7)
                    act.wait_ge(o2_done, c)
                    act.copy(olT, ps[:, 7, 0:2 * P].rearrange("p (c t) -> p c t", c=2)).then_inc(ol_copied, 1)
                act.wait_ge(o2_done, c + 1)
                if c < 8:
                    act.copy(o_a[:, head, q * P:(q + 1) * P], ps[:, 5, 0:P]).then_inc(o2_copied, 1)
                else:
                    act.copy(hid_hi[:, 4 + head, q * P:(q + 1) * P], ps[:, 5, 0:P]).then_inc(ob_hi, 1)

        def mix2_vector(dve, B, link):
            for n in range(n_first):
                gn_scale(dve, n)

            dve.wait_ge(bias_landed, 32)
            for q in range(2):
                w = KEYS[q]
                acc = tmp2[:, 1, 0:w]
                other = tmp2[:, 2, 0:w]
                for n in range(8):
                    m = 8 * q + n
                    dve.wait_ge(ix_relu, m + 1)
                    wgt = iwq[:, q * 8 + n:q * 8 + n + 1]
                    if n == 0:
                        dve.wait_ge(drained_b, B["db"])
                        dve.tensor_scalar(acc, relu[m % 4][:, 0:w], wgt, None, ALU.mult).then_inc(ix_used, 1)
                    else:
                        dve.scalar_tensor_tensor(out=acc, in0=relu[m % 4][:, 0:w], scalar=wgt, in1=acc,
                                                 op0=ALU.mult, op1=ALU.add).then_inc(ix_used, 1)
                    dve.wait_ge(ix_used, m + 1)
                link(dve.tensor_tensor(acc, acc, causal[:, TW - w:TW], ALU.add))
                src, dst = acc, other
                for r in range(TOPK // 8):
                    link(dve.max(top8[:], src))
                    link(dve.match_replace(dst, top8[:], src, TAKEN))
                    src, dst = dst, src
                link(dve.tensor_scalar(sel_add[q][:, 0:w], src, TAKEN * 0.5, -NEG, ALU.is_lt, ALU.mult))
                link(dve.tensor_scalar(sel_add[q][:, 0:w], sel_add[q][:, 0:w], NEG, None, ALU.add))

            def biased(c):
                q, head = combo(c)
                w = KEYS[q]
                off = TW - w
                for m in range(2 if c < 8 else 1):
                    n = (scores_count(c - 1) if c else 0) + m
                    dve.wait_ge(s2_done, n + 1)
                    s = s2[c % 2][m][:, 0:w]
                    bank = 2 * (c % 2) + m
                    bias = m_out[:, head + (4 if c >= 8 else 0), off:TW]
                    dve.scalar_tensor_tensor(out=s, in0=ps[:, bank, 0:w], scalar=HD ** -0.5 if c < 8 else 1.0 / 16,
                                             in1=bias, op0=ALU.mult, op1=ALU.add).then_inc(s2_biased, 1)
                    dve.wait_ge(s2_biased, n + 1)
                    if c >= 8:
                        link(dve.tensor_tensor(s, s, sel_add[q][:, 0:w], ALU.add))
                    dve.tensor_reduce(st2[:, 8 * (c % 2) + m:8 * (c % 2) + m + 1], s, AX, ALU.max, negate=True
                                      ).then_inc(s2_max, 1)

            def weights(c):
                q, _ = combo(c)
                w = KEYS[q]
                st = st2[:, 8 * (c % 2):8 * (c % 2) + 8]
                dve.wait_ge(s2_exp, scores_count(c))
                if c >= 2:
                    dve.wait_ge(t2_done, c - 1)
                e0, e1 = s2[c % 2][0][:, 0:w], s2[c % 2][1][:, 0:w]
                if c < 8:
                    link(dve.reciprocal(st[:, 4:6], st[:, 2:4]))
                    link(dve.tensor_tensor(st[:, 6:7], st[:, 5:6], lam, ALU.mult))
                    link(dve.tensor_scalar(t2[c % 2][:, 0:w], e1, st[:, 6:7], None, ALU.mult))
                    dve.scalar_tensor_tensor(out=p2[c % 2][:, 0:w], in0=e0, scalar=st[:, 4:5], in1=t2[c % 2][:, 0:w],
                                             op0=ALU.mult, op1=ALU.subtract).then_inc(s2_prob, 1)
                else:
                    link(dve.reciprocal(st[:, 4:5], st[:, 2:3]))
                    dve.tensor_scalar(p2[c % 2][:, 0:w], e0, st[:, 4:5], None, ALU.mult).then_inc(s2_prob, 1)

            biased(0)
            for c in range(16):
                if c == 8:
                    dve.wait_ge(o2_copied, 8)
                    for t in range(4):
                        dve.tensor_scalar(o_a[:, t, :], o_a[:, t, :], OA_CLAMP, -OA_CLAMP, ALU.min, ALU.max
                                          ).then_inc(oa_clamped, 1)
                    dve.wait_ge(oa_clamped, 4)
                    for n in range(n_first, len(norms)):
                        gn_scale(dve, n, link)
                if c + 1 < 16:
                    biased(c + 1)
                weights(c)
                if c >= 9:
                    low_b(dve, c - 1)
            low_b(dve, 15)

        def low_b(dve, c):
            q, head = combo(c)
            dve.wait_ge(ob_hi, c - 7)
            cols_q = slice(q * P, (q + 1) * P)
            dve.tensor_tensor(hid_lo[:, 4 + head, cols_q], ps[:, 5, 0:P], hid_hi[:, 4 + head, cols_q].bitcast(F32),
                              ALU.subtract).then_inc(ob_lo, 1)

        def mix2_tensor(pe, B):
            pe.wait_ge(u_landed, 32)
            pe.wait_ge(drained_a, B["da"])
            pe.wait_ge(drained_b, B["db"])
            for n in range(8):
                if n >= 4:
                    pe.wait_ge(ql_copied, n - 3)
                pe.matmul(ps[:, n % 4, 0:SEQ], uk[:, n // 2, (n % 2) * P:(n % 2 + 1) * P],
                          z[:, 8 + n // 2, META:TW], start=True, stop=True).then_inc(ql_done, 1)
            for n in range(n_first):
                gn_sums(pe, n)
            pe.wait_ge(gn_out, 10)
            pe.wait_ge(ql_copied, 8)
            for k, (k0, kn) in enumerate(KT):
                for c in range(2):
                    mm = pe.transpose(ps[0:kn, k, c * P:(c + 1) * P], z[:, 16 + c, k0:k0 + kn], ident[:])
                mm.then_inc(ct_done, 1)
            for n in range(16):
                if n < 3:
                    pe.wait_ge(ct_copied, n + 1)
                if n >= 4:
                    pe.wait_ge(ix_relu, n - 3)
                q, head = n // 8, n % 8
                rows = slice((head % 2) * HD, (head % 2 + 1) * HD)
                pe.matmul(ps[:, n % 4, 0:KEYS[q]], z[rows, 12 + head // 2, META + q * P:META + (q + 1) * P],
                          z[rows, 18, 0:KEYS[q]], start=True, stop=True).then_inc(ix_done, 1)
            pe.wait_ge(ix_relu, 16)
            pe.wait_ge(gn_out, tiles_before[n_first])

            def scores(c):
                q, head = combo(c)
                w = KEYS[q]
                if c >= 2:
                    pe.wait_ge(s2_biased, scores_count(c - 2))
                if c < 8:
                    for m in range(2):
                        rows = slice(m * HD, (m + 1) * HD)
                        pe.matmul(ps[:, 2 * (c % 2) + m, 0:w], z[rows, head, META + q * P:META + (q + 1) * P],
                                  z[rows, 4 + head, 0:w], start=True, stop=True).then_inc(s2_done, 1)
                else:
                    for k in range(2):
                        mm = pe.matmul(ps[:, 2 * (c % 2), 0:w], qlat[:, 2 * head + k, q * P:(q + 1) * P],
                                       z[:, 16 + k, 0:w], start=(k == 0), stop=(k == 1))
                    mm.then_inc(s2_done, 1)

            def turn(c):
                q, _ = combo(c)
                pe.wait_ge(s2_prob, c + 1)
                pe.wait_ge(t2_copied, c)
                for k, (k0, kn) in enumerate(KT[:2 + q]):
                    mm = pe.transpose(ps[0:kn, 6, k * P:(k + 1) * P], p2[c % 2][:, k0:k0 + kn], ident[:])
                mm.then_inc(t2_done, 1)

            def values(c):
                q, head = combo(c)
                kts = KT[:2 + q]
                pe.wait_ge(t2_copied, c + 1)
                if c < 8:
                    pe.wait_ge(o2_copied, c)
                    for k, (_, kn) in enumerate(kts):
                        mm = pe.matmul(ps[:, 5, 0:P], va[0:kn, k, head * P:(head + 1) * P], p2T[0:kn, k, :],
                                       start=(k == 0), stop=(k == len(kts) - 1))
                    mm.then_inc(o2_done, 1)
                    return
                pe.wait_ge(ol_copied, c - 8)
                for f in range(2):
                    for k, (_, kn) in enumerate(kts):
                        mm = pe.matmul(ps[:, 7, f * P:(f + 1) * P], c_tok[0:kn, k, f * P:(f + 1) * P],
                                       p2T[0:kn, k, :], start=(k == 0), stop=(k == len(kts) - 1))
                mm.then_inc(ol_done, 1)
                pe.wait_ge(ol_copied, c - 7)
                pe.wait_ge(ob_lo, c - 8)
                pe.wait_ge(gn_std, len(norms))
                for f in range(2):
                    mm = pe.matmul(ps[:, 5, 0:P], uv[:, head * 2 + f, :], olT[:, f, :], start=(f == 0), stop=(f == 1))
                mm.then_inc(o2_done, 1)

            scores(0)
            scores(1)
            for c in range(16):
                turn(c)
                values(c)
                if c == 7:
                    for n in range(n_first, len(norms)):
                        gn_sums(pe, n)
                if c + 2 < 16:
                    scores(c + 2)

        block = ctx.enter_context(nc.Block())

        @block.sync
        def _(sp):
            xv = A["x"][0].rearrange("(t p) d -> p t d", p=P)
            sp.dma_start(x_stage[:], xv).then_inc(x_landed, 16)
            sp.dma_start(m_stage[:], A["meta_tokens_2"]).then_inc(x_landed, 16)
            cst = A["const"]
            sp.dma_start(ident[:], cst[:, C_IDENT:C_IDENT + P]).then_inc(const_landed, 16)
            sp.dma_start(blk64[:], cst[:, C_BLK:C_BLK + P]).then_inc(const_landed, 16)
            sp.dma_start(freq, cst[:, C_FREQ:C_FREQ + 2]).then_inc(const_landed, 16)
            sp.dma_start(mask_f[:], cst[:, C_MASK:C_MASK + 1152]).then_inc(const_landed, 16)
            sp.dma_start(hot[:, 0:SKEW - 1], cst[0:BUCKETS + 1, C_HOT:C_HOT + SKEW - 1]).then_inc(const_landed, 16)
            sp.dma_start(pos_i[:], A["positions"].to_broadcast([P, SEQ])).then_inc(pos_landed, 16)
            for k, name in enumerate(("a_lambda_q1_2", "a_lambda_q2_2", "a_lambda_k1_2", "a_lambda_k2_2")):
                sp.dma_start(lvec[:, k:k + 1], A[name].rearrange("a d -> d a")).then_inc(lam_landed, 16)
            sp.wait_ge(start_set, 1)
            sp.dma_start(relb[0:BUCKETS, :], A["rel_bias_2"]).then_inc(rel_landed, 16)

            for ph in phases:
                if not ph.n:
                    if ph.kind == "mix2":
                        sp.wait_ge(skew_stored, 16)
                        sp.wait_ge(tile_done, ph.base["t"])
                        skew = bass.AP(scratch.tensor, P - 1, [[N_BIAS * SKEW - 1, P], [SKEW, N_BIAS], [1, TW]])
                        sp.dma_start(m_out[:], skew).then_inc(bias_landed, 16)
                        sp.dma_start(tmp2[:, 0, :], A["const"][:, C_CAUSAL:C_CAUSAL + TW]).then_inc(bias_landed, 16)
                        sp.dma_start(uk[:], A["b_w_uk_2"][0].rearrange("h d c -> d h c")).then_inc(u_landed, 16)
                        sp.dma_start(uv[:], A["b_w_uv_2"][0].rearrange("h (c p) d -> p (h c) d", p=P)).then_inc(u_landed, 16)
                    continue

                def load(i, j, first=False):
                    src = ph.src(i, j)
                    if not first:
                        sp.wait_ge(lo_ready, i * ph.spb + (ph.s0 + j - 1))
                    sp.dma_start(slab_view(raw, ph, j), src).then_inc(raw_landed[j % 2], 16)

                if ph.kind in ("z", "cc_in"):
                    for i in range(ph.n):
                        for j in range(ph.spb):
                            load(i, j)
                    continue
                lo = 0
                if ph.s0 == 0:
                    for j in range(2):
                        load(0, j, first=True)
                    lo = 1
                if ph.n > lo + 1:
                    with sp.Fori(lo, ph.n) as i:
                        for j in range(ph.spb):
                            load(i, j)
                elif ph.n > lo:
                    for j in range(ph.spb):
                        load(lo, j)
            sp.wait_ge(out_copied, 4)
            sp.dma_start(out[0].rearrange("(t p) d -> p t d", p=P), y_out[:]).then_inc(out_stored, 16)
            sp.wait_ge(out_stored, 16)

        @block.scalar
        def _(act):
            row = 0
            for name, rows in param_rows():
                src = A[name]
                if name in ("a_q_norm_2", "a_k_norm_2"):
                    for half in range(2):
                        act.dma_start(p_stage[row % P:row % P + 1, row // P, half * HD:(half + 1) * HD],
                                      src).then_inc(par_landed, 16)
                    row += 1
                    continue
                dims = " ".join("abc"[:len(src.shape)])
                flat = src.rearrange(f"{dims} -> ({dims})").rearrange("(r p) -> r p", p=P)
                done = 0
                while done < rows:
                    k = min(rows - done, P - row % P)
                    act.dma_start(p_stage[row % P:row % P + k, row // P, :], flat[done:done + k, :]
                                  ).then_inc(par_landed, 16)
                    done += k
                    row += k
            act.wait_ge(const_landed, 80)
            act.copy(identb[:], ident[:]).then_inc(consts_cast, 1)
            act.copy(maskb[:], mask_f[:]).then_inc(consts_cast, 1)
            for j in range(2):
                act.wait_ge(par_turned, j + 1)
                w = min(512, n_par - 512 * j)
                act.copy(par[:, 512 * j:512 * j + w], ps[:, 4 + j, 0:w]).then_inc(par_ready, 1)
            act.wait_ge(arg_ready, 2)
            act.activation(trig[4][:], trig[2][:], ACT.Sin).then_inc(trig_ready, 1)
            act.activation(trig[5][:], trig[3][:], ACT.Sin).then_inc(trig_ready, 1)
            act.wait_ge(lam_done, 1)
            act.activation(lexp, ps[:, 5, 0:2], ACT.Exp).then_inc(lam_exp, 1)
            for k in range(N_BIAS):
                act.wait_ge(rel_done, k + 1)
                act.copy(skew_stage[:, k, 0:SKEW - 1], ps[:, 6 + k % 2, 0:SKEW - 1]).then_inc(skew_ready, 1)
            act.wait_ge(skew_ready, N_BIAS)
            act.dma_start(scratch[:, :, 0:SKEW - 1], skew_stage[:, :, 0:SKEW - 1]).then_inc(skew_stored, 16)

            def split_hi(ph, i, j):
                act.wait_ge(raw_landed[j % 2], (i * (ph.spb // 2) + (ph.s0 // 2 + j // 2 + 1)) * 16)
                slot_free(act, ph, i, j)
                act.copy(slab_view(w_hi, ph, j), slab_view(raw, ph, j)).then_inc(hi_ready, 1)

            def split_ahead(ph, i, is_last):
                if not is_last:
                    split_hi(ph, i + 1, 0)
                elif ph.nxt is not None:
                    split_hi(ph.nxt, 0, 0)

            split_hi(streams[0], 0, 0)
            act.wait_ge(skew_stored, 16)
            for ph in phases:
                B = ph.base

                if ph.kind == "prenorm":
                    n, c0, w = B["pre"], ph.c0, ph.w
                    for k in range(KD):
                        h_wait(act, ph, k)
                        act.activation(work[:, k, 0:w], h[:, k, c0:c0 + w], ACT.Square).then_inc(sq_ready, 1)
                    act.wait_ge(sum_done, n + 1)
                    act.activation(std[:, 0:w], ps[:, 4, 0:w], ACT.Sqrt, bias=eps_rms, scale=1.0 / D
                                   ).then_inc(std_ready, 1)
                    for k in range(KD):
                        act.wait_ge(an_ready, KD * n + k + 1)
                        act.copy(a_hi[:, k, 0:w], work[:, k, 0:w]).then_inc(ahi_ready, 1)

                elif ph.kind == "postnorm":
                    act.wait_ge(post_sum, B["post"] + 1)
                    act.activation(std[:, 0:SEQ], ps[:, 4, 0:SEQ], ACT.Sqrt, bias=eps_rms, scale=1.0 / D
                                   ).then_inc(post_std, 1)

                elif ph.kind in ("qk", "v", "z"):
                    def body(i, is_last):
                        split_hi(ph, i, 1)
                        for j in range(4):
                            if j == 2:
                                split_ahead(ph, i, is_last)
                            act.wait_ge(tile_done, i * 4 + (B["t"] + j + 1))
                            if ph.kind == "qk":
                                o = qk[:, bass.ds(i * 4 + j, 1), :].rearrange("p a t -> p (a t)")
                                src = ps[:, j, 0:SEQ]
                            elif ph.kind == "z":
                                o = z[:, bass.ds(i * 4 + j, 1), :].rearrange("p a t -> p (a t)")
                                src = ps[:, j, 0:TW]
                            else:
                                o = v_tok[j % 2][:, bass.ds(i * 512 + (j // 2) * SW, SW)]
                                src = ps[:, j, 0:SW]
                            act.copy(o, src).then_inc(drained_a if j < 2 else drained_b, 1)
                    bodies(act, ph.n, body)

                elif ph.kind == "attention":
                    a0 = HEADS * ph.no + 1

                    def exp_unit(q, n):
                        act.wait_ge(mx_ready[q], n + (a0 + 1))
                        if q == 0:
                            act.wait_ge(pt_done[0], n + a0)
                            src = ps[:, 0, 0:384]
                        else:
                            act.wait_ge(pt_done[2], n + a0)
                            src = ps[:, 1:3, :].rearrange("p a c -> p (a c)")[:, 0:768]
                        act.wait_ge(rv_ready[q], n + a0)
                        act.activation(prob[q][:], src, ACT.Exp, bias=nmax[:, q:q + 1],
                                       accum_out=rsum[:, q:q + 1]).then_inc(ex_ready[q], 1)

                    def drain_o(q, n, head):
                        act.wait_ge(rv_ready[q], n + (a0 + 1))
                        act.wait_ge(o_done[q], n + (a0 + 1))
                        act.activation(o_tok[:, q, bass.ds(head * HD, HD)], ps[:, 6 + q, 0:HD], ACT.Copy,
                                       scale=rinv[:, q:q + 1]).then_inc(o_drained[q], 1)

                    exp_unit(0, 0)

                    def body(i, is_last):
                        for m in range(4):
                            n = i * 4 + m
                            exp_unit(1, n)
                            if not (is_last and m == 3):
                                exp_unit(0, n + 1)
                            drain_o(0, n, n)
                            act.wait_ge(pt_done[2], n + (a0 + 1))
                            act.wait_ge(o_done[1], n + a0)
                            act.copy(probT[2][:], ps[:, 5, 0:384]).then_inc(pt_copied[2], 1)
                            drain_o(1, n, n)
                    bodies(act, 4, body)
                    for k in range(KD):
                        act.wait_ge(oT_done, KD * ph.no + k + 1)
                        act.copy(hid_hi[:, k, 0:SEQ], ps[:, k % 4, 0:SEQ]).then_inc(oT_hi, 1)

                elif ph.kind == "out":
                    def drain(i, j):
                        n = i * 4 + j
                        act.wait_ge(tile_done, n + (B["t"] + 1))
                        g = par[:, bass.ds(n + ph.gain, 1)]
                        src = ps[:, j, 0:SEQ]
                        o = m_out[:, bass.ds(n, 1), 0:SEQ].rearrange("p a t -> p (a t)")
                        if ph.bias is None:
                            act.activation(o, src, ACT.Copy, scale=g)
                            bias = 0.0
                        else:
                            act.activation(o, src, ACT.Identity, scale=g, bias=bgain[:, bass.ds(n, 1)])
                            bias = par[:, bass.ds(n + ph.bias, 1)]
                        act.wait_ge(ssq_ready, n + (B["ssq"] - 1))
                        act.activation(sqt[:, j % 2, 0:SEQ], src, ACT.Square, bias=bias
                                       ).then_inc(drained_a if j < 2 else drained_b, 1)

                    def body(i, is_last):
                        if ph.spb == 2:
                            split_hi(ph, i, 1)
                            drain(i, 0)
                            drain(i, 1)
                            split_ahead(ph, i, is_last)
                            drain(i, 2)
                            drain(i, 3)
                        else:
                            split_hi(ph, i, 1)
                            split_hi(ph, i, 2)
                            split_hi(ph, i, 3)
                            drain(i, 0)
                            drain(i, 1)
                            split_hi(ph, i, 4)
                            split_hi(ph, i, 5)
                            split_ahead(ph, i, is_last)
                            drain(i, 2)
                            drain(i, 3)
                    bodies(act, ph.n, body)

                elif ph.kind == "add":
                    def body(i, is_last):
                        for j in range(1, ph.spb):
                            split_hi(ph, i, j)
                        split_ahead(ph, i, is_last)
                    bodies(act, ph.n, body)

                elif ph.kind == "ffn_in":
                    taps = col["ffn_w_conv"] + ph.layer * 3 * 2 * KF

                    def first_tap(i, j):
                        act.wait_ge(tile_done, i * 4 + (B["t"] + j + 1))
                        if j >= 2:
                            act.wait_ge(hid_mul, i * 2 + (B["fm"] + j - 3))
                        g = par[:, bass.ds(i * 2 + (taps + 2 * 2 * KF + (j % 2) + (j // 2) * KF), 1)]
                        act.activation(cv[:, j, :], ps[:, j, 0:SEQ], ACT.Copy, scale=g).then_inc(tap_ready, 1)

                    def body(i, is_last):
                        split_hi(ph, i, 1)
                        first_tap(i, 0)
                        first_tap(i, 1)
                        for j in range(2):
                            act.wait_ge(drained_a, i * 2 + (B["da"] + j + 1))
                            act.wait_ge(hid_mul, i * 2 + (B["fm"] + j - 1))
                            act.activation(sg[:, j, 0:SEQ], cv[:, j, :], ACT.Silu).then_inc(silu_ready, 1)
                        split_ahead(ph, i, is_last)
                        first_tap(i, 2)
                        first_tap(i, 3)
                    bodies(act, ph.n, body)

                elif ph.kind in ("swiglu", "cc_in"):
                    w = ph.w

                    def body(i, is_last):
                        split_hi(ph, i, 1)
                        for j in range(2):
                            act.wait_ge(tile_done, i * 4 + (B["t"] + j + 1))
                            act.wait_ge(drained_b, i * 2 + (B["db"] + j - 1))
                            if ph.kind == "swiglu":
                                act.activation(sg[:, j, 0:w], ps[:, j, 0:w], ACT.Silu).then_inc(drained_a, 1)
                            else:
                                act.activation(sg[:, j, 0:w], ps[:, j, 0:w], ACT.Sigmoid,
                                               bias=par[:, bass.ds(i * 2 + (col["cc_b_pw1"] + KD + j), 1)]
                                               ).then_inc(drained_a, 1)
                        split_ahead(ph, i, is_last)
                    bodies(act, ph.n, body)

                elif ph.kind == "sc_ch":
                    def body(i, is_last):
                        split_hi(ph, i, 1)
                        split_ahead(ph, i, is_last)
                    bodies(act, ph.n, body)

                elif ph.kind == "sc_b":
                    def body(i, is_last):
                        split_hi(ph, i, 1)
                        for j in range(4):
                            if j == 2:
                                split_ahead(ph, i, is_last)
                            sem_j = drained_a if j < 2 else drained_b
                            act.wait_ge(sem_j, i * 2 + (B["da" if j < 2 else "db"] + j % 2 + 1))
                            act.copy(hid_hi[:, i * 4 + j, 0:SEQ], work[:, i * 4 + j, 0:SEQ]).then_inc(hid_hi_ready, 1)
                    for i in range(ph.n):
                        body(i, i == ph.n - 1)

                elif ph.kind == "cc_mid":
                    act.wait_ge(cc_sum, 1)
                    act.activation(std[:, 0:SEQ], ps[:, 4, 0:SEQ], ACT.Copy, scale=1.0 / D).then_inc(cc_mu, 1)
                    for k in range(KD):
                        act.wait_ge(cc_stat, k + 1)
                        act.activation(work[:, k, 0:SEQ], cacc[:, k, :], ACT.Square).then_inc(cc_norm, 1)
                    act.wait_ge(cc_sum, 2)
                    act.activation(std[:, 0:SEQ], ps[:, 5, 0:SEQ], ACT.Sqrt, bias=eps_ln, scale=1.0 / D
                                   ).then_inc(cc_mu, 1)
                    for k in range(KD):
                        act.wait_ge(cc_stat, KD + k + 1)
                        act.activation(work[:, k, 0:SEQ], cacc[:, k, :], ACT.Silu,
                                       scale=par[:, col["cc_ln_g"] + k:col["cc_ln_g"] + k + 1],
                                       bias=par[:, col["cc_ln_b"] + k:col["cc_ln_b"] + k + 1]).then_inc(cc_silu, 1)
                        act.wait_ge(cc_silu, k + 1)
                        act.copy(hid_hi[:, k, 0:SEQ], work[:, k, 0:SEQ]).then_inc(hid_hi_ready, 1)

                elif ph.kind == "ckv":
                    split_hi(ph, 0, 1)
                    for j in range(2):
                        act.wait_ge(tile_done, B["t"] + j + 1)
                        act.copy(z[:, 16 + j, :], ps[:, j, 0:TW]).then_inc(drained_a, 1)
                    split_ahead(ph, 0, True)
                    act.wait_ge(tile_done, B["t"] + 3)
                    act.copy(z[0:HD, 18, :], ps[0:HD, 2, 0:TW])
                    act.copy(z[HD:P, 18, :], ps[0:HD, 2, 0:TW]).then_inc(drained_b, 1)
                    act.wait_ge(tile_done, B["t"] + 4)
                    act.activation(iwq[:], ps[:, 3, 0:16], ACT.Copy, scale=8.0 ** -0.5).then_inc(drained_b, 1)

                elif ph.kind == "va":
                    split_hi(ph, 0, 1)
                    for j in range(4):
                        if j == 2:
                            split_ahead(ph, 0, True)
                        act.wait_ge(tile_done, B["t"] + j + 1)
                        c = (j // 2) * SW
                        if j % 2 == 0:
                            act.copy(va[:, 1, c:c + SW], ps[:, j, 0:SW]).then_inc(drained_a if j < 2 else drained_b, 1)
                        else:
                            act.copy(va[:, 2, c:c + SW], ps[:, j, 0:SW])
                            act.copy(va[0:META, 0, c:c + SW], ps[0:META, j, SW:2 * SW]
                                     ).then_inc(drained_a if j < 2 else drained_b, 1)

                elif ph.kind == "mix2":
                    mix2_scalar(act, B)

            for t in range(4):
                act.wait_ge(out_done, t + 1)
                act.copy(y_out[:, t // 2, (t % 2) * 512:(t % 2 + 1) * 512], ps[:, 4 + t, :]).then_inc(out_copied, 1)

        @block.vector
        def _(dve):
            linked = [0]

            def link(ins):
                linked[0] += 1
                ins.then_inc(chain, 1)
                dve.wait_ge(chain, linked[0])

            dve.memset(relb, NEG).then_inc(start_set, 1)
            dve.wait_ge(start_set, 1)
            dve.memset(eps_rms, 1e-6)
            dve.memset(eps_ln, 1e-5)
            dve.memset(eps_oa, 1e-6 * OA_SCALE ** 2)
            dve.memset(ones[:], 1.0).then_inc(start_set, 1)
            for k, s in enumerate(sc_done + mx_ready + ex_ready + rv_ready + pt_done + pt_copied + o_done
                                  + o_drained + [rope_in, rope_mid, rope_t1, rope_ready]):
                dve.memset(mark[:, 4 + k:5 + k], 0.0).then_inc(s, 1)
            dve.memset(mark[:, 0:1], 0.0).then_inc(drained_a, 2)
            dve.memset(mark[:, 1:2], 0.0).then_inc(drained_b, 2)
            dve.memset(mark[:, 2:3], 0.0).then_inc(ssq_ready, 2)
            dve.memset(mark[:, 3:4], 0.0).then_inc(hid_mul, 2)
            for k in range(KD):
                dve.wait_ge(tile_done, k + 1)
                dve.tensor_copy(h[:, k, :], ps[:, k % 4, 0:TW]).then_inc(h_ready, 1)
            dve.wait_ge(const_landed, 80)
            dve.wait_ge(pos_landed, 16)
            link(dve.tensor_copy(trig[0][:], pos_i[:]))
            link(dve.tensor_scalar(trig[1][:], trig[0][:], freq[:, 0:1], None, ALU.mult))
            link(dve.tensor_scalar(trig[0][:], trig[1][:], 1.0 / TWO_PI, ROUND, ALU.mult, ALU.add))
            link(dve.tensor_scalar(trig[0][:], trig[0][:], ROUND, None, ALU.subtract))
            for part in (PI_A, PI_B, PI_C):
                link(dve.scalar_tensor_tensor(out=trig[1][:], in0=trig[0][:], scalar=-part, in1=trig[1][:],
                                              op0=ALU.mult, op1=ALU.add))
            edge = 3.1415925
            link(dve.tensor_scalar(trig[3][:], trig[1][:], math.pi / 2, None, ALU.add))
            link(dve.tensor_scalar(trig[0][:], trig[3][:], math.pi, -TWO_PI, ALU.is_gt, ALU.mult))
            link(dve.tensor_tensor(trig[3][:], trig[3][:], trig[0][:], ALU.add))
            dve.tensor_scalar(trig[2][:], trig[1][:], edge, -edge, ALU.min, ALU.max).then_inc(arg_ready, 1)
            dve.tensor_scalar(trig[3][:], trig[3][:], edge, -edge, ALU.min, ALU.max).then_inc(arg_ready, 1)
            dve.wait_ge(lam_landed, 64)
            dve.tensor_tensor(lprod, lvec[:, 0:2], lvec[:, 2:4], ALU.mult).then_inc(lprod_ready, 1)
            dve.wait_ge(rel_landed, 16)
            for k in range(N_BIAS):
                last_rel = dve.tensor_scalar(relw[:, k, :], ones[0:BUCKETS + 1, :], relb[:, k:k + 1], None, ALU.mult)
            last_rel.then_inc(relw_ready, 1)
            dve.wait_ge(trig_ready, 2)
            link(dve.tensor_scalar(trs[:, 1, :], trig[4][:], freq[:, 1:2], None, ALU.mult))
            dve.tensor_scalar(trs[:, 0, :], trs[:, 1, :], 0.125, None, ALU.mult)
            dve.tensor_copy(trc[:, 1, :], trig[5][:])
            dve.tensor_scalar(trc[:, 0, :], trig[5][:], 0.125, None, ALU.mult).then_inc(tables_ready, 1)
            dve.wait_ge(par_ready, 2)
            g0, b0 = col["mix_norm_post"] + 2 * KD, col["cc_b_pw2"]
            dve.tensor_tensor(bgain, par[:, g0:g0 + KD], par[:, b0:b0 + KD], ALU.mult)
            dve.tensor_scalar(sub08, par[:, col["a_subln_2"]:col["a_subln_2"] + 1], (1.0 - LAM_INIT) * OA_SCALE, None, ALU.mult)
            dve.wait_ge(lam_exp, 1)
            dve.scalar_tensor_tensor(out=lam, in0=lexp[:, 0:1], scalar=LAM_INIT, in1=lexp[:, 1:2], op0=ALU.add,
                                     op1=ALU.subtract).then_inc(lam_ready, 1)
            dve.wait_ge(lam_ready, 1)

            def split_lo(ph, i, j):
                dve.wait_ge(hi_ready, i * ph.spb + (ph.s0 + j + 1))
                dve.tensor_tensor(slab_view(w_lo, ph, j), slab_view(raw, ph, j), slab_view(w_hi, ph, j).bitcast(F32),
                                  ALU.subtract).then_inc(lo_ready, 1)

            def split_ahead(ph, i, is_last):
                if not is_last:
                    split_lo(ph, i + 1, 0)
                elif ph.nxt is not None:
                    split_lo(ph.nxt, 0, 0)

            split_lo(streams[0], 0, 0)
            for ph in phases:
                B = ph.base

                if ph.kind == "prenorm":
                    n, c0, w = B["pre"], ph.c0, ph.w
                    dve.wait_ge(std_ready, n + 1)
                    dve.reciprocal(rstd[:, 0:w], std[:, 0:w]).then_inc(rstd_ready, 1)
                    dve.wait_ge(rstd_ready, n + 1)
                    for k in range(KD):
                        dve.scalar_tensor_tensor(out=work[:, k, 0:w], in0=h[:, k, c0:c0 + w],
                                                 scalar=par[:, ph.gain + k:ph.gain + k + 1], in1=rstd[:, 0:w],
                                                 op0=ALU.mult, op1=ALU.mult).then_inc(an_ready, 1)

                elif ph.kind == "postnorm":
                    dve.wait_ge(post_std, B["post"] + 1)
                    dve.reciprocal(rstd[:, 0:SEQ], std[:, 0:SEQ]).then_inc(post_rstd, 1)
                    dve.wait_ge(post_rstd, B["post"] + 1)
                    for k in range(KD):
                        dve.tensor_tensor(m_out[:, k, 0:SEQ], m_out[:, k, 0:SEQ], rstd[:, 0:SEQ], ALU.mult
                                          ).then_inc(mh_ready, 1)

                elif ph.kind in ("qk", "v", "z", "out", "va", "ckv"):
                    def body(i, is_last):
                        for j in range(1, ph.spb):
                            split_lo(ph, i, j)
                        split_ahead(ph, i, is_last)
                    bodies(dve, ph.n, body)

                elif ph.kind == "add":
                    w = ph.w

                    def add(i, j):
                        dve.wait_ge(tile_done, i * 4 + (B["t"] + j + 1))
                        o = h[:, bass.ds(i * 4 + j, 1), ph.c0:ph.c0 + w].rearrange("p a t -> p (a t)")
                        dve.scalar_tensor_tensor(out=o, in0=ps[:, j, 0:w], scalar=ph.scale, in1=o, op0=ALU.mult,
                                                 op1=ALU.add).then_inc(drained_a if j < 2 else drained_b, 1)

                    def body(i, is_last):
                        split_lo(ph, i, 1)
                        if ph.spb == 6:
                            split_lo(ph, i, 2)
                            split_lo(ph, i, 3)
                        add(i, 0)
                        add(i, 1)
                        if ph.spb == 6:
                            split_lo(ph, i, 4)
                            split_lo(ph, i, 5)
                        split_ahead(ph, i, is_last)
                        add(i, 2)
                        add(i, 3)
                    bodies(dve, ph.n, body)

                elif ph.kind == "attention":
                    a0 = HEADS * ph.no + 1
                    r0 = HEADS * ph.no + 1

                    def rope(p, slot, part):
                        n = p * 2 + part
                        src = qk[:].rearrange("p (a g e) t -> p a g e t", a=2, g=3)[:, part, :, bass.ds(p, 1), :
                                                                                  ].rearrange("p g e t -> p g (e t)")
                        dve.wait_ge(rope_ready, n + r0)
                        dve.tensor_tensor(rope_s[:], src, trs[:, part:part + 1, :].to_broadcast([P, GROUPS, SEQ]),
                                          ALU.mult).then_inc(rope_in, 1)
                        dve.wait_ge(rope_in, n + (r0 + 1))
                        dve.tensor_copy(mark[:, 1:2], mark[:, 0:1])
                        dve.stream_shuffle(rope_s[:], rope_s[:], [(j + 8) % 16 if j < 16 else j for j in range(32)]
                                           ).then_inc(rope_mid, 1)

                    def row_max(q, n):
                        dve.wait_ge(sc_done[q], n + (a0 + 1))
                        dve.wait_ge(ex_ready[q], n + a0)
                        src = ps[:, 0, 0:384] if q == 0 else ps[:, 1:3, :].rearrange("p a c -> p (a c)")[:, 0:768]
                        dve.tensor_reduce(nmax[:, q:q + 1], src, AX, ALU.max, negate=True).then_inc(mx_ready[q], 1)

                    def inverse(q, n):
                        dve.wait_ge(ex_ready[q], n + (a0 + 1))
                        dve.wait_ge(o_drained[q], n + a0)
                        dve.reciprocal(rinv[:, q:q + 1], rsum[:, q:q + 1]).then_inc(rv_ready[q], 1)

                    def copy_turned(j, n):
                        dve.wait_ge(pt_done[j], n + (a0 + 1))
                        dve.wait_ge(o_done[min(j, 1)], n + a0)
                        dve.tensor_copy(probT[j][:], ps[:, 3 + j, 0:384]).then_inc(pt_copied[j], 1)

                    dve.wait_ge(tile_done, B["t"])
                    dve.wait_ge(drained_a, B["da"])
                    dve.wait_ge(drained_b, B["db"])
                    rope(0, 0, 0)
                    rope(0, 0, 1)
                    row_max(0, 0)

                    def body(i, is_last):
                        for m in range(4):
                            n = i * 4 + m
                            row_max(1, n)
                            inverse(0, n)
                            copy_turned(0, n)
                            if not (is_last and m >= 2):
                                rope(i * 2 + (m // 2 + 1), (m // 2 + 1) % 2, m % 2)
                            if not (is_last and m == 3):
                                row_max(0, n + 1)
                            inverse(1, n)
                            copy_turned(1, n)
                    bodies(dve, 4, body)
                    for k in range(KD):
                        dve.wait_ge(oT_hi, KD * ph.no + k + 1)
                        dve.tensor_tensor(hid_lo[:, k, 0:SEQ], ps[:, k % 4, 0:SEQ], hid_hi[:, k, 0:SEQ].bitcast(F32),
                                          ALU.subtract).then_inc(hid_ready, 1)

                elif ph.kind == "ffn_in":
                    taps = col["ffn_w_conv"] + ph.layer * 3 * 2 * KF

                    def tap(i, j, back):
                        g = par[:, bass.ds(i * 2 + (taps + (2 - back) * 2 * KF + (j % 2) + (j // 2) * KF), 1)]
                        return dve.scalar_tensor_tensor(out=cv[:, j, back:SEQ], in0=ps[:, j, 0:SEQ - back], scalar=g,
                                                        in1=cv[:, j, back:SEQ], op0=ALU.mult, op1=ALU.add)

                    def conv(i, js):
                        for j in js:
                            dve.wait_ge(tap_ready, i * 4 + (B["tap"] + j + 1))
                            tap(i, j, 1).then_inc(tap_mid, 1)
                        for j in js:
                            dve.wait_ge(tap_mid, i * 4 + (B["tap"] + j + 1))
                            tap(i, j, 2).then_inc(drained_a if j < 2 else drained_b, 1)

                    def body(i, is_last):
                        split_lo(ph, i, 1)
                        conv(i, (0, 1))
                        split_ahead(ph, i, is_last)
                        conv(i, (2, 3))
                    bodies(dve, ph.n, body)

                elif ph.kind in ("swiglu", "cc_in"):
                    w = ph.w
                    if ph.kind == "cc_in":
                        dve.memset(gpad[:, :, 0:PAD], 0.0)

                    def body(i, is_last):
                        split_lo(ph, i, 1)
                        split_ahead(ph, i, is_last)
                        dve.wait_ge(drained_a, i * 2 + (B["da"] + 2))
                        for j in range(2):
                            dve.wait_ge(tile_done, i * 4 + (B["t"] + 3 + j))
                            if ph.kind == "swiglu":
                                dve.wait_ge(hid_ready, i * 2 + (B["hid"] + j - 1))
                                dve.tensor_tensor(hs[:, j, 0:w], ps[:, 2 + j, 0:w], sg[:, j, 0:w], ALU.mult
                                                  ).then_inc(drained_b, 1)
                            else:
                                o = gpad[:, bass.ds(i * 2 + j, 1), PAD:PAD + SEQ].rearrange("p a t -> p (a t)")
                                dve.scalar_tensor_tensor(
                                    out=o, in0=ps[:, 2 + j, 0:w],
                                    scalar=par[:, bass.ds(i * 2 + (col["cc_b_pw1"] + j), 1)],
                                    in1=sg[:, j, 0:w], op0=ALU.add, op1=ALU.mult).then_inc(drained_b, 1)
                    bodies(dve, ph.n, body)

                elif ph.kind == "sc_ch":
                    def body(i, is_last):
                        split_lo(ph, i, 1)
                        for j in range(2):
                            dve.wait_ge(tile_done, i * 4 + (B["t"] + j + 1))
                            dve.tensor_copy(ch[:, j, :], ps[:, j, 0:SEQ]).then_inc(drained_a, 1)
                        split_ahead(ph, i, is_last)
                        for j in range(2):
                            dve.wait_ge(tile_done, i * 4 + (B["t"] + 3 + j))
                            dve.wait_ge(drained_a, i * 2 + (B["da"] + j + 1))
                            dve.tensor_tensor(ch[:, 2 + j, :], ps[:, 2 + j, 0:SEQ], ch[:, j, :], ALU.mult
                                              ).then_inc(drained_b, 1)
                        w0 = col["sc_w_conv"]
                        for back in range(3):
                            for j in range(2):
                                dve.wait_ge(drained_b, i * 2 + (B["db"] + j + 1))
                                g = par[:, bass.ds(i * 2 + (w0 + (2 - back) * KD + j), 1)]
                                o = y_sc[:, bass.ds(i * 2 + j, 1), back:SEQ].rearrange("p a t -> p (a t)")
                                src = ch[:, 2 + j, 0:SEQ - back]
                                if back == 0:
                                    dve.tensor_scalar(o, src, g, None, ALU.mult).then_inc(sc_tap, 1)
                                else:
                                    dve.wait_ge(sc_tap, i * 6 + (2 * back - 1 + j))
                                    dve.scalar_tensor_tensor(out=o, in0=src, scalar=g, in1=o, op0=ALU.mult,
                                                             op1=ALU.add).then_inc(sc_tap, 1)
                    bodies(dve, ph.n, body)
                    dve.wait_ge(sc_tap, 6 * ph.n)

                elif ph.kind == "sc_b":
                    for i in range(ph.n):
                        split_lo(ph, i, 1)
                        for j in range(4):
                            if j == 2:
                                split_ahead(ph, i, i == ph.n - 1)
                            dve.wait_ge(tile_done, i * 4 + (B["t"] + j + 1))
                            dve.tensor_tensor(work[:, 4 * i + j, 0:SEQ], ps[:, j, 0:SEQ], y_sc[:, 4 * i + j, :], ALU.mult
                                              ).then_inc(drained_a if j < 2 else drained_b, 1)

                elif ph.kind == "cc_mid":
                    w0, b0 = col["cc_w_dw"], col["cc_b_dw"]
                    dve.wait_ge(drained_b, B["db"])
                    for k in range(KD):
                        g = w0 + (TAPS - 1) * KD + k
                        dve.tensor_scalar(cacc[:, k, :], gpad[:, k, PAD:PAD + SEQ], par[:, g:g + 1],
                                          par[:, b0 + k:b0 + k + 1], ALU.mult, ALU.add).then_inc(cc_tap, 1)
                    with dve.Fori(0, TAPS - 1) as j:
                        for k in range(KD):
                            dve.wait_ge(cc_tap, j * KD + (k + 1))
                            dve.scalar_tensor_tensor(out=cacc[:, k, :], in0=gpad[:, k, bass.ds(j, SEQ)],
                                                     scalar=par[:, bass.ds(j * KD + (w0 + k), 1)], in1=cacc[:, k, :],
                                                     op0=ALU.mult, op1=ALU.add).then_inc(cc_tap, 1)
                    dve.wait_ge(cc_mu, 1)
                    for k in range(KD):
                        dve.tensor_tensor(cacc[:, k, :], cacc[:, k, :], std[:, 0:SEQ], ALU.subtract).then_inc(cc_stat, 1)
                    dve.wait_ge(cc_mu, 2)
                    link(dve.reciprocal(rstd[:, 0:SEQ], std[:, 0:SEQ]))
                    for k in range(KD):
                        dve.tensor_tensor(cacc[:, k, :], cacc[:, k, :], rstd[:, 0:SEQ], ALU.mult).then_inc(cc_stat, 1)

                elif ph.kind == "mix2":
                    mix2_vector(dve, B, link)

        @block.gpsimd
        def _(pool):
            for ph in phases:
                B = ph.base

                if ph.kind == "prenorm":
                    n, w = B["pre"], ph.w
                    for k in range(KD):
                        pool.wait_ge(ahi_ready, KD * n + k + 1)
                        pool.tensor_tensor(a_lo[:, k, 0:w], work[:, k, 0:w], a_hi[:, k, 0:w].bitcast(F32), ALU.subtract
                                           ).then_inc(a_ready, 1)

                elif ph.kind == "postnorm":
                    for k in range(KD):
                        pool.wait_ge(mh_ready, KD * B["post"] + k + 1)
                        pool.tensor_tensor(h[:, k, META:TW], h[:, k, META:TW], m_out[:, k, 0:SEQ], ALU.add
                                           ).then_inc(h_ready, 1)

                elif ph.kind == "out":
                    for n in range(KD):
                        j = n % 4
                        d, k0 = (drained_a, B["da"]) if j < 2 else (drained_b, B["db"])
                        pool.wait_ge(d, k0 + 2 * (n // 4) + j % 2 + 1)
                        if n == 0:
                            pool.tensor_copy(ssq[:, 0:SEQ], sqt[:, 0, 0:SEQ]).then_inc(ssq_ready, 1)
                        else:
                            pool.wait_ge(ssq_ready, B["ssq"] + n)
                            pool.tensor_tensor(ssq[:, 0:SEQ], ssq[:, 0:SEQ], sqt[:, j % 2, 0:SEQ], ALU.add
                                               ).then_inc(ssq_ready, 1)

                elif ph.kind in ("ffn_in", "swiglu"):
                    w = ph.w

                    def body(i, is_last):
                        for j in range(2):
                            if ph.kind == "ffn_in":
                                pool.wait_ge(silu_ready, i * 2 + (B["fs"] + j + 1))
                                pool.wait_ge(drained_b, i * 2 + (B["db"] + j + 1))
                                pool.tensor_tensor(hs[:, j, 0:w], sg[:, j, 0:w], cv[:, 2 + j, :], ALU.mult
                                                   ).then_inc(hid_mul, 1)
                                pool.wait_ge(hid_mul, i * 2 + (B["fm"] + j + 1))
                            else:
                                pool.wait_ge(drained_b, i * 2 + (B["db"] + j + 1))
                            hi = hid_hi[:, bass.ds(i * 2 + j, 1), 0:w].rearrange("p a t -> p (a t)")
                            lo = hid_lo[:, bass.ds(i * 2 + j, 1), 0:w].rearrange("p a t -> p (a t)")
                            pool.tensor_copy(hi, hs[:, j, 0:w]).then_inc(hid_hi_ready, 1)
                            pool.wait_ge(hid_hi_ready, i * 2 + (B["hh"] + j + 1))
                            pool.tensor_tensor(lo, hs[:, j, 0:w], hi.bitcast(F32), ALU.subtract).then_inc(hid_ready, 1)
                    bodies(pool, ph.n, body)

                elif ph.kind in ("sc_b", "cc_mid"):
                    for k in range(KD):
                        pool.wait_ge(hid_hi_ready, B["hh"] + k + 1)
                        pool.tensor_tensor(hid_lo[:, k, 0:SEQ], work[:, k, 0:SEQ], hid_hi[:, k, 0:SEQ].bitcast(F32),
                                           ALU.subtract).then_inc(hid_ready, 1)

                elif ph.kind == "attention":
                    r0 = HEADS * ph.no + 1

                    def rope(p, slot, part):
                        n = p * 2 + part
                        src = qk[:].rearrange("p (a g e) t -> p a g e t", a=2, g=3)[:, part, :, bass.ds(p, 1), :
                                                                                  ].rearrange("p g e t -> p g (e t)")
                        o = roped[slot][:, 3 * part:3 * part + 3, :]
                        pool.wait_ge(rope_ready, n + r0)
                        pool.tensor_tensor(rope_c[:], src, trc[:, part:part + 1, :].to_broadcast([P, GROUPS, SEQ]),
                                           ALU.mult).then_inc(rope_t1, 1)
                        pool.wait_ge(rope_t1, n + (r0 + 1))
                        pool.wait_ge(rope_mid, n + (r0 + 1))
                        pool.tensor_tensor(o, rope_c[:], rope_s[:], ALU.add).then_inc(rope_ready, 1)

                    pool.wait_ge(tables_ready, 1)
                    pool.wait_ge(tile_done, B["t"])
                    pool.wait_ge(drained_a, B["da"])
                    pool.wait_ge(drained_b, B["db"])
                    rope(0, 0, 0)
                    rope(0, 0, 1)

                    def body(i, is_last):
                        for m in range(4):
                            if not (is_last and m >= 2):
                                pool.wait_ge(sc_done[1], i * 4 + (a0 + 2 * (m // 2)))
                                rope(i * 2 + (m // 2 + 1), (m // 2 + 1) % 2, m % 2)
                    a0 = HEADS * ph.no + 1
                    bodies(pool, 4, body)

                elif ph.kind == "mix2":
                    for t in range(4):
                        pool.wait_ge(oa_hi, t + 1)
                        pool.tensor_tensor(hid_lo[:, t, 0:SEQ], o_a[:, t, :], hid_hi[:, t, 0:SEQ].bitcast(F32),
                                           ALU.subtract).then_inc(hid_ready, 1)

        @block.tensor
        def _(pe):
            pe.wait_ge(const_landed, 80)
            pe.wait_ge(x_landed, 32)
            for k in range(KD):
                if k >= 4:
                    pe.wait_ge(h_ready, k - 3)
                cs = slice(k * P, (k + 1) * P)
                pe.transpose(ps[:, k % 4, 0:META], m_stage[0:META, cs], ident[0:META, 0:META])
                pe.transpose(ps[:, k % 4, META:META + P], x_stage[:, 0, cs], ident[:])
                pe.transpose(ps[:, k % 4, META + P:TW], x_stage[:, 1, cs], ident[:]).then_inc(tile_done, 1)
            pe.wait_ge(par_landed, 16 * n_par_loads)
            for t in range(n_par_tiles):
                r = min(P, n_par - t * P)
                mm = pe.transpose(ps[:, 4 + t // 4, (t % 4) * P:(t % 4) * P + r], p_stage[0:r, t, :], ident[0:r, 0:r])
                if t % 4 == 3 or t == n_par_tiles - 1:
                    mm.then_inc(par_turned, 1)
            pe.wait_ge(par_ready, 2)
            pe.wait_ge(start_set, 2)
            pe.wait_ge(lprod_ready, 1)
            pe.matmul(ps[:, 5, 0:2], ones[0:HD, :], lprod, start=True, stop=True).then_inc(lam_done, 1)
            pe.wait_ge(relw_ready, 1)
            for k in range(N_BIAS):
                if k >= 2:
                    pe.wait_ge(skew_ready, k - 1)
                pe.matmul(ps[:, 6 + k % 2, 0:SKEW - 1], relw[:, k, :], hot[:, 0:SKEW - 1], start=True, stop=True
                          ).then_inc(rel_done, 1)

            def mm3(o, wh, wl, xh, xl, start, stop):
                pe.matmul(o, wh, xh, start=start, stop=False)
                pe.matmul(o, wh, xl, start=False, stop=False)
                return pe.matmul(o, wl, xh, start=False, stop=stop)

            def bank_free(ph, i, j):
                if j < 2:
                    pe.wait_ge(drained_a, i * 2 + (ph.base["da"] + j - 1))
                else:
                    pe.wait_ge(drained_b, i * 2 + (ph.base["db"] + j - 3))

            def slab_split(ph, i, j):
                pe.wait_ge(lo_ready, i * ph.spb + (ph.s0 + j + 1))

            for ph in phases:
                B = ph.base

                if ph.kind == "prenorm":
                    n, w = B["pre"], ph.w
                    for k in range(KD):
                        pe.wait_ge(sq_ready, KD * n + k + 1)
                        mm = pe.matmul(ps[:, 4, 0:w], ones[:], work[:, k, 0:w], start=(k == 0), stop=(k == KD - 1))
                    mm.then_inc(sum_done, 1)

                elif ph.kind == "postnorm":
                    pe.wait_ge(ssq_ready, B["ssq"])
                    pe.matmul(ps[:, 4, 0:SEQ], ones[:], ssq[:, 0:SEQ], start=True, stop=True).then_inc(post_sum, 1)

                elif ph.kind in ("qk", "sc_ch", "sc_b", "cc_in", "ffn_in", "swiglu", "z"):
                    pe.wait_ge(a_ready, KD * B["pre"])
                    w = TW if ph.kind == "z" else ph.w

                    def body(i):
                        for j in range(4):
                            if j % 2 == 0:
                                slab_split(ph, i, j // 2)
                            bank_free(ph, i, j)
                            c = slice((j % 2) * P, (j % 2 + 1) * P)
                            for k in range(KD):
                                mm = mm3(ps[:, j, 0:w], w_hi[j // 2][:, k, c], w_lo[j // 2][:, k, c],
                                         a_hi[:, k, 0:w], a_lo[:, k, 0:w], k == 0, k == KD - 1)
                            mm.then_inc(tile_done, 1)
                    with pe.Fori(0, ph.n) as i:
                        body(i)

                elif ph.kind == "v":
                    with pe.Fori(0, ph.n) as i:
                        for j in range(4):
                            if j % 2 == 0:
                                slab_split(ph, i, j // 2)
                            bank_free(ph, i, j)
                            c = slice((j % 2) * P, (j % 2 + 1) * P)
                            for k in range(KD):
                                mm = mm3(ps[:, j, 0:SW], a_hi[:, k, c], a_lo[:, k, c],
                                         w_hi[j // 2][:, k, :], w_lo[j // 2][:, k, :], k == 0, k == KD - 1)
                            mm.then_inc(tile_done, 1)

                elif ph.kind in ("out", "add"):
                    pe.wait_ge(hid_ready, B["hid"])
                    if ph.kind == "add" and ph.spb == 2:
                        pe.wait_ge(ob_lo, 8)
                    w = ph.w
                    if ph.spb == 2:
                        with pe.Fori(0, ph.n) as i:
                            for j in range(4):
                                if j % 2 == 0:
                                    slab_split(ph, i, j // 2)
                                bank_free(ph, i, j)
                                c = slice((j % 2) * P, (j % 2 + 1) * P)
                                for k in range(KD):
                                    mm = mm3(ps[:, j, 0:w], w_hi[j // 2][:, k, c], w_lo[j // 2][:, k, c],
                                             hid_hi[:, k, 0:w], hid_lo[:, k, 0:w], k == 0, k == KD - 1)
                                mm.then_inc(tile_done, 1)
                    else:
                        with pe.Fori(0, ph.n) as i:
                            for pair in range(2):
                                k0 = 0
                                for part in range(3):
                                    s = 3 * pair + part
                                    slab_split(ph, i, s)
                                    kn = ph.kts[s]
                                    for t in range(2):
                                        j = 2 * pair + t
                                        if part == 0:
                                            bank_free(ph, i, j)
                                        c = slice(t * P, (t + 1) * P)
                                        for k in range(kn):
                                            mm = mm3(ps[:, j, 0:w], w_hi[s % 2][:, k, c], w_lo[s % 2][:, k, c],
                                                     hid_hi[:, k0 + k, 0:w], hid_lo[:, k0 + k, 0:w],
                                                     k0 + k == 0, k0 + k == KF - 1)
                                        if part == 2:
                                            mm.then_inc(tile_done, 1)
                                    if part < 2:
                                        mm.then_inc(mid_used, 1)
                                    k0 += kn

                elif ph.kind == "ckv":
                    for j in range(3):
                        if j % 2 == 0:
                            slab_split(ph, 0, j // 2)
                        bank_free(ph, 0, j)
                        c = slice((j % 2) * P, (j % 2 + 1) * P)
                        for k in range(KD):
                            mm = mm3(ps[:, j, 0:TW], w_hi[j // 2][:, k, c], w_lo[j // 2][:, k, c],
                                     a_hi[:, k, :], a_lo[:, k, :], k == 0, k == KD - 1)
                        mm.then_inc(tile_done, 1)
                    bank_free(ph, 0, 3)
                    for q in range(2):
                        c = slice(META + q * P, META + (q + 1) * P)
                        for k in range(KD):
                            mm = mm3(ps[:, 3, 8 * q:8 * q + 8], a_hi[:, k, c], a_lo[:, k, c],
                                     w_hi[1][:, k, HD:HD + 8], w_lo[1][:, k, HD:HD + 8], k == 0, k == KD - 1)
                    mm.then_inc(tile_done, 1)

                elif ph.kind == "va":
                    for j in range(4):
                        if j % 2 == 0:
                            slab_split(ph, 0, j // 2)
                        bank_free(ph, 0, j)
                        parts = [(META, 0)] if j % 2 == 0 else [(META + P, 0), (0, SW)]
                        for t0, c0 in parts:
                            c = slice(t0, t0 + P)
                            for k in range(KD):
                                mm = mm3(ps[:, j, c0:c0 + SW], a_hi[:, k, c], a_lo[:, k, c],
                                         w_hi[j // 2][:, k, :], w_lo[j // 2][:, k, :], k == 0, k == KD - 1)
                        mm.then_inc(tile_done, 1)

                elif ph.kind == "attention":
                    a0 = HEADS * ph.no + 1

                    def scores(q, n, slot, half):
                        pe.wait_ge(ex_ready[q], n + a0)
                        rows = slice(half * HD, (half + 1) * HD)
                        wk = (q + 1) * P
                        outs = [(0, g * wk) for g in range(3)] if q == 0 else [(1, 0), (1, 256), (2, 0)]
                        for g, (bank, c) in enumerate(outs):
                            pe.matmul(ps[:, bank, c:c + wk], roped[slot][rows, g, q * P:(q + 1) * P],
                                      roped[slot][rows, 3 + g, 0:wk], start=True, stop=False, skip_group_check=True)
                            m0 = 0 if q == 0 else 384
                            mm = pe.matmul(ps[:, bank, c:c + wk], identb[:], maskb[:, m0 + g * wk:m0 + (g + 1) * wk],
                                           start=False, stop=True, skip_group_check=True)
                        mm.then_inc(sc_done[q], 1)

                    def turn(j, n):
                        q = min(j, 1)
                        pe.wait_ge(ex_ready[q], n + (a0 + 1))
                        pe.wait_ge(pt_copied[j], n + a0)
                        b0 = 3 if j == 2 else 0
                        for b in range(3):
                            mm = pe.transpose(ps[:, 3 + j, b * P:(b + 1) * P],
                                              prob[q][:, (b0 + b) * P:(b0 + b + 1) * P], ident[:])
                        mm.then_inc(pt_done[j], 1)

                    def values(j, n, head):
                        q = min(j, 1)
                        pe.wait_ge(pt_copied[j], n + (a0 + 1))
                        if j < 2:
                            pe.wait_ge(o_drained[q], n + a0)
                        for b in range(3):
                            blk = b + (3 if j == 2 else 0)
                            g, kt = (blk, 0) if q == 0 else (blk // 2, blk % 2)
                            mm = pe.matmul(ps[:, 6 + q, 0:HD], probT[j][:, b * P:(b + 1) * P],
                                           v_tok[kt][:, bass.ds(head * HD + g * D, HD)],
                                           start=(b == 0 and j < 2), stop=(b == 2 and j != 1))
                        if j != 1:
                            mm.then_inc(o_done[q], 1)

                    pe.wait_ge(consts_cast, 2)
                    pe.wait_ge(drained_a, B["da"])
                    pe.wait_ge(drained_b, B["db"])
                    pe.wait_ge(rope_ready, a0 + 2)
                    scores(0, 0, 0, 0)

                    def body(i, is_last):
                        for m in range(4):
                            n = i * 4 + m
                            scores(1, n, m // 2, m % 2)
                            turn(0, n)
                            if not (is_last and m == 3):
                                if m % 2 == 1:
                                    pe.wait_ge(rope_ready, i * 4 + (a0 + 2 * (m // 2) + 4))
                                scores(0, n + 1, ((m + 1) // 2) % 2, (m + 1) % 2)
                            values(0, n, n)
                            turn(1, n)
                            turn(2, n)
                            values(1, n, n)
                            values(2, n, n)
                    bodies(pe, 4, body)
                    pe.wait_ge(o_drained[0], a0 + HEADS)
                    pe.wait_ge(o_drained[1], a0 + HEADS)
                    for k in range(KD):
                        if k >= 4:
                            pe.wait_ge(hid_ready, B["hid"] + k - 3)
                        for q in range(2):
                            mm = pe.transpose(ps[:, k % 4, q * P:(q + 1) * P], o_tok[:, q, k * P:(k + 1) * P], ident[:])
                        mm.then_inc(oT_done, 1)

                elif ph.kind == "cc_mid":
                    pe.wait_ge(cc_tap, TAPS * KD)
                    for k in range(KD):
                        mm = pe.matmul(ps[:, 4, 0:SEQ], ones[:], cacc[:, k, :], start=(k == 0), stop=(k == KD - 1))
                    mm.then_inc(cc_sum, 1)
                    for k in range(KD):
                        pe.wait_ge(cc_norm, k + 1)
                        mm = pe.matmul(ps[:, 5, 0:SEQ], ones[:], work[:, k, 0:SEQ], start=(k == 0), stop=(k == KD - 1))
                    mm.then_inc(cc_sum, 1)

                elif ph.kind == "mix2":
                    mix2_tensor(pe, B)

            for t in range(2):
                for k in range(KD):
                    h_wait(pe, final, k)
                    mm = pe.transpose(ps[:, 4 + 2 * t + k // 4, (k % 4) * P:(k % 4 + 1) * P],
                                      h[:, k, META + t * P:META + (t + 1) * P], ident[:])
                    if k % 4 == 3:
                        mm.then_inc(out_done, 1)


_INS = ['x', 'positions', 'mix_norm_pre', 'mix_norm_post', 'ffn_norm_pre', 'ffn_norm_post', 'attn_w_qkv',
        'attn_w_o', 'sc_w_in', 'sc_w_conv', 'sc_w_out', 'cc_w_pw1', 'cc_b_pw1', 'cc_w_dw', 'cc_b_dw', 'cc_ln_g',
        'cc_ln_b', 'cc_w_pw2', 'cc_b_pw2', 'ffn_w_in', 'ffn_w_conv', 'ffn_w_out', 'meta_tokens_2', 'rel_bias_2',
        'ffn1_norm_2', 'ffn1_w_gate_2', 'ffn1_w_up_2', 'ffn1_w_down_2', 'mix_norm_2', 'w_in_2', 'a_q_norm_2',
        'a_k_norm_2', 'a_lambda_q1_2', 'a_lambda_k1_2', 'a_lambda_q2_2', 'a_lambda_k2_2', 'a_subln_2',
        'b_kv_norm_2', 'b_w_uk_2', 'b_q_norm_2', 'b_w_uv_2', 'w_out_2', 'ffn2_norm_2', 'ffn2_w_gate_2',
        'ffn2_w_up_2', 'ffn2_w_down_2']


def kernel(**inputs):
    import numpy as _np
    import concourse.bacc as _bacc
    from concourse.bass_utils import run_bass_kernel_spmd as _run

    nc = _bacc.Bacc("TRN2", target_bir_lowering=False, num_devices=1)
    arrays, args = {}, {}
    for name in _INS + ["const"]:
        a = constants() if name == "const" else _np.ascontiguousarray(inputs[name])
        arrays[f"in_{name}_dram"] = a
        args[name] = nc.dram_tensor(f"in_{name}_dram", a.shape, mybir.dt.from_np(a.dtype), kind="ExternalInput").ap()
    out = nc.dram_tensor("out_0_dram", (1, SEQ, D), F32, kind="ExternalOutput").ap()
    build(nc, args, out)
    r = _run(nc, [arrays], core_ids=[0])
    return r.results[0]["out_0_dram"]
```

```python
import math
from contextlib import ExitStack

import numpy as np
import concourse.bass as bass
from concourse import mybir

F32 = mybir.dt.float32
F32R = mybir.dt.float32r
BF16 = mybir.dt.bfloat16
I32 = mybir.dt.int32
ALU = mybir.AluOpType
ACT = mybir.ActivationFunctionType
AX = mybir.AxisListType.X

P = 128
SEQ = 256
META = 16
TW = SEQ + META
D = 1024
KD = D // P
FF = 2816
KF = FF // P
DEPTH = 4
NEG = -1.0e30
TAKEN = -3.0e38
TAPS = 31
PAD = TAPS - 1
CC_POOL, CC_DVE, CC_PE = (0,), (1, 2, 3, 4), (5, 6, 7)
SW = 256
GROUPS = 3
HEADS = 16
HD = 64
N_BIAS = 8
BUCKETS = 32
SKEW = 400
TOPK = SEQ // 4
LAM_INIT = 0.8 - 0.6 * math.exp(0.0)
OA_CLAMP = 2.0 ** 65
OA_SCALE = 2.0 ** -10
OA_STD_MAX = math.sqrt(2.0 ** 128 * OA_SCALE ** 2 / P)
TWO_PI = 2.0 * math.pi
PI_A = 6.28125
PI_B = float(np.float32(np.floor((TWO_PI - PI_A) * 2.0 ** 20) / 2.0 ** 20))
PI_C = TWO_PI - PI_A - PI_B
ROUND = 1.5 * 2.0 ** 23

GN_EARLY = 8

C_IDENT, C_BLK, C_FREQ, C_SIGN, C_HOT, C_CAUSAL = 0, 128, 256, 257, 258, 258 + SKEW
C_MASK = C_CAUSAL + TW
C_END = C_MASK + 1152


def constants():
    c = np.zeros((P, C_END), np.float32)
    p = np.arange(P)
    c[:, C_IDENT:C_IDENT + P] = np.eye(P)
    c[:, C_BLK:C_BLK + P] = (p[:, None] // HD == p[None, :] // HD)
    rot = p % HD < 16
    inv = np.float32(500000.0) ** (-np.arange(0, 16, 2, dtype=np.float32) / np.float32(16))
    c[:, C_FREQ] = np.where(rot, inv[p % 8], 0.0)
    c[:, C_SIGN] = np.where(p % HD < 8, 1.0, -1.0)
    half = BUCKETS // 2
    for i in range(SKEW - 1):
        n = TW - 1 - i
        if n < 0:
            b = BUCKETS
        elif n < half:
            b = n
        else:
            large = np.float32(np.log(np.float32(n) / np.float32(half))) / np.float32(math.log(128 / half))
            b = min(half + int(np.float32(large * np.float32(half))), BUCKETS - 1)
        c[b, C_HOT + i] = 1.0
    k = np.arange(TW)
    c[:, C_CAUSAL:C_CAUSAL + TW] = np.where(k[None, :] > (P + META + p)[:, None], NEG, 0.0)
    at = C_MASK
    for qt in range(2):
        for window, dil in ((128, 1), (512, 4), (2048, 16)):
            dist = (qt * P + p)[:, None] - np.arange((qt + 1) * P)[None, :]
            ok = (dist >= 0) & (dist % dil == 0) & (dist <= window)
            c[:, at:at + (qt + 1) * P] = np.where(ok, 0.0, NEG)
            at += (qt + 1) * P
    return c


TABLES = {"ffn_in": ACT.Silu, "swiglu": ACT.Silu, "cc_in": ACT.Sigmoid, "qk": ACT.Exp}


class Phase:

    def __init__(self, kind, n, kts, src, c0=META, w=SEQ, gain=0, bias=None, scale=1.0, layer=0, no=0):
        self.kind, self.n, self.kts, self.src = kind, n, kts, src
        self.spb = len(kts)
        self.c0, self.w = c0, w
        self.gain, self.bias, self.scale, self.layer, self.no = gain, bias, scale, layer, no
        self.s0, self.base, self.before, self.prev, self.nxt = 0, {}, None, None, None


def param_rows():
    return [
        ("mix_norm_pre", DEPTH * KD), ("mix_norm_post", DEPTH * KD), ("ffn_norm_pre", DEPTH * KD),
        ("ffn_norm_post", DEPTH * KD), ("ffn_w_conv", DEPTH * 3 * 2 * KF), ("sc_w_conv", 3 * KD),
        ("cc_b_pw1", 2 * KD), ("cc_w_dw", TAPS * KD), ("cc_b_dw", KD), ("cc_ln_g", KD),
        ("cc_ln_b", KD), ("cc_b_pw2", KD), ("ffn1_norm_2", KD), ("mix_norm_2", KD),
        ("ffn2_norm_2", KD), ("a_subln_2", 1), ("b_kv_norm_2", 2), ("b_q_norm_2", 2),
        ("a_q_norm_2", 1), ("a_k_norm_2", 1),
    ]


def par_loads():
    n, row = 0, 0
    for name, rows in param_rows():
        if name in ("a_q_norm_2", "a_k_norm_2"):
            n += 2
        else:
            n += (row + rows - 1) // P - row // P + 1
        row += rows
    return n


def build(nc, A, out):
    col, at = {}, 0
    for name, rows in param_rows():
        col[name] = at
        at += rows
    n_par = at
    n_par_tiles = -(-n_par // P)

    def kmajor(w):
        return w.rearrange("(k p) n -> p k n", p=P)

    phases = []

    def cols(w, first, step):
        v = kmajor(w)
        return lambda i, j: v[:, :, bass.ds(i * step[j] + first[j], SW)]

    def ffn_out(w):
        v = kmajor(w)
        ks = [(0, 8), (8, 15), (15, 22)]
        return lambda i, j: v[:, ks[j % 3][0]:ks[j % 3][1], bass.ds(i * 2 * SW + (j // 3) * SW, SW)]

    K8 = [KD, KD]
    K22 = [8, 7, 7, 8, 7, 7]
    attn_no = 0
    for l in range(DEPTH):
        kind = l % 3
        gain = dict(gain=col["mix_norm_post"] + l * KD)
        phases.append(Phase("prenorm", 0, [], None, gain=col["mix_norm_pre"] + l * KD, c0=META, w=SEQ))
        if kind == 0:
            wq, wo = A["attn_w_qkv"][l // 3], A["attn_w_o"][l // 3]
            phases.append(Phase("qk", 12, K8, cols(wq, (0, SW), (512, 512))))
            phases.append(Phase("v", 6, K8, cols(wq, (6144, 6144 + SW), (512, 512)), no=attn_no))
            phases.append(Phase("attention", 0, [], None, no=attn_no))
            attn_no += 1
            phases.append(Phase("out", 2, K8, cols(wo, (0, SW), (512, 512)), **gain))
        elif kind == 1:
            wi, wo = A["sc_w_in"][0], A["sc_w_out"][0]
            phases.append(Phase("sc_ch", 4, K8, cols(wi, (D, 2 * D), (SW, SW))))
            phases.append(Phase("sc_b", 2, K8, cols(wi, (0, SW), (512, 512))))
            phases.append(Phase("out", 2, K8, cols(wo, (0, SW), (512, 512)), **gain))
        else:
            wi, wo = A["cc_w_pw1"][0], A["cc_w_pw2"][0]
            phases.append(Phase("cc_in", 4, K8, cols(wi, (D, 0), (SW, SW))))
            phases.append(Phase("cc_mid", 0, [], None))
            phases.append(Phase("out", 2, K8, cols(wo, (0, SW), (512, 512)), bias=col["cc_b_pw2"], **gain))
        phases.append(Phase("postnorm", 0, [], None))
        phases.append(Phase("prenorm", 0, [], None, gain=col["ffn_norm_pre"] + l * KD, c0=META, w=SEQ))
        phases.append(Phase("ffn_in", 11, K8, cols(A["ffn_w_in"][l], (0, FF), (SW, SW)), layer=l))
        phases.append(Phase("out", 2, K22, ffn_out(A["ffn_w_out"][l]),
                            gain=col["ffn_norm_post"] + l * KD))
        phases.append(Phase("postnorm", 0, [], None))

    def swiglu(tag, c0, w):
        phases.append(Phase("prenorm", 0, [], None, gain=col[tag + "_norm_2"], c0=c0, w=w))
        g, u = kmajor(A[tag + "_w_gate_2"][0]), kmajor(A[tag + "_w_up_2"][0])
        phases.append(Phase("swiglu", 11, K8, lambda i, j: (g, u)[j][:, :, bass.ds(i * SW, SW)], c0=c0, w=w))
        phases.append(Phase("add", 2, K22, ffn_out(A[tag + "_w_down_2"][0]), c0=c0, w=w, scale=0.5))

    swiglu("ffn1", 0, TW)
    phases.append(Phase("prenorm", 0, [], None, gain=col["mix_norm_2"], c0=0, w=TW))
    win = kmajor(A["w_in_2"][0])
    z_cols = [0, 512, 1536, 2304]
    phases.append(Phase("z", 4, K8, lambda i, j: win[:, :, z_cols[i] + j * SW:z_cols[i] + (j + 1) * SW]))
    phases.append(Phase("ckv", 1, K8, lambda i, j: win[:, :, 2048:2304] if j == 0 else win[:, :, 2816:2888]))
    phases.append(Phase("va", 1, K8, lambda i, j: win[:, :, 1024 + j * SW:1024 + (j + 1) * SW]))
    phases.append(Phase("mix2", 0, [], None))
    phases.append(Phase("add", 2, K8, cols(A["w_out_2"][0], (0, SW), (512, 512)), c0=META, w=SEQ, scale=1.0))
    swiglu("ffn2", META, SEQ)

    s = 0
    count = dict(t=KD, da=2, db=2, mid=0, pre=0, post=0, hid=0, hh=0, h=KD, fm=2, fs=2, tap=0, ssq=2)
    previous = None
    streams = []
    for ph in phases:
        ph.s0 = s
        ph.base = dict(count)
        s += ph.n * ph.spb
        if ph.n:
            streams.append(ph)
            count["t"] += 4 * ph.n
            count["da"] += 2 * ph.n
            count["db"] += 2 * ph.n
        if ph.kind == "prenorm":
            count["pre"] += 1
        if ph.kind == "postnorm":
            count["post"] += 1
            count["h"] += KD
        ph.follows = None
        ph.before = previous
        if ph.kind in ("add", "postnorm"):
            previous = ph if ph.kind == "add" else None
        if ph.spb == 6:
            count["mid"] += 4 * ph.n
        if ph.kind in ("ffn_in", "swiglu"):
            count["hid"] += KF
            count["hh"] += KF
        if ph.kind == "ffn_in":
            count["fm"] += KF
            count["fs"] += KF
            count["tap"] += 2 * KF
        if ph.kind in ("attention", "sc_b", "cc_mid"):
            count["hid"] += KD
        if ph.kind in ("sc_b", "cc_mid"):
            count["hh"] += KD
        if ph.kind == "mix2":
            count["hid"] += 4
        if ph.kind == "out":
            count["ssq"] += KD
    for ph, after in zip(phases, phases[1:]):
        ph.follows, after.prior = after.kind, ph
    for prev, ph in zip(streams, streams[1:]):
        prev.nxt, ph.prev = ph, prev
    final = Phase("end", 0, [], None)
    final.base, final.before = count, previous
    n_par_loads = par_loads()

    with ExitStack() as ctx:
        def sb(name, shape, dt=F32):
            return ctx.enter_context(nc.sbuf_tensor(name, shape, dt))

        def sem(name):
            return ctx.enter_context(nc.semaphore(name))

        raw = [sb(f"raw{j}", [P, KD, SW]) for j in range(2)]
        w_hi = [sb(f"w_hi{j}", [P, KD, SW], F32R) for j in range(2)]
        w_lo = [sb(f"w_lo{j}", [P, KD, SW], F32R) for j in range(2)]
        h = sb("h", [P, KD, TW])

        base = nc.sbuf_base
        where = [base]

        def region(nbytes):
            at = where[0]
            where[0] += -(-nbytes // 32) * 32
            return at

        TILE = TW * 4
        R_A = region(2 * KD * TILE)
        R_M = region(2 * KD * TILE)
        R_H = region(2 * KF * TILE)
        R_Q = region(48 * SEQ * 4)
        sb("regions", [P, (where[0] - base) // 4])

        def put(name, shape, offset, dt=F32):
            return nc.alloc_sbuf_tensor_at(name, shape, dt, offset=offset)

        a_hi = put("a_hi", [P, KD, TW], R_A, F32R)
        a_lo = put("a_lo", [P, KD, TW], R_A + KD * TILE, F32R)
        m_out = put("m_out", [P, KD, TW], R_M)
        work = put("work", [P, KD, TW], R_M + KD * TILE)
        hid_hi = put("hid_hi", [P, KF, TW], R_H, F32R)
        hid_lo = put("hid_lo", [P, KF, TW], R_H + KF * TILE, F32R)
        qk = put("qk", [P, 48, SEQ], R_Q)
        v_tok = [put(f"v_tok{t}", [P, 3072], R_H + t * KF * TILE + KD * TILE) for t in range(2)]
        roped = [put(f"roped{j}", [P, 6, SEQ], R_H + j * KF * TILE) for j in range(2)]
        prob = [put("prob0", [P, 384], R_A + 12 * SEQ * 4),
                put("prob1", [P, 768], R_A + 12 * SEQ * 4 + 384 * 4)]
        o_tok = put("o_tok", [P, 2, D], R_M)
        probT = [put(f"probT{j}", [P, 384], R_M + 2 * D * 4 + j * 384 * 4) for j in range(3)]
        rope_c = put("rope_c", [P, 3, SEQ], R_M + 2 * D * 4 + 3 * 384 * 4)
        rope_s = sb("rope_s", [P, 3, SEQ])
        cv = put("cv", [P, 4, SEQ], R_Q)
        sg = put("sg", [P, 2, TW], R_Q + 4 * SEQ * 4)
        hs = put("hs", [P, 2, TW], R_Q + 4 * SEQ * 4 + 2 * TILE)
        ch = put("ch", [P, 4, SEQ], R_Q + 4 * SEQ * 4 + 4 * TILE)
        y_sc = put("y_sc", [P, KD, SEQ], R_Q + 4 * SEQ * 4 + 4 * TILE + 4 * SEQ * 4)
        gpad = put("gpad", [P, KD, PAD + SEQ], R_Q + 8192)
        cacc = put("cacc", [P, KD, SEQ], R_Q + 8192 + KD * (PAD + SEQ) * 4)
        diag = put("diag", [P, len(CC_PE) * TAPS, P], R_H)
        p_stage = put("p_stage", [P, 8, P], R_M)
        x_stage = put("x_stage", [P, 2, D], R_Q)
        m_stage = put("m_stage", [META, D], R_Q + 8 * D)
        skew_stage = put("skew_stage", [P, N_BIAS, SKEW], R_Q + 26 * D)
        trig = [put(f"trig{j}", [P, SEQ], R_Q + 25 * D + j * D) for j in range(6)]
        pos_i = put("pos_i", [P, SEQ], R_Q + 32 * D, I32)
        hot = put("hot", [BUCKETS + 1, SKEW], R_Q + 39 * D)
        relw = put("relw", [BUCKETS + 1, N_BIAS, P], R_Q + 41 * D)
        mask_f = put("mask_f", [P, 1152], R_Q + 40 * D)
        z = put("z", [P, 20, TW], R_Q)
        o2 = R_Q + 20 * TILE
        qlat = put("qlat", [P, 8, SEQ], o2)
        c_tok = put("c_tok", [P, 3, 256], o2 + 8 * SEQ * 4)
        va = put("va", [P, 3, 512], o2 + 8 * SEQ * 4 + 3072)
        uk = put("uk", [P, 4, 256], o2 + 8 * SEQ * 4 + 3072 + 6144)
        uv = put("uv", [P, 8, P], o2 + 8 * SEQ * 4 + 3072 + 6144 + 4096)
        tmp1 = put("tmp1", [P, 14, TW], R_H + KD * TILE)
        tmp2 = put("tmp2", [P, 14, TW], R_H + KF * TILE + KD * TILE)
        y_out = put("y_out", [P, 2, D], R_Q)

        par = sb("par", [P, n_par])
        ident = sb("ident", [P, P])
        identb = sb("identb", [P, P], BF16)
        ones = sb("ones", [P, P])
        blk64 = sb("blk64", [P, P])
        maskb = sb("maskb", [P, 1152], BF16)
        trc = sb("trc", [P, 2, SEQ])
        trs = sb("trs", [P, 2, SEQ])
        rstd = sb("rstd", [P, TW])
        std = sb("std", [P, TW])
        ssq = sb("ssq", [P, TW])
        sqt = sb("sqt", [P, 2, TW])
        small = sb("small", [P, 64])
        freq = small[:, 0:2]
        eps_rms, eps_ln = small[:, 2:3], small[:, 3:4]
        nmax, rsum, rinv = small[:, 4:6], small[:, 6:8], small[:, 8:10]
        lam = small[:, 10:11]
        lvec = small[0:HD, 12:16]
        lprod = small[0:HD, 16:18]
        lexp = small[:, 18:20]
        sub08 = small[:, 20:21]
        bgain = small[:, 24:32]
        relb = small[0:BUCKETS + 1, 32:40]
        iwq = sb("iwq", [P, 16])
        mark = sb("mark", [P, 27])
        warm = sb("warm", [P, 64])
        st2 = sb("st2", [P, 16])
        top8 = sb("top8", [P, 8])

        ps = ctx.enter_context(nc.psum_tensor("ps", [P, 8, 512], F32))

        raw_landed = [sem(f"raw_landed{j}") for j in range(2)]
        hi_ready, lo_ready, mid_used = sem("hi_ready"), sem("lo_ready"), sem("mid_used")
        tile_done, drained_a, drained_b = sem("tile_done"), sem("drained_a"), sem("drained_b")
        x_landed, ident_landed, const_landed = sem("x_landed"), sem("ident_landed"), sem("const_landed")
        hot_landed = sem("hot_landed")
        par_landed, par_landed_pool = sem("par_landed"), sem("par_landed_pool")
        pos_landed, lam_landed, rel_landed = sem("pos_landed"), sem("lam_landed"), sem("rel_landed")
        consts_cast, par_turned, par_ready = sem("consts_cast"), sem("par_turned"), sem("par_ready")
        start_set, chain, lam_exp, cc_silu = sem("start_set"), sem("chain"), sem("lam_exp"), sem("cc_silu")
        relw_ready, rel_done, skew_ready, skew_stored, bias_landed = (
            sem("relw_ready"), sem("rel_done"), sem("skew_ready"), sem("skew_stored"), sem("bias_landed"))
        trig_ready, lprod_ready, lam_done, lam_ready = (
            sem("trig_ready"), sem("lprod_ready"), sem("lam_done"), sem("lam_ready"))
        arg_ready = sem("arg_ready")
        sq_ready, sum_done, std_ready, rstd_ready, an_ready, ahi_ready, a_ready = (
            sem("sq_ready"), sem("sum_done"), sem("std_ready"), sem("rstd_ready"), sem("an_ready"),
            sem("ahi_ready"), sem("a_ready"))
        h_ready, mh_ready = sem("h_ready"), sem("mh_ready")
        ssq_ready, post_sum, post_std, post_rstd = (
            sem("ssq_ready"), sem("post_sum"), sem("post_std"), sem("post_rstd"))
        tap_ready, silu_ready, hid_mul, hid_hi_ready, hid_ready = (
            sem("tap_ready"), sem("silu_ready"), sem("hid_mul"), sem("hid_hi_ready"), sem("hid_ready"))
        rope_in, rope_mid, rope_t1, rope_ready = sem("rope_in"), sem("rope_mid"), sem("rope_t1"), sem("rope_ready")
        sc_done = [sem(f"scores_done{q}") for q in range(2)]
        mx_ready = [sem(f"max_ready{q}") for q in range(2)]
        ex_ready = [sem(f"exp_ready{q}") for q in range(2)]
        rv_ready = [sem(f"rinv_ready{q}") for q in range(2)]
        pt_done = [sem(f"turned{j}") for j in range(3)]
        pt_copied = [sem(f"turned_copied{j}") for j in range(3)]
        o_done = [sem(f"o_done{q}") for q in range(2)]
        o_drained = [sem(f"o_drained{q}") for q in range(2)]
        oT_done, oT_hi = sem("oT_done"), sem("oT_hi")
        out_done, out_copied, out_stored = sem("out_done"), sem("out_copied"), sem("out_stored")
        cc_sum, cc_stat, cc_mu, cc_norm = sem("cc_sum"), sem("cc_stat"), sem("cc_mu"), sem("cc_norm")
        cc_tap_pool, diag_ready, cc_product, cc_drained = (
            sem("cc_tap_pool"), sem("diag_ready"), sem("cc_product"), sem("cc_drained"))
        u_landed, tap_mid, sc_tap, cc_tap, tables_ready = (
            sem("u_landed"), sem("tap_mid"), sem("sc_tap"), sem("cc_tap"), sem("tables_ready"))
        oa_clamped, oa_sq, oa_sum, oa_var, oa_root, oa_out = (
            sem("oa_clamped"), sem("oa_sq"), sem("oa_sum"), sem("oa_var"), sem("oa_root"), sem("oa_out"))
        oa_hi, ob_hi, ob_lo = sem("oa_hi"), sem("ob_hi"), sem("ob_lo")
        ql_done, ql_copied = sem("ql_done"), sem("ql_copied")
        gn_sq, gn_sum, gn_std, gn_rstd, gn_out = (
            sem("gn_sq"), sem("gn_sum"), sem("gn_std"), sem("gn_rstd"), sem("gn_out"))
        ct_done, ct_copied = sem("ct_done"), sem("ct_copied")
        ix_done, ix_relu, ix_used = sem("ix_done"), sem("ix_relu"), sem("ix_used")
        s2_done, s2_biased, s2_max, s2_exp, s2_prob = (
            sem("s2_done"), sem("s2_biased"), sem("s2_max"), sem("s2_exp"), sem("s2_prob"))
        t2_done, t2_copied, ol_done, ol_copied, o2_done, o2_copied = (
            sem("t2_done"), sem("t2_copied"), sem("ol_done"), sem("ol_copied"), sem("o2_done"), sem("o2_copied"))

        scratch = nc.dram_tensor("skew_scratch", (P, N_BIAS, SKEW), F32, kind="Internal").ap()

        def bodies(eng, n, body):
            if n > 1:
                with eng.Fori(0, n - 1) as i:
                    body(i, False)
            body(n - 1, True)

        def slot_free(eng, ph, i, j):
            first = isinstance(i, int) and i == 0
            if first and ph.s0 == 0 and j < 2:
                return
            if j == 1:
                eng.wait_ge(tile_done, i * 4 + ph.base["t"])
            elif j == 0 and first:
                if ph.prev.spb == 2:
                    eng.wait_ge(tile_done, ph.base["t"] - 2)
                else:
                    eng.wait_ge(mid_used, ph.base["mid"])
            elif j == 0 and ph.spb == 2:
                eng.wait_ge(tile_done, i * 4 + (ph.base["t"] - 2))
            elif j == 0:
                eng.wait_ge(mid_used, i * 4 + ph.base["mid"])
            elif j == 4:
                eng.wait_ge(tile_done, i * 4 + (ph.base["t"] + 2))
            else:
                eng.wait_ge(mid_used, i * 4 + (ph.base["mid"] + {2: 1, 3: 2, 5: 3}[j]))

        def h_wait(eng, ph, k):
            b = ph.before
            if b is None:
                eng.wait_ge(h_ready, ph.base["h"] - KD + k + 1)
            elif k % 4 < 2:
                eng.wait_ge(drained_a, b.base["da"] + 2 * (k // 4) + k % 2 + 1)
            else:
                eng.wait_ge(drained_b, b.base["db"] + 2 * (k // 4) + k % 2 + 1)

        def slab_view(t, ph, j):
            if ph.kind == "ckv" and j == 1:
                return t[j % 2][:, :, 0:72]
            return t[j % 2][:, 0:ph.kts[j], :]

        KEYS = [META + P, TW]
        KT = [(0, META), (META, P), (META + P, P)]
        tmp1f = tmp1[:].rearrange("p a t -> p (a t)")
        tmp2f = tmp2[:].rearrange("p a t -> p (a t)")
        causal = tmp2[:, 0, :]
        sel_add = [tmp2[:, 3, :], tmp2[:, 4, :]]
        relu = [tmp2[:, 5 + j, :] for j in range(4)]
        oa_std = [tmp2f[:, 5 * TW + t * SEQ:5 * TW + (t + 1) * SEQ] for t in range(4)]
        oa_std_all = tmp2f[:, 5 * TW:5 * TW + 4 * SEQ]
        o_a = tmp2f[:, 9 * TW:9 * TW + 4 * SEQ].rearrange("p (h t) -> p h t", h=4)
        s2 = [[tmp1[:, 2 * c + m, :] for m in range(2)] for c in range(2)]
        t2 = [tmp1[:, 4 + c, :] for c in range(2)]
        p2 = [tmp1[:, 6 + c, :] for c in range(2)]
        p2T = tmp1f[:, 8 * TW:8 * TW + 3 * P].rearrange("p (k t) -> p k t", k=3)
        olT = tmp1f[:, 10 * TW:10 * TW + 2 * P].rearrange("p (c t) -> p c t", c=2)

        gq, gk, gc, gl = col["a_q_norm_2"], col["a_k_norm_2"], col["b_kv_norm_2"], col["b_q_norm_2"]
        norms = [([z[:, t, :]], blk64, 1.0 / HD, [par[:, gq:gq + 1]]) for t in range(4)]
        norms += [([z[:, 4 + t, :]], blk64, 1.0 / HD, [par[:, gk:gk + 1]]) for t in range(4)]
        norms += [([z[:, 16, :], z[:, 17, :]], ones, 1.0 / 256, [par[:, gc:gc + 1], par[:, gc + 1:gc + 2]])]
        norms += [([qlat[:, 2 * t, :], qlat[:, 2 * t + 1, :]], ones, 1.0 / 256,
                   [par[:, gl:gl + 1], par[:, gl + 1:gl + 2]]) for t in range(4)]
        tiles_before = [sum(len(x[0]) for x in norms[:n]) for n in range(len(norms) + 1)]

        def gn_squares(act, n):
            for k, src in enumerate(norms[n][0]):
                slot = tiles_before[n] + k
                if slot >= KD:
                    owner = max(m for m in range(len(norms)) if tiles_before[m] <= slot - KD)
                    act.wait_ge(gn_sum, owner + 1)
                act.activation(work[:, slot % KD, 0:src.shape[-1]], src, ACT.Square).then_inc(gn_sq, 1)

        def gn_root(act, n):
            act.wait_ge(gn_sum, n + 1)
            act.wait_ge(gn_rstd, n)
            w = norms[n][0][0].shape[-1]
            act.activation(std[:, 0:w], ps[:, 4 + n % 2, 0:w], ACT.Sqrt, bias=eps_rms, scale=norms[n][2]
                           ).then_inc(gn_std, 1)

        def gn_sums(pe, n):
            srcs, mat = norms[n][0], norms[n][1]
            if n >= 2:
                pe.wait_ge(gn_std, n - 1)
            pe.wait_ge(gn_sq, tiles_before[n + 1])
            for k, src in enumerate(srcs):
                w = src.shape[-1]
                mm = pe.matmul(ps[:, 4 + n % 2, 0:w], mat[:], work[:, (tiles_before[n] + k) % KD, 0:w],
                               start=(k == 0), stop=(k == len(srcs) - 1))
            mm.then_inc(gn_sum, 1)

        def gn_scale(dve, n):
            srcs, _, _, gains = norms[n]
            w = srcs[0].shape[-1]
            dve.wait_ge(gn_std, n + 1)
            dve.wait_ge(gn_out, tiles_before[n])
            dve.reciprocal(rstd[:, 0:w], std[:, 0:w]).then_inc(gn_rstd, 1)
            dve.wait_ge(gn_rstd, n + 1)
            for src, g in zip(srcs, gains):
                dve.scalar_tensor_tensor(out=src, in0=src, scalar=g, in1=rstd[:, 0:w], op0=ALU.mult,
                                         op1=ALU.mult).then_inc(gn_out, 1)

        attn = [n for n, ph in enumerate(phases) if ph.kind == "attention"][0]
        rel_phase = phases[attn + 1]
        last_qk = [ph for ph in phases if ph.kind == "qk"][-1]
        gaps = [ph for ph in phases[attn:] if ph.kind in ("prenorm", "postnorm")][:3]
        rel_heads = [(0, 1, 2), (3, 4, 5), (6, 7)]

        def rel_sums(pe, ph):
            if ph in gaps:
                pe.wait_ge(relw_ready, 1)
                pe.wait_ge(hot_landed, 16)
                for k in rel_heads[gaps.index(ph)]:
                    if k >= 3:
                        pe.wait_ge(skew_ready, k - 2)
                    pe.matmul(ps[:, 5 + k % 3, 0:SKEW - 1], relw[:, k, :], hot[:, 0:SKEW - 1],
                              start=True, stop=True).then_inc(rel_done, 1)

        def rel_copies(act, ph):
            if ph in gaps:
                for k in rel_heads[gaps.index(ph)]:
                    act.wait_ge(rel_done, k + 1)
                    act.copy(skew_stage[:, k, 0:SKEW - 1], ps[:, 5 + k % 3, 0:SKEW - 1]).then_inc(skew_ready, 1)
                if ph is gaps[-1]:
                    act.wait_ge(skew_ready, N_BIAS)
                    act.dma_start(scratch[:, :, 0:SKEW - 1], skew_stage[:, :, 0:SKEW - 1]).then_inc(skew_stored, 16)

        loaded = [0]

        def load_table(act, func):
            loaded[0] += 1
            act.activation(warm[:, loaded[0]:loaded[0] + 1], ident[:, 0:1], func)

        def combo(c):
            return (c % 8) // 4, c % 4

        def scores_count(c):
            return 2 * (c + 1) if c < 8 else 16 + (c - 7)

        def mix2_scalar(act, B):
            act.wait_ge(drained_b, B["db"])
            act.wait_ge(drained_a, B["da"])
            for n in range(8):
                act.wait_ge(ql_done, n + 1)
                act.copy(qlat[:, n, :], ps[:, n % 4, 0:SEQ]).then_inc(ql_copied, 1)
            gn_squares(act, GN_EARLY)
            for n in range(GN_EARLY, len(norms)):
                if n + 1 < len(norms):
                    if n + 1 == len(norms) - 4:
                        act.wait_ge(ql_copied, 8)
                    gn_squares(act, n + 1)
                gn_root(act, n)
            load_table(act, ACT.Exp)
            for k, (k0, kn) in enumerate(KT):
                act.wait_ge(ct_done, k + 1)
                act.copy(c_tok[0:kn, k, :], ps[0:kn, k, 0:256]).then_inc(ct_copied, 1)
            for n in range(16):
                act.wait_ge(ix_done, n + 1)
                if n >= 4:
                    act.wait_ge(ix_used, n - 3)
                w = KEYS[n // 8]
                act.activation(relu[n % 4][:, 0:w], ps[:, n % 4, 0:w], ACT.Relu, scale=HD ** -0.5
                               ).then_inc(ix_relu, 1)

            def exps(c):
                q, _ = combo(c)
                w = KEYS[q]
                for m in range(2 if c < 8 else 1):
                    act.wait_ge(s2_max, scores_count(c - 1) + m + 1 if c else m + 1)
                    act.activation(s2[c % 2][m][:, 0:w], s2[c % 2][m][:, 0:w], ACT.Exp,
                                   bias=st2[:, 8 * (c % 2) + m:8 * (c % 2) + m + 1],
                                   accum_out=st2[:, 8 * (c % 2) + 2 + m:8 * (c % 2) + 3 + m]).then_inc(s2_exp, 1)

            def high_b(c):
                q, head = combo(c)
                act.wait_ge(o2_done, c + 1)
                act.copy(hid_hi[:, 4 + head, q * P:(q + 1) * P], ps[:, 5, 0:P]).then_inc(ob_hi, 1)

            exps(0)
            exps(1)
            for c in range(16):
                q, head = combo(c)
                act.wait_ge(t2_done, c + 1)
                if 1 <= c <= 8:
                    act.wait_ge(o2_done, c)
                elif c > 8:
                    act.wait_ge(ol_done, c - 8)
                act.copy(p2T[0:META, 0, :], ps[0:META, 6, 0:P])
                act.copy(p2T[:, 1:2 + q, :], ps[:, 6, P:(2 + q) * P].rearrange("p (k t) -> p k t", t=P)
                         ).then_inc(t2_copied, 1)
                if c + 2 < 16:
                    exps(c + 2)
                if c >= 9:
                    high_b(c - 1)
                if c < 8:
                    act.wait_ge(o2_done, c + 1)
                    act.copy(o_a[:, head, q * P:(q + 1) * P], ps[:, 5, 0:P]).then_inc(o2_copied, 1)
                else:
                    act.wait_ge(ol_done, c - 7)
                    act.wait_ge(o2_done, c)
                    act.copy(olT, ps[:, 7, 0:2 * P].rearrange("p (c t) -> p c t", c=2)).then_inc(ol_copied, 1)
                if 8 <= c < 12:
                    act.wait_ge(oa_clamped, c - 7)
                    act.activation(work[:, c - 8, 0:SEQ], o_a[:, c - 8, :], ACT.Square, scale=OA_SCALE
                                   ).then_inc(oa_sq, 1)
                if c == 13:
                    act.wait_ge(oa_var, 4)
                    act.activation(oa_std_all, oa_std_all, ACT.Sqrt).then_inc(oa_root, 1)
            high_b(15)
            for t in range(4):
                act.wait_ge(oa_out, t + 1)
                act.copy(hid_hi[:, t, 0:SEQ], o_a[:, t, :]).then_inc(oa_hi, 1)

        def mix2_vector(dve, B, link):
            for n in range(GN_EARLY, len(norms)):
                gn_scale(dve, n)

            dve.wait_ge(bias_landed, 32)
            for q in range(2):
                w = KEYS[q]
                acc = tmp2[:, 1, 0:w]
                other = tmp2[:, 2, 0:w]
                for n in range(8):
                    m = 8 * q + n
                    dve.wait_ge(ix_relu, m + 1)
                    wgt = iwq[:, q * 8 + n:q * 8 + n + 1]
                    if n == 0:
                        dve.wait_ge(drained_b, B["db"])
                        dve.tensor_scalar(acc, relu[m % 4][:, 0:w], wgt, None, ALU.mult).then_inc(ix_used, 1)
                    else:
                        dve.scalar_tensor_tensor(out=acc, in0=relu[m % 4][:, 0:w], scalar=wgt, in1=acc,
                                                 op0=ALU.mult, op1=ALU.add).then_inc(ix_used, 1)
                    dve.wait_ge(ix_used, m + 1)
                link(dve.tensor_tensor(acc, acc, causal[:, TW - w:TW], ALU.add))
                src, dst = acc, other
                for r in range(TOPK // 8):
                    link(dve.max(top8[:], src))
                    link(dve.match_replace(dst, top8[:], src, TAKEN))
                    src, dst = dst, src
                link(dve.tensor_scalar(sel_add[q][:, 0:w], src, TAKEN * 0.5, -NEG, ALU.is_lt, ALU.mult))
                link(dve.tensor_scalar(sel_add[q][:, 0:w], sel_add[q][:, 0:w], NEG, None, ALU.add))

            def biased(c):
                q, head = combo(c)
                w = KEYS[q]
                off = TW - w
                for m in range(2 if c < 8 else 1):
                    n = (scores_count(c - 1) if c else 0) + m
                    dve.wait_ge(s2_done, n + 1)
                    s = s2[c % 2][m][:, 0:w]
                    bank = 2 * (c % 2) + m
                    bias = m_out[:, head + (4 if c >= 8 else 0), off:TW]
                    dve.scalar_tensor_tensor(out=s, in0=ps[:, bank, 0:w], scalar=HD ** -0.5 if c < 8 else 1.0 / 16,
                                             in1=bias, op0=ALU.mult, op1=ALU.add).then_inc(s2_biased, 1)
                    dve.wait_ge(s2_biased, n + 1)
                    if c >= 8:
                        link(dve.tensor_tensor(s, s, sel_add[q][:, 0:w], ALU.add))
                    dve.tensor_reduce(st2[:, 8 * (c % 2) + m:8 * (c % 2) + m + 1], s, AX, ALU.max, negate=True
                                      ).then_inc(s2_max, 1)

            def weights(c):
                q, _ = combo(c)
                w = KEYS[q]
                st = st2[:, 8 * (c % 2):8 * (c % 2) + 8]
                dve.wait_ge(s2_exp, scores_count(c))
                if c >= 2:
                    dve.wait_ge(t2_done, c - 1)
                e0, e1 = s2[c % 2][0][:, 0:w], s2[c % 2][1][:, 0:w]
                if c < 8:
                    link(dve.reciprocal(st[:, 4:6], st[:, 2:4]))
                    link(dve.tensor_tensor(st[:, 6:7], st[:, 5:6], lam, ALU.mult))
                    link(dve.tensor_scalar(t2[c % 2][:, 0:w], e1, st[:, 6:7], None, ALU.mult))
                    dve.scalar_tensor_tensor(out=p2[c % 2][:, 0:w], in0=e0, scalar=st[:, 4:5], in1=t2[c % 2][:, 0:w],
                                             op0=ALU.mult, op1=ALU.subtract).then_inc(s2_prob, 1)
                else:
                    link(dve.reciprocal(st[:, 4:5], st[:, 2:3]))
                    dve.tensor_scalar(p2[c % 2][:, 0:w], e0, st[:, 4:5], None, ALU.mult).then_inc(s2_prob, 1)

            def oa_variance(t):
                dve.wait_ge(oa_sum, t + 1)
                dve.tensor_scalar(oa_std[t], ps[:, 4, 0:SEQ], 1.0 / P, 1e-6 * OA_SCALE ** 2, ALU.mult, ALU.add
                                  ).then_inc(oa_var, 1)

            def oa_scale(t):
                r = work[:, 4 + t, 0:SEQ]
                dve.wait_ge(oa_root, 1)
                link(dve.reciprocal(r, oa_std[t]))
                link(dve.scalar_tensor_tensor(out=r, in0=oa_std[t], scalar=OA_STD_MAX, in1=r, op0=ALU.is_lt,
                                              op1=ALU.mult))
                dve.scalar_tensor_tensor(out=o_a[:, t, :], in0=o_a[:, t, :], scalar=sub08, in1=r, op0=ALU.mult,
                                         op1=ALU.mult).then_inc(oa_out, 1)

            biased(0)
            biased(1)
            for c in range(16):
                weights(c)
                if c + 2 < 16:
                    dve.wait_ge(s2_prob, c + 1)
                    biased(c + 2)
                if c >= 10:
                    low_b(dve, c - 2)
                if c == 8:
                    dve.wait_ge(o2_copied, 8)
                    for t in range(4):
                        dve.tensor_scalar(o_a[:, t, :], o_a[:, t, :], OA_CLAMP, -OA_CLAMP, ALU.min, ALU.max
                                          ).then_inc(oa_clamped, 1)
                if 9 <= c < 13:
                    oa_variance(c - 9)
                if c >= 14:
                    oa_scale(2 * (c - 14))
                    oa_scale(2 * (c - 14) + 1)
            low_b(dve, 14)
            low_b(dve, 15)

        def low_b(dve, c):
            q, head = combo(c)
            dve.wait_ge(ob_hi, c - 7)
            cols_q = slice(q * P, (q + 1) * P)
            dve.tensor_tensor(hid_lo[:, 4 + head, cols_q], ps[:, 5, 0:P], hid_hi[:, 4 + head, cols_q].bitcast(F32),
                              ALU.subtract).then_inc(ob_lo, 1)

        def mix2_tensor(pe, B):
            pe.wait_ge(u_landed, 32)
            pe.wait_ge(drained_a, B["da"])
            pe.wait_ge(drained_b, B["db"])
            for n in range(8):
                if n >= 4:
                    pe.wait_ge(ql_copied, n - 3)
                pe.matmul(ps[:, n % 4, 0:SEQ], uk[:, n // 2, (n % 2) * P:(n % 2 + 1) * P],
                          z[:, 8 + n // 2, META:TW], start=True, stop=True).then_inc(ql_done, 1)
            for n in range(GN_EARLY, len(norms)):
                gn_sums(pe, n)
            pe.wait_ge(gn_out, 10)
            pe.wait_ge(ql_copied, 8)
            for k, (k0, kn) in enumerate(KT):
                for c in range(2):
                    mm = pe.transpose(ps[0:kn, k, c * P:(c + 1) * P], z[:, 16 + c, k0:k0 + kn], ident[:])
                mm.then_inc(ct_done, 1)
            for n in range(16):
                if n < 3:
                    pe.wait_ge(ct_copied, n + 1)
                if n >= 4:
                    pe.wait_ge(ix_relu, n - 3)
                q, head = n // 8, n % 8
                rows = slice((head % 2) * HD, (head % 2 + 1) * HD)
                pe.matmul(ps[:, n % 4, 0:KEYS[q]], z[rows, 12 + head // 2, META + q * P:META + (q + 1) * P],
                          z[rows, 18, 0:KEYS[q]], start=True, stop=True).then_inc(ix_done, 1)
            pe.wait_ge(ix_relu, 16)
            pe.wait_ge(gn_out, tiles_before[len(norms)])

            def scores(c):
                q, head = combo(c)
                w = KEYS[q]
                if c >= 2:
                    pe.wait_ge(s2_biased, scores_count(c - 2))
                if c < 8:
                    for m in range(2):
                        rows = slice(m * HD, (m + 1) * HD)
                        pe.matmul(ps[:, 2 * (c % 2) + m, 0:w], z[rows, head, META + q * P:META + (q + 1) * P],
                                  z[rows, 4 + head, 0:w], start=True, stop=True).then_inc(s2_done, 1)
                else:
                    for k in range(2):
                        mm = pe.matmul(ps[:, 2 * (c % 2), 0:w], qlat[:, 2 * head + k, q * P:(q + 1) * P],
                                       z[:, 16 + k, 0:w], start=(k == 0), stop=(k == 1))
                    mm.then_inc(s2_done, 1)

            def turn(c):
                q, _ = combo(c)
                pe.wait_ge(s2_prob, c + 1)
                pe.wait_ge(t2_copied, c)
                for k, (k0, kn) in enumerate(KT[:2 + q]):
                    mm = pe.transpose(ps[0:kn, 6, k * P:(k + 1) * P], p2[c % 2][:, k0:k0 + kn], ident[:])
                mm.then_inc(t2_done, 1)

            def values(c):
                q, head = combo(c)
                kts = KT[:2 + q]
                pe.wait_ge(t2_copied, c + 1)
                if c < 8:
                    pe.wait_ge(o2_copied, c)
                    for k, (_, kn) in enumerate(kts):
                        mm = pe.matmul(ps[:, 5, 0:P], va[0:kn, k, head * P:(head + 1) * P], p2T[0:kn, k, :],
                                       start=(k == 0), stop=(k == len(kts) - 1))
                    mm.then_inc(o2_done, 1)
                    return
                pe.wait_ge(ol_copied, c - 8)
                for f in range(2):
                    for k, (_, kn) in enumerate(kts):
                        mm = pe.matmul(ps[:, 7, f * P:(f + 1) * P], c_tok[0:kn, k, f * P:(f + 1) * P],
                                       p2T[0:kn, k, :], start=(k == 0), stop=(k == len(kts) - 1))
                mm.then_inc(ol_done, 1)

            def project(c):
                head = combo(c)[1]
                pe.wait_ge(ol_copied, c - 7)
                pe.wait_ge(ob_lo, c - 8)
                pe.wait_ge(o2_copied, 8)
                for f in range(2):
                    mm = pe.matmul(ps[:, 5, 0:P], uv[:, head * 2 + f, :], olT[:, f, :], start=(f == 0), stop=(f == 1))
                mm.then_inc(o2_done, 1)

            scores(0)
            scores(1)
            for c in range(16):
                if c + 2 < 16:
                    scores(c + 2)
                turn(c)
                if c >= 9:
                    project(c - 1)
                values(c)
                if 8 <= c < 12:
                    pe.wait_ge(oa_sq, c - 7)
                    pe.wait_ge(oa_var, c - 8)
                    pe.matmul(ps[:, 4, 0:SEQ], ones[:], work[:, c - 8, 0:SEQ], start=True, stop=True
                              ).then_inc(oa_sum, 1)
            project(15)

        def load_params(eng, share, landed):
            row, n = 0, 0
            for name, rows in param_rows():
                src = A[name]
                pieces = []
                if name in ("a_q_norm_2", "a_k_norm_2"):
                    for half in range(2):
                        pieces.append((p_stage[row % P:row % P + 1, row // P, half * HD:(half + 1) * HD], src))
                    row += 1
                else:
                    dims = " ".join("abc"[:len(src.shape)])
                    flat = src.rearrange(f"{dims} -> ({dims})").rearrange("(r p) -> r p", p=P)
                    done = 0
                    while done < rows:
                        k = min(rows - done, P - row % P)
                        pieces.append((p_stage[row % P:row % P + k, row // P, :], flat[done:done + k, :]))
                        done += k
                        row += k
                for dst, piece in pieces:
                    if n % 3 == share:
                        eng.dma_start(dst, piece).then_inc(landed, 16)
                    n += 1

        block = ctx.enter_context(nc.Block())

        @block.sync
        def _(sp):
            xv = A["x"][0].rearrange("(t p) d -> p t d", p=P)
            sp.dma_start(ident[:], A["const"][:, C_IDENT:C_IDENT + P]).then_inc(ident_landed, 16)
            sp.dma_start(x_stage[:], xv).then_inc(x_landed, 16)
            sp.dma_start(m_stage[:], A["meta_tokens_2"]).then_inc(x_landed, 16)
            cst = A["const"]
            sp.dma_start(blk64[:], cst[:, C_BLK:C_BLK + P]).then_inc(const_landed, 16)
            sp.dma_start(freq, cst[:, C_FREQ:C_FREQ + 2]).then_inc(const_landed, 16)
            sp.dma_start(mask_f[:], cst[:, C_MASK:C_MASK + 1152]).then_inc(const_landed, 16)
            sp.dma_start(pos_i[:], A["positions"].to_broadcast([P, SEQ])).then_inc(pos_landed, 16)
            for k, name in enumerate(("a_lambda_q1_2", "a_lambda_q2_2", "a_lambda_k1_2", "a_lambda_k2_2")):
                sp.dma_start(lvec[:, k:k + 1], A[name].rearrange("a d -> d a")).then_inc(lam_landed, 16)
            load_params(sp, 0, par_landed)
            sp.wait_ge(start_set, 1)
            sp.dma_start(relb[0:BUCKETS, :], A["rel_bias_2"]).then_inc(rel_landed, 16)

            for ph in phases:
                if not ph.n:
                    continue
                if ph.kind == "ckv":
                    sp.wait_ge(skew_stored, 16)
                    sp.wait_ge(tile_done, ph.prior.base["t"])
                    skew = bass.AP(scratch.tensor, P - 1, [[N_BIAS * SKEW - 1, P], [SKEW, N_BIAS], [1, TW]])
                    sp.dma_start(m_out[:], skew).then_inc(bias_landed, 16)
                    sp.dma_start(tmp2[:, 0, :], A["const"][:, C_CAUSAL:C_CAUSAL + TW]).then_inc(bias_landed, 16)
                    sp.dma_start(uk[:], A["b_w_uk_2"][0].rearrange("h d c -> d h c")).then_inc(u_landed, 16)
                    sp.dma_start(uv[:], A["b_w_uv_2"][0].rearrange("h (c p) d -> p (h c) d", p=P)).then_inc(u_landed, 16)

                if ph.prev is rel_phase:
                    sp.wait_ge(hid_ready, rel_phase.base["hid"])
                    sp.dma_start(hot[:, 0:SKEW - 1], A["const"][0:BUCKETS + 1, C_HOT:C_HOT + SKEW - 1]
                                 ).then_inc(hot_landed, 16)

                def load(i, j, first=False):
                    src = ph.src(i, j)
                    if not first:
                        sp.wait_ge(lo_ready, i * ph.spb + (ph.s0 + j - 1))
                    sp.dma_start(slab_view(raw, ph, j), src).then_inc(raw_landed[j % 2], 16)

                if ph.kind in ("z", "cc_in"):
                    for i in range(ph.n):
                        for j in range(ph.spb):
                            load(i, j)
                    continue
                lo = 0
                if ph.s0 == 0:
                    for j in range(2):
                        load(0, j, first=True)
                    lo = 1
                if ph.n > lo + 1:
                    with sp.Fori(lo, ph.n) as i:
                        for j in range(ph.spb):
                            load(i, j)
                elif ph.n > lo:
                    for j in range(ph.spb):
                        load(lo, j)
            sp.wait_ge(out_copied, 4)
            sp.dma_start(out[0].rearrange("(t p) d -> p t d", p=P), y_out[:]).then_inc(out_stored, 16)
            sp.wait_ge(out_stored, 16)

        @block.scalar
        def _(act):
            load_params(act, 1, par_landed)
            act.wait_ge(ident_landed, 16)
            act.wait_ge(const_landed, 48)
            act.copy(identb[:], ident[:]).then_inc(consts_cast, 1)
            act.copy(maskb[:], mask_f[:]).then_inc(consts_cast, 1)
            for j in range(2):
                act.wait_ge(par_turned, j + 1)
                w = min(512, n_par - 512 * j)
                act.copy(par[:, 512 * j:512 * j + w], ps[:, 4 + j, 0:w]).then_inc(par_ready, 1)
            act.wait_ge(arg_ready, 2)
            act.activation(trig[4][:], trig[2][:], ACT.Sin).then_inc(trig_ready, 1)
            act.activation(trig[5][:], trig[3][:], ACT.Sin).then_inc(trig_ready, 1)
            act.wait_ge(lam_done, 1)
            act.activation(lexp, ps[:, 5, 0:2], ACT.Exp).then_inc(lam_exp, 1)
            def split_hi(ph, i, j):
                act.wait_ge(raw_landed[j % 2], (i * (ph.spb // 2) + (ph.s0 // 2 + j // 2 + 1)) * 16)
                slot_free(act, ph, i, j)
                act.copy(slab_view(w_hi, ph, j), slab_view(raw, ph, j)).then_inc(hi_ready, 1)

            def split_ahead(ph, i, is_last):
                if not is_last:
                    split_hi(ph, i + 1, 0)
                elif ph.nxt is not None:
                    split_hi(ph.nxt, 0, 0)

            split_hi(streams[0], 0, 0)
            for ph in phases:
                B = ph.base

                if ph.kind == "prenorm":
                    n, c0, w = B["pre"], ph.c0, ph.w
                    for k in range(KD):
                        h_wait(act, ph, k)
                        act.activation(work[:, k, 0:w], h[:, k, c0:c0 + w], ACT.Square).then_inc(sq_ready, 1)
                    act.wait_ge(sum_done, n + 1)
                    act.activation(std[:, 0:w], ps[:, 4, 0:w], ACT.Sqrt, bias=eps_rms, scale=1.0 / D
                                   ).then_inc(std_ready, 1)
                    if ph.follows in TABLES:
                        load_table(act, TABLES[ph.follows])
                    for k in range(KD):
                        act.wait_ge(an_ready, KD * n + k + 1)
                        act.copy(a_hi[:, k, 0:w], work[:, k, 0:w]).then_inc(ahi_ready, 1)
                    rel_copies(act, ph)

                elif ph.kind == "postnorm":
                    act.wait_ge(post_sum, B["post"] + 1)
                    act.activation(std[:, 0:SEQ], ps[:, 4, 0:SEQ], ACT.Sqrt, bias=eps_rms, scale=1.0 / D
                                   ).then_inc(post_std, 1)
                    rel_copies(act, ph)

                elif ph.kind in ("qk", "v", "z"):
                    if ph is last_qk:
                        act.wait_ge(skew_stored, 16)

                    def body(i, is_last):
                        split_hi(ph, i, 1)
                        for j in range(4):
                            if j == 2:
                                split_ahead(ph, i, is_last)
                            act.wait_ge(tile_done, i * 4 + (B["t"] + j + 1))
                            if ph.kind == "qk":
                                o = qk[:, bass.ds(i * 4 + j, 1), :].rearrange("p a t -> p (a t)")
                                src = ps[:, j, 0:SEQ]
                            elif ph.kind == "z":
                                o = z[:, bass.ds(i * 4 + j, 1), :].rearrange("p a t -> p (a t)")
                                src = ps[:, j, 0:TW]
                            else:
                                o = v_tok[j % 2][:, bass.ds(i * 512 + (j // 2) * SW, SW)]
                                src = ps[:, j, 0:SW]
                            act.copy(o, src).then_inc(drained_a if j < 2 else drained_b, 1)
                    bodies(act, ph.n, body)

                elif ph.kind == "attention":
                    a0 = HEADS * ph.no + 1

                    def exp_unit(q, n):
                        act.wait_ge(mx_ready[q], n + (a0 + 1))
                        if q == 0:
                            act.wait_ge(pt_done[0], n + a0)
                            src = ps[:, 0, 0:384]
                        else:
                            act.wait_ge(pt_done[2], n + a0)
                            src = ps[:, 1:3, :].rearrange("p a c -> p (a c)")[:, 0:768]
                        act.wait_ge(rv_ready[q], n + a0)
                        act.activation(prob[q][:], src, ACT.Exp, bias=nmax[:, q:q + 1],
                                       accum_out=rsum[:, q:q + 1]).then_inc(ex_ready[q], 1)

                    def drain_o(q, n, head):
                        act.wait_ge(rv_ready[q], n + (a0 + 1))
                        act.wait_ge(o_done[q], n + (a0 + 1))
                        act.activation(o_tok[:, q, bass.ds(head * HD, HD)], ps[:, 6 + q, 0:HD], ACT.Copy,
                                       scale=rinv[:, q:q + 1]).then_inc(o_drained[q], 1)

                    def copy_turned(j, n):
                        act.wait_ge(pt_done[j], n + (a0 + 1))
                        act.wait_ge(o_done[min(j, 1)], n + a0)
                        act.copy(probT[j][:], ps[:, 3 + j, 0:384]).then_inc(pt_copied[j], 1)

                    exp_unit(0, 0)
                    exp_unit(1, 0)

                    def body(i, is_last):
                        for m in range(4):
                            n = i * 4 + m
                            copy_turned(0, n)
                            if m:
                                drain_o(1, n - 1, n - 1)
                            if not (is_last and m == 3):
                                exp_unit(0, n + 1)
                            drain_o(0, n, n)
                            copy_turned(1, n)
                            copy_turned(2, n)
                            if not (is_last and m == 3):
                                exp_unit(1, n + 1)
                            if m == 3:
                                drain_o(1, n, n)
                    bodies(act, 4, body)
                    for k in range(KD):
                        act.wait_ge(oT_done, KD * ph.no + k + 1)
                        act.copy(hid_hi[:, k, 0:SEQ], ps[:, 4 + k % 4, 0:SEQ]).then_inc(oT_hi, 1)

                elif ph.kind == "out":
                    load_table(act, ACT.Sqrt)

                    def drain(i, j):
                        n = i * 4 + j
                        act.wait_ge(tile_done, n + (B["t"] + 1))
                        g = par[:, bass.ds(n + ph.gain, 1)]
                        src = ps[:, j, 0:SEQ]
                        o = m_out[:, bass.ds(n, 1), 0:SEQ].rearrange("p a t -> p (a t)")
                        if ph.bias is None:
                            act.activation(o, src, ACT.Copy, scale=g)
                            bias = 0.0
                        else:
                            act.activation(o, src, ACT.Identity, scale=g, bias=bgain[:, bass.ds(n, 1)])
                            bias = par[:, bass.ds(n + ph.bias, 1)]
                        act.wait_ge(ssq_ready, n + (B["ssq"] - 1))
                        act.activation(sqt[:, j % 2, 0:SEQ], src, ACT.Square, bias=bias
                                       ).then_inc(drained_a if j < 2 else drained_b, 1)

                    def body(i, is_last):
                        if ph.spb == 2:
                            split_hi(ph, i, 1)
                            drain(i, 0)
                            drain(i, 1)
                            split_ahead(ph, i, is_last)
                            drain(i, 2)
                            drain(i, 3)
                        else:
                            split_hi(ph, i, 1)
                            split_hi(ph, i, 2)
                            split_hi(ph, i, 3)
                            drain(i, 0)
                            drain(i, 1)
                            split_hi(ph, i, 4)
                            split_hi(ph, i, 5)
                            split_ahead(ph, i, is_last)
                            drain(i, 2)
                            drain(i, 3)
                    bodies(act, ph.n, body)

                elif ph.kind == "add":
                    load_table(act, ACT.Sqrt)

                    def body(i, is_last):
                        for j in range(1, ph.spb):
                            split_hi(ph, i, j)
                        split_ahead(ph, i, is_last)
                    bodies(act, ph.n, body)

                elif ph.kind == "ffn_in":
                    taps = col["ffn_w_conv"] + ph.layer * 3 * 2 * KF

                    def first_tap(i, j):
                        act.wait_ge(tile_done, i * 4 + (B["t"] + j + 1))
                        if j >= 2:
                            act.wait_ge(hid_mul, i * 2 + (B["fm"] + j - 3))
                        else:
                            act.wait_ge(silu_ready, i * 2 + (B["fs"] + j - 1))
                        g = par[:, bass.ds(i * 2 + (taps + 2 * 2 * KF + (j % 2) + (j // 2) * KF), 1)]
                        act.activation(cv[:, j, :], ps[:, j, 0:SEQ], ACT.Copy, scale=g).then_inc(tap_ready, 1)

                    def body(i, is_last):
                        split_hi(ph, i, 1)
                        first_tap(i, 0)
                        first_tap(i, 1)
                        split_ahead(ph, i, is_last)
                        for j in range(2):
                            act.wait_ge(drained_a, i * 2 + (B["da"] + j + 1))
                            act.wait_ge(hid_mul, i * 2 + (B["fm"] + j - 1))
                            act.activation(sg[:, j, 0:SEQ], cv[:, j, :], ACT.Silu).then_inc(silu_ready, 1)
                        first_tap(i, 2)
                        first_tap(i, 3)
                    bodies(act, ph.n, body)

                elif ph.kind in ("swiglu", "cc_in"):
                    w = ph.w

                    def body(i, is_last):
                        split_hi(ph, i, 1)
                        for j in range(2):
                            act.wait_ge(tile_done, i * 4 + (B["t"] + j + 1))
                            act.wait_ge(drained_b, i * 2 + (B["db"] + j - 1))
                            if ph.kind == "swiglu":
                                act.activation(sg[:, j, 0:w], ps[:, j, 0:w], ACT.Silu).then_inc(drained_a, 1)
                            else:
                                act.activation(sg[:, j, 0:w], ps[:, j, 0:w], ACT.Sigmoid,
                                               bias=par[:, bass.ds(i * 2 + (col["cc_b_pw1"] + KD + j), 1)]
                                               ).then_inc(drained_a, 1)
                        split_ahead(ph, i, is_last)
                    bodies(act, ph.n, body)

                elif ph.kind == "sc_ch":
                    def body(i, is_last):
                        split_hi(ph, i, 1)
                        split_ahead(ph, i, is_last)
                    bodies(act, ph.n, body)

                elif ph.kind == "sc_b":
                    def body(i, is_last):
                        split_hi(ph, i, 1)
                        for j in range(4):
                            if j == 2:
                                split_ahead(ph, i, is_last)
                            sem_j = drained_a if j < 2 else drained_b
                            act.wait_ge(sem_j, i * 2 + (B["da" if j < 2 else "db"] + j % 2 + 1))
                            act.copy(hid_hi[:, i * 4 + j, 0:SEQ], work[:, i * 4 + j, 0:SEQ]).then_inc(hid_hi_ready, 1)
                    for i in range(ph.n):
                        body(i, i == ph.n - 1)

                elif ph.kind == "cc_mid":
                    for t, k in enumerate(CC_PE):
                        with act.Fori(0, TAPS) as j:
                            act.activation(diag[:, bass.ds(j + t * TAPS, 1), :].rearrange("p a c -> p (a c)"), ident[:],
                                           ACT.Copy, scale=par[:, bass.ds(j * KD + (col["cc_w_dw"] + k), 1)]
                                           ).then_inc(diag_ready, 1)
                    load_table(act, ACT.Sqrt)
                    for t, k in enumerate(CC_PE):
                        act.wait_ge(cc_product, t + 1)
                        act.activation(cacc[:, k, :], ps[:, 5 + t, 0:SEQ], ACT.Identity,
                                       bias=par[:, col["cc_b_dw"] + k:col["cc_b_dw"] + k + 1]).then_inc(cc_drained, 1)
                    act.wait_ge(cc_sum, 1)
                    act.activation(std[:, 0:SEQ], ps[:, 4, 0:SEQ], ACT.Copy, scale=1.0 / D).then_inc(cc_mu, 1)
                    for k in range(KD):
                        act.wait_ge(cc_stat, k + 1)
                        act.activation(work[:, k, 0:SEQ], cacc[:, k, :], ACT.Square).then_inc(cc_norm, 1)
                    act.wait_ge(cc_sum, 2)
                    act.activation(std[:, 0:SEQ], ps[:, 5, 0:SEQ], ACT.Sqrt, bias=eps_ln, scale=1.0 / D
                                   ).then_inc(cc_mu, 1)
                    load_table(act, ACT.Silu)
                    for k in range(KD):
                        act.wait_ge(cc_stat, KD + k + 1)
                        act.activation(work[:, k, 0:SEQ], cacc[:, k, :], ACT.Silu,
                                       scale=par[:, col["cc_ln_g"] + k:col["cc_ln_g"] + k + 1],
                                       bias=par[:, col["cc_ln_b"] + k:col["cc_ln_b"] + k + 1]).then_inc(cc_silu, 1)
                        act.wait_ge(cc_silu, k + 1)
                        act.copy(hid_hi[:, k, 0:SEQ], work[:, k, 0:SEQ]).then_inc(hid_hi_ready, 1)

                elif ph.kind == "ckv":
                    act.wait_ge(drained_a, B["da"])
                    act.wait_ge(drained_b, B["db"])
                    gn_squares(act, 0)
                    split_hi(ph, 0, 1)
                    for j in range(2):
                        act.wait_ge(tile_done, B["t"] + j + 1)
                        act.copy(z[:, 16 + j, :], ps[:, j, 0:TW]).then_inc(drained_a, 1)
                        if j == 1:
                            split_ahead(ph, 0, True)
                        gn_squares(act, j + 1)
                        gn_root(act, j)
                    act.wait_ge(tile_done, B["t"] + 3)
                    act.copy(z[0:HD, 18, :], ps[0:HD, 2, 0:TW])
                    act.copy(z[HD:P, 18, :], ps[0:HD, 2, 0:TW]).then_inc(drained_b, 1)
                    gn_squares(act, 3)
                    gn_root(act, 2)
                    act.wait_ge(tile_done, B["t"] + 4)
                    act.activation(iwq[:], ps[:, 3, 0:16], ACT.Copy, scale=8.0 ** -0.5).then_inc(drained_b, 1)
                    gn_squares(act, 4)
                    gn_root(act, 3)

                elif ph.kind == "va":
                    split_hi(ph, 0, 1)
                    for j in range(4):
                        if j == 2:
                            split_ahead(ph, 0, True)
                        act.wait_ge(tile_done, B["t"] + j + 1)
                        c = (j // 2) * SW
                        if j % 2 == 0:
                            act.copy(va[:, 1, c:c + SW], ps[:, j, 0:SW]).then_inc(drained_a if j < 2 else drained_b, 1)
                        else:
                            act.copy(va[:, 2, c:c + SW], ps[:, j, 0:SW])
                            act.copy(va[0:META, 0, c:c + SW], ps[0:META, j, SW:2 * SW]
                                     ).then_inc(drained_a if j < 2 else drained_b, 1)
                        if j < 3:
                            gn_squares(act, 5 + j)
                        gn_root(act, 4 + j)

                elif ph.kind == "mix2":
                    mix2_scalar(act, B)

            for t in range(4):
                act.wait_ge(out_done, t + 1)
                act.copy(y_out[:, t // 2, (t % 2) * 512:(t % 2 + 1) * 512], ps[:, 4 + t, :]).then_inc(out_copied, 1)

        @block.vector
        def _(dve):
            linked = [0]

            def link(ins):
                linked[0] += 1
                ins.then_inc(chain, 1)
                dve.wait_ge(chain, linked[0])

            dve.memset(relb, NEG).then_inc(start_set, 1)
            dve.wait_ge(start_set, 1)
            dve.memset(eps_rms, 1e-6)
            dve.memset(eps_ln, 1e-5)
            dve.memset(ones[:], 1.0).then_inc(start_set, 1)
            for k, s in enumerate(sc_done + mx_ready + ex_ready + rv_ready + pt_done + pt_copied + o_done
                                  + o_drained + [rope_in, rope_mid, rope_t1, rope_ready]):
                dve.memset(mark[:, 4 + k:5 + k], 0.0).then_inc(s, 1)
            dve.memset(mark[:, 0:1], 0.0).then_inc(drained_a, 2)
            dve.memset(mark[:, 1:2], 0.0).then_inc(drained_b, 2)
            dve.memset(mark[:, 2:3], 0.0).then_inc(ssq_ready, 2)
            dve.memset(mark[:, 3:4], 0.0).then_inc(hid_mul, 2)
            dve.memset(mark[:, 26:27], 0.0).then_inc(silu_ready, 2)
            for k in range(KD):
                dve.wait_ge(tile_done, k + 1)
                dve.tensor_copy(h[:, k, :], ps[:, k % 4, 0:TW]).then_inc(h_ready, 1)
            dve.wait_ge(ident_landed, 16)
            dve.wait_ge(const_landed, 48)
            dve.wait_ge(pos_landed, 16)
            link(dve.tensor_copy(trig[0][:], pos_i[:]))
            link(dve.tensor_scalar(trig[1][:], trig[0][:], freq[:, 0:1], None, ALU.mult))
            link(dve.tensor_scalar(trig[0][:], trig[1][:], 1.0 / TWO_PI, ROUND, ALU.mult, ALU.add))
            link(dve.tensor_scalar(trig[0][:], trig[0][:], ROUND, None, ALU.subtract))
            for part in (PI_A, PI_B, PI_C):
                link(dve.scalar_tensor_tensor(out=trig[1][:], in0=trig[0][:], scalar=-part, in1=trig[1][:],
                                              op0=ALU.mult, op1=ALU.add))
            edge = 3.1415925
            link(dve.tensor_scalar(trig[3][:], trig[1][:], math.pi / 2, None, ALU.add))
            link(dve.tensor_scalar(trig[0][:], trig[3][:], math.pi, -TWO_PI, ALU.is_gt, ALU.mult))
            link(dve.tensor_tensor(trig[3][:], trig[3][:], trig[0][:], ALU.add))
            dve.tensor_scalar(trig[2][:], trig[1][:], edge, -edge, ALU.min, ALU.max).then_inc(arg_ready, 1)
            dve.tensor_scalar(trig[3][:], trig[3][:], edge, -edge, ALU.min, ALU.max).then_inc(arg_ready, 1)
            dve.wait_ge(lam_landed, 64)
            dve.tensor_tensor(lprod, lvec[:, 0:2], lvec[:, 2:4], ALU.mult).then_inc(lprod_ready, 1)
            dve.wait_ge(trig_ready, 2)
            link(dve.tensor_scalar(trs[:, 1, :], trig[4][:], freq[:, 1:2], None, ALU.mult))
            dve.tensor_scalar(trs[:, 0, :], trs[:, 1, :], 0.125, None, ALU.mult)
            dve.tensor_copy(trc[:, 1, :], trig[5][:])
            dve.tensor_scalar(trc[:, 0, :], trig[5][:], 0.125, None, ALU.mult).then_inc(tables_ready, 1)
            dve.wait_ge(par_ready, 2)
            g0, b0 = col["mix_norm_post"] + 2 * KD, col["cc_b_pw2"]
            dve.tensor_tensor(bgain, par[:, g0:g0 + KD], par[:, b0:b0 + KD], ALU.mult)
            dve.tensor_scalar(sub08, par[:, col["a_subln_2"]:col["a_subln_2"] + 1], (1.0 - LAM_INIT) * OA_SCALE, None, ALU.mult)
            dve.wait_ge(lam_exp, 1)
            dve.scalar_tensor_tensor(out=lam, in0=lexp[:, 0:1], scalar=LAM_INIT, in1=lexp[:, 1:2], op0=ALU.add,
                                     op1=ALU.subtract).then_inc(lam_ready, 1)
            dve.wait_ge(lam_ready, 1)

            def split_lo(ph, i, j):
                dve.wait_ge(hi_ready, i * ph.spb + (ph.s0 + j + 1))
                dve.tensor_tensor(slab_view(w_lo, ph, j), slab_view(raw, ph, j), slab_view(w_hi, ph, j).bitcast(F32),
                                  ALU.subtract).then_inc(lo_ready, 1)

            def split_ahead(ph, i, is_last):
                if not is_last:
                    split_lo(ph, i + 1, 0)
                elif ph.nxt is not None:
                    split_lo(ph.nxt, 0, 0)

            def rope(no, p, part):
                n = p * 2 + part
                r0 = HEADS * no + 1
                src = qk[:].rearrange("p (a g e) t -> p a g e t", a=2, g=3)[:, part, :, bass.ds(p, 1), :
                                                                          ].rearrange("p g e t -> p g (e t)")
                dve.wait_ge(rope_ready, n + r0)
                dve.tensor_tensor(rope_s[:], src, trs[:, part:part + 1, :].to_broadcast([P, GROUPS, SEQ]),
                                  ALU.mult).then_inc(rope_in, 1)
                dve.wait_ge(rope_in, n + (r0 + 1))
                dve.tensor_copy(mark[:, 1:2], mark[:, 0:1])
                dve.stream_shuffle(rope_s[:], rope_s[:], [(j + 8) % 16 if j < 16 else j for j in range(32)]
                                   ).then_inc(rope_mid, 1)

            split_lo(streams[0], 0, 0)
            for ph in phases:
                B = ph.base

                if ph.kind == "prenorm":
                    n, c0, w = B["pre"], ph.c0, ph.w
                    dve.wait_ge(std_ready, n + 1)
                    dve.reciprocal(rstd[:, 0:w], std[:, 0:w]).then_inc(rstd_ready, 1)
                    dve.wait_ge(rstd_ready, n + 1)
                    for k in range(KD):
                        dve.scalar_tensor_tensor(out=work[:, k, 0:w], in0=h[:, k, c0:c0 + w],
                                                 scalar=par[:, ph.gain + k:ph.gain + k + 1], in1=rstd[:, 0:w],
                                                 op0=ALU.mult, op1=ALU.mult).then_inc(an_ready, 1)

                elif ph.kind == "postnorm":
                    dve.wait_ge(post_std, B["post"] + 1)
                    dve.reciprocal(rstd[:, 0:SEQ], std[:, 0:SEQ]).then_inc(post_rstd, 1)
                    dve.wait_ge(post_rstd, B["post"] + 1)
                    for k in range(KD):
                        dve.tensor_tensor(m_out[:, k, 0:SEQ], m_out[:, k, 0:SEQ], rstd[:, 0:SEQ], ALU.mult
                                          ).then_inc(mh_ready, 1)

                elif ph.kind == "v":
                    def body(i, is_last):
                        if is_last:
                            dve.wait_ge(drained_a, B["da"])
                            dve.wait_ge(drained_b, B["db"])
                            rope(ph.no, 0, 0)
                        split_lo(ph, i, 1)
                        if is_last:
                            rope(ph.no, 0, 1)
                        split_ahead(ph, i, is_last)
                    bodies(dve, ph.n, body)

                elif ph.kind in ("ckv", "va"):
                    first = 0 if ph.kind == "ckv" else 4
                    split_lo(ph, 0, 1)
                    gn_scale(dve, first)
                    split_ahead(ph, 0, True)
                    for n in range(first + 1, first + 4):
                        gn_scale(dve, n)

                elif ph.kind in ("qk", "z", "out"):
                    if ph is rel_phase:
                        dve.wait_ge(hid_ready, B["hid"])
                        dve.wait_ge(rel_landed, 16)
                        for k in range(N_BIAS):
                            op = dve.tensor_scalar(relw[:, k, :], ones[0:BUCKETS + 1, :], relb[:, k:k + 1], None, ALU.mult)
                        op.then_inc(relw_ready, 1)

                    def body(i, is_last):
                        for j in range(1, ph.spb):
                            split_lo(ph, i, j)
                        split_ahead(ph, i, is_last)
                    bodies(dve, ph.n, body)

                elif ph.kind == "add":
                    w = ph.w

                    def add(i, j):
                        dve.wait_ge(tile_done, i * 4 + (B["t"] + j + 1))
                        o = h[:, bass.ds(i * 4 + j, 1), ph.c0:ph.c0 + w].rearrange("p a t -> p (a t)")
                        dve.scalar_tensor_tensor(out=o, in0=ps[:, j, 0:w], scalar=ph.scale, in1=o, op0=ALU.mult,
                                                 op1=ALU.add).then_inc(drained_a if j < 2 else drained_b, 1)

                    def body(i, is_last):
                        split_lo(ph, i, 1)
                        if ph.spb == 6:
                            split_lo(ph, i, 2)
                            split_lo(ph, i, 3)
                        add(i, 0)
                        add(i, 1)
                        if ph.spb == 6:
                            split_lo(ph, i, 4)
                            split_lo(ph, i, 5)
                        split_ahead(ph, i, is_last)
                        add(i, 2)
                        add(i, 3)
                    bodies(dve, ph.n, body)

                elif ph.kind == "attention":
                    a0 = HEADS * ph.no + 1

                    def row_max(q, n):
                        dve.wait_ge(sc_done[q], n + (a0 + 1))
                        dve.wait_ge(ex_ready[q], n + a0)
                        src = ps[:, 0, 0:384] if q == 0 else ps[:, 1:3, :].rearrange("p a c -> p (a c)")[:, 0:768]
                        dve.tensor_reduce(nmax[:, q:q + 1], src, AX, ALU.max, negate=True).then_inc(mx_ready[q], 1)

                    def inverse(q, n):
                        dve.wait_ge(ex_ready[q], n + (a0 + 1))
                        dve.wait_ge(o_drained[q], n + a0)
                        dve.reciprocal(rinv[:, q:q + 1], rsum[:, q:q + 1]).then_inc(rv_ready[q], 1)

                    row_max(0, 0)
                    row_max(1, 0)
                    rope(ph.no, 1, 0)

                    def body(i, is_last):
                        for m in range(4):
                            n = i * 4 + m
                            inverse(0, n)
                            if not (is_last and m == 3):
                                row_max(0, n + 1)
                            inverse(1, n)
                            if not (is_last and m >= 1):
                                rope(ph.no, i * 2 + (m + 3) // 2, (m + 3) % 2)
                            if not (is_last and m == 3):
                                row_max(1, n + 1)
                    bodies(dve, 4, body)
                    for k in range(KD):
                        dve.wait_ge(oT_hi, KD * ph.no + k + 1)
                        dve.tensor_tensor(hid_lo[:, k, 0:SEQ], ps[:, 4 + k % 4, 0:SEQ], hid_hi[:, k, 0:SEQ].bitcast(F32),
                                          ALU.subtract).then_inc(hid_ready, 1)

                elif ph.kind == "ffn_in":
                    taps = col["ffn_w_conv"] + ph.layer * 3 * 2 * KF

                    def tap(i, j, back):
                        g = par[:, bass.ds(i * 2 + (taps + (2 - back) * 2 * KF + (j % 2) + (j // 2) * KF), 1)]
                        return dve.scalar_tensor_tensor(out=cv[:, j, back:SEQ], in0=ps[:, j, 0:SEQ - back], scalar=g,
                                                        in1=cv[:, j, back:SEQ], op0=ALU.mult, op1=ALU.add)

                    def conv(i, js):
                        for j in js:
                            dve.wait_ge(tap_ready, i * 4 + (B["tap"] + j + 1))
                            tap(i, j, 1).then_inc(tap_mid, 1)
                        for j in js:
                            dve.wait_ge(tap_mid, i * 4 + (B["tap"] + j + 1))
                            tap(i, j, 2).then_inc(drained_a if j < 2 else drained_b, 1)

                    def body(i, is_last):
                        split_lo(ph, i, 1)
                        conv(i, (0, 1))
                        split_ahead(ph, i, is_last)
                        conv(i, (2, 3))
                    bodies(dve, ph.n, body)

                elif ph.kind in ("swiglu", "cc_in"):
                    w = ph.w
                    if ph.kind == "cc_in":
                        dve.memset(gpad[:, :, 0:PAD], 0.0)

                    def body(i, is_last):
                        split_lo(ph, i, 1)
                        split_ahead(ph, i, is_last)
                        dve.wait_ge(drained_a, i * 2 + (B["da"] + 2))
                        for j in range(2):
                            dve.wait_ge(tile_done, i * 4 + (B["t"] + 3 + j))
                            if ph.kind == "swiglu":
                                dve.wait_ge(hid_ready, i * 2 + (B["hid"] + j - 1))
                                dve.tensor_tensor(hs[:, j, 0:w], ps[:, 2 + j, 0:w], sg[:, j, 0:w], ALU.mult
                                                  ).then_inc(drained_b, 1)
                            else:
                                o = gpad[:, bass.ds(i * 2 + j, 1), PAD:PAD + SEQ].rearrange("p a t -> p (a t)")
                                dve.scalar_tensor_tensor(
                                    out=o, in0=ps[:, 2 + j, 0:w],
                                    scalar=par[:, bass.ds(i * 2 + (col["cc_b_pw1"] + j), 1)],
                                    in1=sg[:, j, 0:w], op0=ALU.add, op1=ALU.mult).then_inc(drained_b, 1)
                    bodies(dve, ph.n, body)

                elif ph.kind == "sc_ch":
                    def body(i, is_last):
                        split_lo(ph, i, 1)
                        for j in range(2):
                            dve.wait_ge(tile_done, i * 4 + (B["t"] + j + 1))
                            dve.tensor_copy(ch[:, j, :], ps[:, j, 0:SEQ]).then_inc(drained_a, 1)
                        split_ahead(ph, i, is_last)
                        for j in range(2):
                            dve.wait_ge(tile_done, i * 4 + (B["t"] + 3 + j))
                            dve.wait_ge(drained_a, i * 2 + (B["da"] + j + 1))
                            dve.tensor_tensor(ch[:, 2 + j, :], ps[:, 2 + j, 0:SEQ], ch[:, j, :], ALU.mult
                                              ).then_inc(drained_b, 1)
                        w0 = col["sc_w_conv"]
                        for back in range(3):
                            for j in range(2):
                                dve.wait_ge(drained_b, i * 2 + (B["db"] + j + 1))
                                g = par[:, bass.ds(i * 2 + (w0 + (2 - back) * KD + j), 1)]
                                o = y_sc[:, bass.ds(i * 2 + j, 1), back:SEQ].rearrange("p a t -> p (a t)")
                                src = ch[:, 2 + j, 0:SEQ - back]
                                if back == 0:
                                    dve.tensor_scalar(o, src, g, None, ALU.mult).then_inc(sc_tap, 1)
                                else:
                                    dve.wait_ge(sc_tap, i * 6 + (2 * back - 1 + j))
                                    dve.scalar_tensor_tensor(out=o, in0=src, scalar=g, in1=o, op0=ALU.mult,
                                                             op1=ALU.add).then_inc(sc_tap, 1)
                    bodies(dve, ph.n, body)
                    dve.wait_ge(sc_tap, 6 * ph.n)

                elif ph.kind == "sc_b":
                    for i in range(ph.n):
                        split_lo(ph, i, 1)
                        for j in range(4):
                            if j == 2:
                                split_ahead(ph, i, i == ph.n - 1)
                            dve.wait_ge(tile_done, i * 4 + (B["t"] + j + 1))
                            dve.tensor_tensor(work[:, 4 * i + j, 0:SEQ], ps[:, j, 0:SEQ], y_sc[:, 4 * i + j, :], ALU.mult
                                              ).then_inc(drained_a if j < 2 else drained_b, 1)

                elif ph.kind == "cc_mid":
                    w0, b0 = col["cc_w_dw"], col["cc_b_dw"]
                    dve.wait_ge(drained_b, B["db"])
                    for k in CC_DVE:
                        g = w0 + (TAPS - 1) * KD + k
                        dve.tensor_scalar(cacc[:, k, :], gpad[:, k, PAD:PAD + SEQ], par[:, g:g + 1],
                                          par[:, b0 + k:b0 + k + 1], ALU.mult, ALU.add).then_inc(cc_tap, 1)
                    with dve.Fori(0, TAPS - 1) as j:
                        for c, k in enumerate(CC_DVE):
                            dve.wait_ge(cc_tap, j * len(CC_DVE) + (c + 1))
                            dve.scalar_tensor_tensor(out=cacc[:, k, :], in0=gpad[:, k, bass.ds(j, SEQ)],
                                                     scalar=par[:, bass.ds(j * KD + (w0 + k), 1)], in1=cacc[:, k, :],
                                                     op0=ALU.mult, op1=ALU.add).then_inc(cc_tap, 1)
                    dve.wait_ge(cc_mu, 1)
                    for k in range(KD):
                        dve.tensor_tensor(cacc[:, k, :], cacc[:, k, :], std[:, 0:SEQ], ALU.subtract).then_inc(cc_stat, 1)
                    dve.wait_ge(cc_mu, 2)
                    link(dve.reciprocal(rstd[:, 0:SEQ], std[:, 0:SEQ]))
                    for k in range(KD):
                        dve.tensor_tensor(cacc[:, k, :], cacc[:, k, :], rstd[:, 0:SEQ], ALU.mult).then_inc(cc_stat, 1)

                elif ph.kind == "mix2":
                    mix2_vector(dve, B, link)

        @block.gpsimd
        def _(pool):
            load_params(pool, 2, par_landed_pool)
            for ph in phases:
                B = ph.base

                if ph.kind == "prenorm":
                    n, w = B["pre"], ph.w
                    for k in range(KD):
                        pool.wait_ge(ahi_ready, KD * n + k + 1)
                        pool.tensor_tensor(a_lo[:, k, 0:w], work[:, k, 0:w], a_hi[:, k, 0:w].bitcast(F32), ALU.subtract
                                           ).then_inc(a_ready, 1)

                elif ph.kind == "postnorm":
                    for k in range(KD):
                        pool.wait_ge(mh_ready, KD * B["post"] + k + 1)
                        pool.tensor_tensor(h[:, k, META:TW], h[:, k, META:TW], m_out[:, k, 0:SEQ], ALU.add
                                           ).then_inc(h_ready, 1)

                elif ph.kind == "out":
                    for n in range(KD):
                        j = n % 4
                        d, k0 = (drained_a, B["da"]) if j < 2 else (drained_b, B["db"])
                        pool.wait_ge(d, k0 + 2 * (n // 4) + j % 2 + 1)
                        if n == 0:
                            pool.tensor_copy(ssq[:, 0:SEQ], sqt[:, 0, 0:SEQ]).then_inc(ssq_ready, 1)
                        else:
                            pool.wait_ge(ssq_ready, B["ssq"] + n)
                            pool.tensor_tensor(ssq[:, 0:SEQ], ssq[:, 0:SEQ], sqt[:, j % 2, 0:SEQ], ALU.add
                                               ).then_inc(ssq_ready, 1)

                elif ph.kind in ("ffn_in", "swiglu"):
                    w = ph.w

                    def body(i, is_last):
                        for j in range(2):
                            if ph.kind == "ffn_in":
                                pool.wait_ge(silu_ready, i * 2 + (B["fs"] + j + 1))
                                pool.wait_ge(drained_b, i * 2 + (B["db"] + j + 1))
                                pool.tensor_tensor(hs[:, j, 0:w], sg[:, j, 0:w], cv[:, 2 + j, :], ALU.mult
                                                   ).then_inc(hid_mul, 1)
                                pool.wait_ge(hid_mul, i * 2 + (B["fm"] + j + 1))
                            else:
                                pool.wait_ge(drained_b, i * 2 + (B["db"] + j + 1))
                            hi = hid_hi[:, bass.ds(i * 2 + j, 1), 0:w].rearrange("p a t -> p (a t)")
                            lo = hid_lo[:, bass.ds(i * 2 + j, 1), 0:w].rearrange("p a t -> p (a t)")
                            pool.tensor_copy(hi, hs[:, j, 0:w]).then_inc(hid_hi_ready, 1)
                            pool.wait_ge(hid_hi_ready, i * 2 + (B["hh"] + j + 1))
                            pool.tensor_tensor(lo, hs[:, j, 0:w], hi.bitcast(F32), ALU.subtract).then_inc(hid_ready, 1)
                    bodies(pool, ph.n, body)

                elif ph.kind == "cc_in":
                    w0, b0 = col["cc_w_dw"], col["cc_b_dw"]
                    for k in CC_POOL:
                        pool.wait_ge(drained_b, B["db"] + k + 1)
                    done = 0
                    for j in range(TAPS):
                        g = [par[:, w0 + j * KD + k:w0 + j * KD + k + 1] for k in CC_POOL]
                        if j == 0:
                            for c, k in enumerate(CC_POOL):
                                pool.tensor_scalar(cacc[:, k, :], gpad[:, k, 0:SEQ], g[c], par[:, b0 + k:b0 + k + 1],
                                                   ALU.mult, ALU.add).then_inc(cc_tap_pool, 1)
                            done += len(CC_POOL)
                            continue
                        for c, k in enumerate(CC_POOL):
                            if j > 1:
                                pool.wait_ge(cc_tap_pool, done - len(CC_POOL) + c + 1)
                            pool.tensor_scalar(work[:, c, 0:SEQ], gpad[:, k, j:j + SEQ], g[c], None, ALU.mult
                                               ).then_inc(cc_tap_pool, 1)
                        done += len(CC_POOL)
                        for c, k in enumerate(CC_POOL):
                            pool.wait_ge(cc_tap_pool, done - len(CC_POOL) + c + 1)
                            pool.tensor_tensor(cacc[:, k, :], cacc[:, k, :], work[:, c, 0:SEQ], ALU.add
                                               ).then_inc(cc_tap_pool, 1)
                        done += len(CC_POOL)

                elif ph.kind in ("sc_b", "cc_mid"):
                    for k in range(KD):
                        pool.wait_ge(hid_hi_ready, B["hh"] + k + 1)
                        pool.tensor_tensor(hid_lo[:, k, 0:SEQ], work[:, k, 0:SEQ], hid_hi[:, k, 0:SEQ].bitcast(F32),
                                           ALU.subtract).then_inc(hid_ready, 1)

                elif ph.kind == "attention":
                    r0 = HEADS * ph.no + 1

                    def rope(p, slot, part):
                        n = p * 2 + part
                        src = qk[:].rearrange("p (a g e) t -> p a g e t", a=2, g=3)[:, part, :, bass.ds(p, 1), :
                                                                                  ].rearrange("p g e t -> p g (e t)")
                        o = roped[slot][:, 3 * part:3 * part + 3, :]
                        pool.wait_ge(rope_ready, n + r0)
                        pool.tensor_tensor(rope_c[:], src, trc[:, part:part + 1, :].to_broadcast([P, GROUPS, SEQ]),
                                           ALU.mult).then_inc(rope_t1, 1)
                        pool.wait_ge(rope_t1, n + (r0 + 1))
                        pool.wait_ge(rope_mid, n + (r0 + 1))
                        pool.tensor_tensor(o, rope_c[:], rope_s[:], ALU.add).then_inc(rope_ready, 1)

                    pool.wait_ge(tables_ready, 1)
                    pool.wait_ge(drained_a, ph.prior.base["da"])
                    pool.wait_ge(drained_b, ph.prior.base["db"])
                    rope(0, 0, 0)
                    rope(0, 0, 1)
                    rope(1, 1, 0)

                    def body(i, is_last):
                        for m in range(4):
                            if not (is_last and m >= 1):
                                pool.wait_ge(sc_done[1], i * 4 + (a0 + m + 1 - (m + 1) % 2))
                                rope(i * 2 + (m + 3) // 2, (m + 3) // 2 % 2, (m + 3) % 2)
                    a0 = HEADS * ph.no + 1
                    bodies(pool, 4, body)

                elif ph.kind == "mix2":
                    for t in range(4):
                        pool.wait_ge(oa_hi, t + 1)
                        pool.tensor_tensor(hid_lo[:, t, 0:SEQ], o_a[:, t, :], hid_hi[:, t, 0:SEQ].bitcast(F32),
                                           ALU.subtract).then_inc(hid_ready, 1)

        @block.tensor
        def _(pe):
            pe.wait_ge(ident_landed, 16)
            pe.wait_ge(x_landed, 32)
            for k in range(KD):
                if k >= 4:
                    pe.wait_ge(h_ready, k - 3)
                cs = slice(k * P, (k + 1) * P)
                pe.transpose(ps[:, k % 4, 0:META], m_stage[0:META, cs], ident[0:META, 0:META])
                pe.transpose(ps[:, k % 4, META:META + P], x_stage[:, 0, cs], ident[:])
                pe.transpose(ps[:, k % 4, META + P:TW], x_stage[:, 1, cs], ident[:]).then_inc(tile_done, 1)
            pe.wait_ge(par_landed, 16 * (n_par_loads - n_par_loads // 3))
            pe.wait_ge(par_landed_pool, 16 * (n_par_loads // 3))
            for t in range(n_par_tiles):
                r = min(P, n_par - t * P)
                mm = pe.transpose(ps[:, 4 + t // 4, (t % 4) * P:(t % 4) * P + r], p_stage[0:r, t, :], ident[0:r, 0:r])
                if t % 4 == 3 or t == n_par_tiles - 1:
                    mm.then_inc(par_turned, 1)
            pe.wait_ge(par_ready, 2)
            pe.wait_ge(start_set, 2)
            pe.wait_ge(lprod_ready, 1)
            pe.matmul(ps[:, 5, 0:2], ones[0:HD, :], lprod, start=True, stop=True).then_inc(lam_done, 1)
            def mm3(o, wh, wl, xh, xl, start, stop):
                pe.matmul(o, wh, xh, start=start, stop=False)
                pe.matmul(o, wh, xl, start=False, stop=False)
                return pe.matmul(o, wl, xh, start=False, stop=stop)

            def bank_free(ph, i, j):
                if j < 2:
                    pe.wait_ge(drained_a, i * 2 + (ph.base["da"] + j - 1))
                else:
                    pe.wait_ge(drained_b, i * 2 + (ph.base["db"] + j - 3))

            def slab_split(ph, i, j):
                pe.wait_ge(lo_ready, i * ph.spb + (ph.s0 + j + 1))

            for ph in phases:
                B = ph.base

                if ph.kind == "prenorm":
                    n, w = B["pre"], ph.w
                    for k in range(KD):
                        pe.wait_ge(sq_ready, KD * n + k + 1)
                        mm = pe.matmul(ps[:, 4, 0:w], ones[:], work[:, k, 0:w], start=(k == 0), stop=(k == KD - 1))
                    mm.then_inc(sum_done, 1)
                    rel_sums(pe, ph)

                elif ph.kind == "postnorm":
                    pe.wait_ge(ssq_ready, B["ssq"])
                    pe.matmul(ps[:, 4, 0:SEQ], ones[:], ssq[:, 0:SEQ], start=True, stop=True).then_inc(post_sum, 1)
                    rel_sums(pe, ph)

                elif ph.kind in ("qk", "sc_ch", "sc_b", "cc_in", "ffn_in", "swiglu", "z"):
                    w = TW if ph.kind == "z" else ph.w

                    def body(i):
                        for j in range(4):
                            if j % 2 == 0:
                                slab_split(ph, i, j // 2)
                            bank_free(ph, i, j)
                            c = slice((j % 2) * P, (j % 2 + 1) * P)
                            for k in range(KD):
                                if j == 0:
                                    pe.wait_ge(a_ready, KD * (B["pre"] - 1) + k + 1)
                                mm = mm3(ps[:, j, 0:w], w_hi[j // 2][:, k, c], w_lo[j // 2][:, k, c],
                                         a_hi[:, k, 0:w], a_lo[:, k, 0:w], k == 0, k == KD - 1)
                            mm.then_inc(tile_done, 1)
                    with pe.Fori(0, ph.n) as i:
                        body(i)

                elif ph.kind == "v":
                    with pe.Fori(0, ph.n) as i:
                        for j in range(4):
                            if j % 2 == 0:
                                slab_split(ph, i, j // 2)
                            bank_free(ph, i, j)
                            c = slice((j % 2) * P, (j % 2 + 1) * P)
                            for k in range(KD):
                                mm = mm3(ps[:, j, 0:SW], a_hi[:, k, c], a_lo[:, k, c],
                                         w_hi[j // 2][:, k, :], w_lo[j // 2][:, k, :], k == 0, k == KD - 1)
                            mm.then_inc(tile_done, 1)

                elif ph.kind in ("out", "add"):
                    if ph.kind == "add" and ph.spb == 2:
                        pe.wait_ge(hid_ready, B["hid"])
                        pe.wait_ge(ob_lo, 8)
                    w = ph.w
                    if ph.spb == 2:
                        with pe.Fori(0, ph.n) as i:
                            for j in range(4):
                                if j % 2 == 0:
                                    slab_split(ph, i, j // 2)
                                bank_free(ph, i, j)
                                c = slice((j % 2) * P, (j % 2 + 1) * P)
                                for k in range(KD):
                                    if j == 0 and ph.kind == "out":
                                        pe.wait_ge(hid_ready, B["hid"] - KD + k + 1)
                                    mm = mm3(ps[:, j, 0:w], w_hi[j // 2][:, k, c], w_lo[j // 2][:, k, c],
                                             hid_hi[:, k, 0:w], hid_lo[:, k, 0:w], k == 0, k == KD - 1)
                                mm.then_inc(tile_done, 1)
                    else:
                        with pe.Fori(0, ph.n) as i:
                            for pair in range(2):
                                k0 = 0
                                for part in range(3):
                                    s = 3 * pair + part
                                    slab_split(ph, i, s)
                                    kn = ph.kts[s]
                                    for t in range(2):
                                        j = 2 * pair + t
                                        if part == 0:
                                            bank_free(ph, i, j)
                                        c = slice(t * P, (t + 1) * P)
                                        for k in range(kn):
                                            if j == 0:
                                                pe.wait_ge(hid_ready, B["hid"] - KF + k0 + k + 1)
                                            mm = mm3(ps[:, j, 0:w], w_hi[s % 2][:, k, c], w_lo[s % 2][:, k, c],
                                                     hid_hi[:, k0 + k, 0:w], hid_lo[:, k0 + k, 0:w],
                                                     k0 + k == 0, k0 + k == KF - 1)
                                        if part == 2:
                                            mm.then_inc(tile_done, 1)
                                    if part < 2:
                                        mm.then_inc(mid_used, 1)
                                    k0 += kn

                elif ph.kind == "ckv":
                    for j in range(3):
                        if j % 2 == 0:
                            slab_split(ph, 0, j // 2)
                        bank_free(ph, 0, j)
                        c = slice((j % 2) * P, (j % 2 + 1) * P)
                        for k in range(KD):
                            mm = mm3(ps[:, j, 0:TW], w_hi[j // 2][:, k, c], w_lo[j // 2][:, k, c],
                                     a_hi[:, k, :], a_lo[:, k, :], k == 0, k == KD - 1)
                        mm.then_inc(tile_done, 1)
                        gn_sums(pe, j)
                    bank_free(ph, 0, 3)
                    for q in range(2):
                        c = slice(META + q * P, META + (q + 1) * P)
                        for k in range(KD):
                            mm = mm3(ps[:, 3, 8 * q:8 * q + 8], a_hi[:, k, c], a_lo[:, k, c],
                                     w_hi[1][:, k, HD:HD + 8], w_lo[1][:, k, HD:HD + 8], k == 0, k == KD - 1)
                    mm.then_inc(tile_done, 1)
                    gn_sums(pe, 3)

                elif ph.kind == "va":
                    for j in range(4):
                        if j % 2 == 0:
                            slab_split(ph, 0, j // 2)
                        bank_free(ph, 0, j)
                        parts = [(META, 0)] if j % 2 == 0 else [(META + P, 0), (0, SW)]
                        for t0, c0 in parts:
                            c = slice(t0, t0 + P)
                            for k in range(KD):
                                mm = mm3(ps[:, j, c0:c0 + SW], a_hi[:, k, c], a_lo[:, k, c],
                                         w_hi[j // 2][:, k, :], w_lo[j // 2][:, k, :], k == 0, k == KD - 1)
                        mm.then_inc(tile_done, 1)
                        gn_sums(pe, 4 + j)

                elif ph.kind == "attention":
                    a0 = HEADS * ph.no + 1

                    def scores(q, n, slot, half):
                        pe.wait_ge(ex_ready[q], n + a0)
                        rows = slice(half * HD, (half + 1) * HD)
                        wk = (q + 1) * P
                        outs = [(0, g * wk) for g in range(3)] if q == 0 else [(1, 0), (1, 256), (2, 0)]
                        if q == 1:
                            pe.matmul(ps[:, 1, :], identb[:], maskb[:, 0:512], start=True, stop=True,
                                      skip_group_check=True)
                        for g, (bank, c) in enumerate(outs):
                            pe.matmul(ps[:, bank, c:c + wk], roped[slot][rows, g, q * P:(q + 1) * P],
                                      roped[slot][rows, 3 + g, 0:wk], start=True, stop=False, skip_group_check=True)
                            m0 = 0 if q == 0 else 384
                            mm = pe.matmul(ps[:, bank, c:c + wk], identb[:], maskb[:, m0 + g * wk:m0 + (g + 1) * wk],
                                           start=False, stop=True, skip_group_check=True)
                        mm.then_inc(sc_done[q], 1)

                    def turn(j, n):
                        q = min(j, 1)
                        pe.wait_ge(ex_ready[q], n + (a0 + 1))
                        pe.wait_ge(pt_copied[j], n + a0)
                        b0 = 3 if j == 2 else 0
                        for b in range(3):
                            mm = pe.transpose(ps[:, 3 + j, b * P:(b + 1) * P],
                                              prob[q][:, (b0 + b) * P:(b0 + b + 1) * P], ident[:])
                        mm.then_inc(pt_done[j], 1)

                    def values(j, n, head):
                        q = min(j, 1)
                        pe.wait_ge(pt_copied[j], n + (a0 + 1))
                        if j < 2:
                            pe.wait_ge(o_drained[q], n + a0)
                        for b in range(3):
                            blk = b + (3 if j == 2 else 0)
                            g, kt = (blk, 0) if q == 0 else (blk // 2, blk % 2)
                            mm = pe.matmul(ps[:, 6 + q, 0:HD], probT[j][:, b * P:(b + 1) * P],
                                           v_tok[kt][:, bass.ds(head * HD + g * D, HD)],
                                           start=(b == 0 and j < 2), stop=(b == 2 and j != 1))
                        if j != 1:
                            mm.then_inc(o_done[q], 1)

                    pe.wait_ge(consts_cast, 2)
                    pe.wait_ge(drained_a, B["da"])
                    pe.wait_ge(drained_b, B["db"] - 1)
                    pe.wait_ge(rope_ready, a0 + 2)
                    scores(0, 0, 0, 0)
                    scores(1, 0, 0, 0)
                    pe.wait_ge(drained_b, B["db"])

                    def body(i, is_last):
                        for m in range(4):
                            n = i * 4 + m
                            turn(0, n)
                            if not (is_last and m == 3):
                                if m % 2 == 1:
                                    pe.wait_ge(rope_ready, i * 4 + (a0 + 2 * (m // 2) + 4))
                                scores(0, n + 1, ((m + 1) // 2) % 2, (m + 1) % 2)
                            values(0, n, n)
                            turn(1, n)
                            turn(2, n)
                            if not (is_last and m == 3):
                                scores(1, n + 1, ((m + 1) // 2) % 2, (m + 1) % 2)
                            values(1, n, n)
                            values(2, n, n)
                    bodies(pe, 4, body)
                    pe.wait_ge(o_drained[0], a0 + HEADS)
                    pe.wait_ge(o_drained[1], a0 + HEADS)
                    for k in range(KD):
                        if k >= 4:
                            pe.wait_ge(hid_ready, B["hid"] + k - 3)
                        for q in range(2):
                            mm = pe.transpose(ps[:, 4 + k % 4, q * P:(q + 1) * P], o_tok[:, q, k * P:(k + 1) * P], ident[:])
                        mm.then_inc(oT_done, 1)

                elif ph.kind == "cc_mid":
                    pe.wait_ge(drained_b, B["db"])
                    for t, k in enumerate(CC_PE):
                        for j in range(TAPS):
                            pe.wait_ge(diag_ready, t * TAPS + j + 1)
                            mm = pe.matmul(ps[:, 5 + t, 0:SEQ], diag[:, t * TAPS + j, :], gpad[:, k, j:j + SEQ],
                                           start=(j == 0), stop=(j == TAPS - 1))
                        mm.then_inc(cc_product, 1)
                    pe.wait_ge(cc_tap_pool, (2 * TAPS - 1) * len(CC_POOL))
                    pe.wait_ge(cc_tap, TAPS * len(CC_DVE))
                    pe.wait_ge(cc_drained, len(CC_PE))
                    for k in range(KD):
                        mm = pe.matmul(ps[:, 4, 0:SEQ], ones[:], cacc[:, k, :], start=(k == 0), stop=(k == KD - 1))
                    mm.then_inc(cc_sum, 1)
                    for k in range(KD):
                        pe.wait_ge(cc_norm, k + 1)
                        mm = pe.matmul(ps[:, 5, 0:SEQ], ones[:], work[:, k, 0:SEQ], start=(k == 0), stop=(k == KD - 1))
                    mm.then_inc(cc_sum, 1)

                elif ph.kind == "mix2":
                    mix2_tensor(pe, B)

            for t in range(2):
                for k in range(KD):
                    h_wait(pe, final, k)
                    mm = pe.transpose(ps[:, 4 + 2 * t + k // 4, (k % 4) * P:(k % 4 + 1) * P],
                                      h[:, k, META + t * P:META + (t + 1) * P], ident[:])
                    if k % 4 == 3:
                        mm.then_inc(out_done, 1)


_INS = ['x', 'positions', 'mix_norm_pre', 'mix_norm_post', 'ffn_norm_pre', 'ffn_norm_post', 'attn_w_qkv',
        'attn_w_o', 'sc_w_in', 'sc_w_conv', 'sc_w_out', 'cc_w_pw1', 'cc_b_pw1', 'cc_w_dw', 'cc_b_dw', 'cc_ln_g',
        'cc_ln_b', 'cc_w_pw2', 'cc_b_pw2', 'ffn_w_in', 'ffn_w_conv', 'ffn_w_out', 'meta_tokens_2', 'rel_bias_2',
        'ffn1_norm_2', 'ffn1_w_gate_2', 'ffn1_w_up_2', 'ffn1_w_down_2', 'mix_norm_2', 'w_in_2', 'a_q_norm_2',
        'a_k_norm_2', 'a_lambda_q1_2', 'a_lambda_k1_2', 'a_lambda_q2_2', 'a_lambda_k2_2', 'a_subln_2',
        'b_kv_norm_2', 'b_w_uk_2', 'b_q_norm_2', 'b_w_uv_2', 'w_out_2', 'ffn2_norm_2', 'ffn2_w_gate_2',
        'ffn2_w_up_2', 'ffn2_w_down_2']


def kernel(**inputs):
    import numpy as _np
    import concourse.bacc as _bacc
    from concourse.bass_utils import run_bass_kernel_spmd as _run

    nc = _bacc.Bacc("TRN2", target_bir_lowering=False, num_devices=1)
    arrays, args = {}, {}
    for name in _INS + ["const"]:
        a = constants() if name == "const" else _np.ascontiguousarray(inputs[name])
        arrays[f"in_{name}_dram"] = a
        args[name] = nc.dram_tensor(f"in_{name}_dram", a.shape, mybir.dt.from_np(a.dtype), kind="ExternalInput").ap()
    out = nc.dram_tensor("out_0_dram", (1, SEQ, D), F32, kind="ExternalOutput").ap()
    build(nc, args, out)
    r = _run(nc, [arrays], core_ids=[0])
    return r.results[0]["out_0_dram"]
```
